# Optimizing a Trainium2 kernel written in Bass

```python
import math
import jax, jax.numpy as jnp
from jax import lax
import numpy as np

D_MODEL = 1024
BATCH = 1
SEQ = 512
DEPTH = 1

CHUNK = 64
HEAD_DIM = 64
SWA_Q_HEADS = 8
SWA_KV_HEADS = 2
SWA_WINDOW = 128
SWA_WIN_CHUNKS = SWA_WINDOW // CHUNK
FOX_HEADS = 8
FOX_BLOCK = 128
MEM_LEN = 256
MEM_HEADS = 4
MEM_HEAD_DIM = D_MODEL // MEM_HEADS
D_FF = 2816
N_BRANCH = 2
ROPE_THETA = 10000.0
LN_EPS = 1e-5
NEG_INF = -1e30
ALPHA = (2.0 * DEPTH) ** 0.25
BETA = (8.0 * DEPTH) ** -0.25

SWA_Q = SWA_Q_HEADS * HEAD_DIM
SWA_KV = SWA_KV_HEADS * HEAD_DIM
FOX_W = FOX_HEADS * HEAD_DIM
IN_SIZES = (SWA_Q, SWA_KV, SWA_KV, FOX_W, FOX_W, FOX_W, FOX_HEADS, N_BRANCH * D_MODEL)

kernel_name = "hybrid_swa_sink_fox_macaron_deepnorm_layer"

def layer_norm(x, g, b):
    xf = x.astype(jnp.float32)
    mu = jnp.mean(xf, axis=-1, keepdims=True)
    var = jnp.mean(jnp.square(xf - mu), axis=-1, keepdims=True)
    y = (xf - mu) * lax.rsqrt(var + LN_EPS) * g.astype(jnp.float32) + b.astype(jnp.float32)
    return y.astype(x.dtype)

def swiglu(x, w_gate, w_up, w_down):
    return (jax.nn.silu(x @ w_gate) * (x @ w_up)) @ w_down

def rope(x, pos):
    half = x.shape[-1] // 2
    inv = ROPE_THETA ** (-jnp.arange(half, dtype=jnp.float32) / half)
    ang = pos.astype(jnp.float32)[:, None] * inv[None, :]
    cos = jnp.cos(ang)[None, :, None, :]
    sin = jnp.sin(ang)[None, :, None, :]
    x1 = x[..., :half].astype(jnp.float32)
    x2 = x[..., half:].astype(jnp.float32)
    return jnp.concatenate([x1 * cos - x2 * sin, x2 * cos + x1 * sin], axis=-1).astype(x.dtype)

def swa_sink_attention(q, k, v, sinks):
    B, S, Hq, d = q.shape
    Hkv = k.shape[2]
    G = Hq // Hkv
    nC = S // CHUNK
    W = SWA_WIN_CHUNKS
    qc = q.reshape(B, nC, CHUNK, Hkv, G, d)

    def band(t):
        tc = t.reshape(B, nC, CHUNK, Hkv, d)
        tp = jnp.pad(tc, ((0, 0), (W - 1, 0), (0, 0), (0, 0), (0, 0)))
        return jnp.concatenate([tp[:, i:i + nC] for i in range(W)], axis=2)

    kb, vb = band(k), band(v)
    s = jnp.einsum('bcqhgd,bckhd->bchgqk', qc, kb).astype(jnp.float32) * (d ** -0.5)
    key_chunk = jnp.arange(nC)[:, None] - (W - 1) + jnp.arange(W * CHUNK)[None, :] // CHUNK
    valid = (key_chunk >= 0)[None, :, None, None, None, :]
    s = jnp.where(valid, s, NEG_INF)
    sink = jnp.broadcast_to(sinks.astype(jnp.float32).reshape(1, 1, Hkv, G, 1, 1), s.shape[:-1] + (1,))
    p = jax.nn.softmax(jnp.concatenate([s, sink], axis=-1), axis=-1)[..., :-1]
    o = jnp.einsum('bchgqk,bckhd->bcqhgd', p.astype(v.dtype), vb)
    return o.reshape(B, S, Hq * d)

def forgetting_attention(q, k, v, f_logit):
    B, S, H, d = q.shape
    c = jnp.cumsum(jax.nn.log_sigmoid(f_logit.astype(jnp.float32)), axis=1)
    cT = c.transpose(0, 2, 1)
    nQ = S // FOX_BLOCK
    qb = q.reshape(B, nQ, FOX_BLOCK, H, d).transpose(1, 0, 2, 3, 4)
    cb = c.reshape(B, nQ, FOX_BLOCK, H).transpose(1, 0, 3, 2)
    kpos = jnp.arange(S)
    scale = d ** -0.5

    def block(args):
        i, qi, ci = args
        s = jnp.einsum('bqhd,bkhd->bhqk', qi, k).astype(jnp.float32) * scale
        s = s + ci[..., None] - cT[:, :, None, :]
        qpos = i * FOX_BLOCK + jnp.arange(FOX_BLOCK)
        s = jnp.where(kpos[None, :] <= qpos[:, None], s, NEG_INF)
        p = jax.nn.softmax(s, axis=-1)
        return jnp.einsum('bhqk,bkhd->bqhd', p.astype(v.dtype), v)

    o = lax.map(block, (jnp.arange(nQ), qb, cb))
    return o.transpose(1, 0, 2, 3, 4).reshape(B, S, H * d)

def hybrid_mixer(x, w_in, b_gate, b_forget, swa_sinks, w_branch_swa, w_branch_fox, w_out):
    B, S, D = x.shape
    z = x @ w_in
    idx = [int(v) for v in np.cumsum(IN_SIZES)[:-1]]
    q_s, k_s, v_s, q_f, k_f, v_f, f_l, g = jnp.split(z, idx, axis=-1)
    pos = jnp.arange(S)
    q_s = rope(q_s.reshape(B, S, SWA_Q_HEADS, HEAD_DIM), pos)
    k_s = rope(k_s.reshape(B, S, SWA_KV_HEADS, HEAD_DIM), pos)
    v_s = v_s.reshape(B, S, SWA_KV_HEADS, HEAD_DIM)
    o_s = swa_sink_attention(q_s, k_s, v_s, swa_sinks)
    o_f = forgetting_attention(q_f.reshape(B, S, FOX_HEADS, HEAD_DIM),
                               k_f.reshape(B, S, FOX_HEADS, HEAD_DIM),
                               v_f.reshape(B, S, FOX_HEADS, HEAD_DIM),
                               f_l + b_forget)
    gates = jax.nn.sigmoid((g + b_gate.reshape(-1)).astype(jnp.float32)).astype(x.dtype)
    gates = gates.reshape(B, S, N_BRANCH, D)
    merged = gates[:, :, 0] * (o_s @ w_branch_swa) + gates[:, :, 1] * (o_f @ w_branch_fox)
    return merged @ w_out

def memory_cross_attention(x, mem, w_q, w_k, w_v, w_o):
    B, S, D = x.shape
    q = (x @ w_q).reshape(B, S, MEM_HEADS, MEM_HEAD_DIM)
    k = (mem @ w_k).reshape(B, MEM_LEN, MEM_HEADS, MEM_HEAD_DIM)
    v = (mem @ w_v).reshape(B, MEM_LEN, MEM_HEADS, MEM_HEAD_DIM)
    s = jnp.einsum('bshd,bmhd->bhsm', q, k).astype(jnp.float32) * (MEM_HEAD_DIM ** -0.5)
    p = jax.nn.softmax(s, axis=-1)
    o = jnp.einsum('bhsm,bmhd->bshd', p.astype(v.dtype), v).reshape(B, S, D)
    return o @ w_o

def setup_inputs(seed: int = 0) -> dict:
    key = jax.random.key(seed)
    ks = iter(jax.random.split(key, 48))
    L, D = DEPTH, D_MODEL

    def nrm(shape, scale):
        return jax.random.normal(next(ks), shape, jnp.float32) * scale

    def gain():
        return 1.0 + nrm((L, D), 0.02)

    def bias():
        return nrm((L, D), 0.02)

    sd = D ** -0.5
    x = nrm((BATCH, SEQ, D), 1.0)
    mem = nrm((BATCH, MEM_LEN, D), 1.0)
    ffn1_w_gate = nrm((L, D, D_FF), sd)
    ffn1_w_up = nrm((L, D, D_FF), BETA * sd)
    ffn1_w_down = nrm((L, D_FF, D), BETA * D_FF ** -0.5)
    ln1_g, ln1_b = gain(), bias()
    mix_w_in = jnp.concatenate([
        nrm((L, D, SWA_Q), sd), nrm((L, D, SWA_KV), sd), nrm((L, D, SWA_KV), BETA * sd),
        nrm((L, D, FOX_W), sd), nrm((L, D, FOX_W), sd), nrm((L, D, FOX_W), BETA * sd),
        nrm((L, D, FOX_HEADS), 0.1 * sd), nrm((L, D, N_BRANCH * D), sd)], axis=-1)
    mix_b_gate = nrm((L, N_BRANCH, D), 0.01)
    mix_b_forget = jnp.linspace(1.0, 4.0, FOX_HEADS, dtype=jnp.float32)[None, :] + nrm((L, FOX_HEADS), 0.1)
    swa_sinks = nrm((L, SWA_Q_HEADS), 0.5)
    mix_w_branch_swa = nrm((L, SWA_Q, D), BETA * SWA_Q ** -0.5)
    mix_w_branch_fox = nrm((L, FOX_W, D), BETA * FOX_W ** -0.5)
    mix_w_out = nrm((L, D, D), BETA * sd)
    ln2_g, ln2_b = gain(), bias()
    mem_w_q = nrm((L, D, D), sd)
    mem_w_k = nrm((L, D, D), sd)
    mem_w_v = nrm((L, D, D), BETA * sd)
    mem_w_o = nrm((L, D, D), BETA * sd)
    ln3_g, ln3_b = gain(), bias()
    ffn2_w_gate = nrm((L, D, D_FF), sd)
    ffn2_w_up = nrm((L, D, D_FF), BETA * sd)
    ffn2_w_down = nrm((L, D_FF, D), BETA * D_FF ** -0.5)
    ln4_g, ln4_b = gain(), bias()
    return {"x": x, "mem": mem,
            "ffn1_w_gate": ffn1_w_gate, "ffn1_w_up": ffn1_w_up, "ffn1_w_down": ffn1_w_down,
            "ln1_g": ln1_g, "ln1_b": ln1_b,
            "mix_w_in": mix_w_in, "mix_b_gate": mix_b_gate, "mix_b_forget": mix_b_forget,
            "swa_sinks": swa_sinks, "mix_w_branch_swa": mix_w_branch_swa,
            "mix_w_branch_fox": mix_w_branch_fox, "mix_w_out": mix_w_out,
            "ln2_g": ln2_g, "ln2_b": ln2_b,
            "mem_w_q": mem_w_q, "mem_w_k": mem_w_k, "mem_w_v": mem_w_v, "mem_w_o": mem_w_o,
            "ln3_g": ln3_g, "ln3_b": ln3_b,
            "ffn2_w_gate": ffn2_w_gate, "ffn2_w_up": ffn2_w_up, "ffn2_w_down": ffn2_w_down,
            "ln4_g": ln4_g, "ln4_b": ln4_b}

def reference(x, mem, ffn1_w_gate, ffn1_w_up, ffn1_w_down, ln1_g, ln1_b,
              mix_w_in, mix_b_gate, mix_b_forget, swa_sinks, mix_w_branch_swa,
              mix_w_branch_fox, mix_w_out, ln2_g, ln2_b,
              mem_w_q, mem_w_k, mem_w_v, mem_w_o, ln3_g, ln3_b,
              ffn2_w_gate, ffn2_w_up, ffn2_w_down, ln4_g, ln4_b):
    for l in range(DEPTH):
        x = layer_norm(ALPHA * x + 0.5 * swiglu(x, ffn1_w_gate[l], ffn1_w_up[l], ffn1_w_down[l]),
                       ln1_g[l], ln1_b[l])
        x = layer_norm(ALPHA * x + hybrid_mixer(x, mix_w_in[l], mix_b_gate[l], mix_b_forget[l], swa_sinks[l],
                                                mix_w_branch_swa[l], mix_w_branch_fox[l], mix_w_out[l]),
                       ln2_g[l], ln2_b[l])
        x = layer_norm(ALPHA * x + memory_cross_attention(x, mem, mem_w_q[l], mem_w_k[l], mem_w_v[l], mem_w_o[l]),
                       ln3_g[l], ln3_b[l])
        x = layer_norm(ALPHA * x + 0.5 * swiglu(x, ffn2_w_gate[l], ffn2_w_up[l], ffn2_w_down[l]),
                       ln4_g[l], ln4_b[l])
    return x


_drawn_inputs = setup_inputs


def setup_inputs(seed=0):
    import zlib

    import numpy as np

    out = dict(_drawn_inputs(seed))
    spreads = {}
    factors = {'ln1_g': 2.694,
     'ln1_b': 2.713,
     'mix_b_gate': 63.85,
     'mix_b_forget': 2.88,
     'swa_sinks': 64.0,
     'mix_w_branch_swa': 3.862,
     'ln2_g': 2.737,
     'ln2_b': 2.82,
     'ln3_g': 9.282,
     'ln3_b': 8.213,
     'ln4_g': 7.533,
     'ln4_b': 7.799}
    for name, (base, spread) in spreads.items():
        noise = np.random.default_rng([zlib.crc32(name.encode()), seed]).standard_normal(out[name].shape)
        drawn = base * np.exp(spread * noise) if base else spread * noise
        out[name] = __import__('jax').numpy.asarray(drawn.astype(out[name].dtype))
    for name, factor in factors.items():
        out[name] = (out[name] * factor).astype(out[name].dtype)
    return out
```

```python
from contextlib import ExitStack

import concourse.bass as bass
from concourse import mybir

F32 = mybir.dt.float32
F32R = mybir.dt.float32r
BF16 = mybir.dt.bfloat16
ACT = mybir.ActivationFunctionType
ALU = mybir.AluOpType
AX = mybir.AxisListType

P = 128
D = 1024
SEQ = 512
TB = SEQ // P
KC = D // P
HALF = 512
HD = 64
SWA_HEADS, SWA_KV, FOX_HEADS = 8, 2, 8
WINDOW = 256
CHUNK = 64
MEM = 256
MB = MEM // P
MEM_HEADS = 4
D_FF = 2816
FF_PAIRS = D_FF // P // 2
ALPHA = 2.0 ** 0.25
LN_EPS = 1e-5
ROPE_THETA = 10000.0
NEG = -1e30
QK_SCALE = HD ** -0.5
MEM_SCALE = (D // MEM_HEADS) ** -0.5

C_QS = 0
C_KS = C_QS + SWA_HEADS * HD
C_VS = C_KS + SWA_KV * HD
C_QF = C_VS + SWA_KV * HD
C_KF = C_QF + FOX_HEADS * HD
C_VF = C_KF + FOX_HEADS * HD
C_F = C_VF + FOX_HEADS * HD
C_G = C_F + FOX_HEADS

U_FFN1 = 0
U_MK = U_FFN1 + 6 * FF_PAIRS
U_F = U_MK + KC
U_KS = U_F + 1
U_VS = U_KS + 1
U_QS = U_VS + 1
U_QF = U_QS + 4
U_KF = U_QF + 4
U_VF = U_KF + 4
U_G0 = U_VF + 4
U_G1 = U_G0 + 12
U_OUT = U_G1 + 12
U_MV = U_OUT + KC
U_MQ = U_MV + KC
U_MO = U_MQ + KC
U_FFN2 = U_MO + KC
U_END = U_FFN2 + 6 * FF_PAIRS
FOX_COPIES = P // FOX_HEADS
RAW = 3
RING = 6
AHEAD = 3

O_MK = 0
O_F = O_MK + KC
O_KS = O_F + 1
O_VS = O_KS + 1
O_QS = O_VS + 1
O_QF = O_QS + 4
O_KF = O_QF + 4
O_VF = O_KF + 4
O_G0 = O_VF + 4
O_G1 = O_G0 + 16
O_MQ = O_G1 + 16
O_END = O_MQ + KC

HEADS = SWA_HEADS + FOX_HEADS

T_F, T_KS, T_C, T_VS, T_QS = 0, 1, 2, 3, 4


def fill(slot):
    first = 3 * (slot // 2) + (slot % 2)
    return range(first, first + 1 + slot % 2)


def t_uses():
    n, heads, values = T_QS + 4, [], {}
    for slot in range(HEADS + 1):
        if slot >= 1:
            heads.append(n)
            n += 2 if slot - 1 < SWA_HEADS else 3
        if slot < SWA_HEADS:
            for u in fill(slot):
                if u >= 8:
                    values[u - 8] = n
                    n += 1
    return heads, values, n


T_HEAD, T_VF, T_END = t_uses()

FOX_AT = {3: (0, 512), 2: (512, 384), 0: (896, 128), 1: (1024, 256)}
FOX_T = {0: 0, 1: 512, 2: 1024, 3: 896}
SWA_T = {0: 0, 1: 256, 2: 512, 3: 768}


def fox_transposes():
    every = [(q, k, FOX_T[k] + P * (q - k)) for k in range(TB) for q in range(k, TB)]
    return [[x for x in every if x[2] // HALF == b] for b in range(3)]


def swa_transposes():
    every = [(q, k, SWA_T[k] + P * (q - k)) for k in range(TB) for q in (k, k + 1) if q < TB]
    return [[x for x in every if x[2] // HALF == b] for b in range(2)]


def program(nc, t, out, x_spill):
    ctx = ExitStack()
    with ctx:
        base = [(nc.sbuf_base + 63) // 64 * 64]

        def place(name, shape, dt, at=None):
            size = 2 if dt == BF16 else 4
            for n in shape[1:]:
                size *= n
            where = base[0] if at is None else at
            if at is None:
                base[0] += (size + 31) // 32 * 32
            return nc.alloc_sbuf_tensor_at(name, shape, dt, offset=where)

        def zone(kib):
            where = base[0]
            base[0] += kib * 1024
            return where

        def sem(name):
            return ctx.enter_context(nc.semaphore(name))

        ring_hi = place("ring_hi", [P, RING, D], F32R)
        ring_lo = place("ring_lo", [P, RING, D], F32R)
        z_xh, z_xl, z_r = zone(16), zone(16), zone(32)
        xT_hi = place("xT_hi", [P, KC, SEQ], F32R, z_xh)
        xT_lo = place("xT_lo", [P, KC, SEQ], F32R, z_xl)
        h_hi = place("h_hi", [P, 2, SEQ], F32R, z_r)
        h_lo = place("h_lo", [P, 2, SEQ], F32R, z_r + 4096)
        os_hi = place("os_hi", [P, 4, SEQ], F32R, z_r)
        os_lo = place("os_lo", [P, 4, SEQ], F32R, z_r + 8192)
        of_hi = place("of_hi", [P, 4, SEQ], F32R, z_r + 16384)
        of_lo = place("of_lo", [P, 4, SEQ], F32R, z_r + 24576)
        memT_hi = place("memT_hi", [P, KC, MEM], F32R, z_r + 16384)
        memT_lo = place("memT_lo", [P, KC, MEM], F32R, z_r + 24576)
        m0_hi = place("m0_hi", [P, 4, SEQ], F32R, z_r)
        m0_lo = place("m0_lo", [P, 4, SEQ], F32R, z_r + 8192)
        m1_hi = place("m1_hi", [P, 4, SEQ], F32R, z_xh)
        m1_lo = place("m1_lo", [P, 4, SEQ], F32R, z_xl)
        om_hi = place("om_hi", [P, KC, SEQ], F32R, z_r)
        om_lo = place("om_lo", [P, KC, SEQ], F32R, z_r + 16384)

        raw = place("raw", [P, RAW, D], F32)
        z_a, z_b, z_q, z_v = zone(16), zone(16), zone(8), zone(8)
        z_p = zone(10)
        xa = place("xa", [P, TB, D], F32, z_a)
        xb = place("xb", [P, TB, D], F32, z_b)
        part = place("part", [P, KC, SEQ], F32, z_a)
        qm = place("qm", [P, KC, SEQ], F32, z_a)
        qs = place("qs", [P, 4, SEQ], F32, z_a)
        ks = place("ks", [P, 2, 2, SEQ], F32, z_a + 8192)
        kf = place("kf", [P, FOX_HEADS, SEQ], F32, z_b)
        qf = place("qf", [P, 4, SEQ], F32, z_q)
        vf = place("vf", [P, TB, FOX_HEADS * HD], F32, z_v)
        vm = place("vm", [P, MB, D], F32, z_q)
        mem_in = place("mem_in", [P, MB, D], F32, z_v)
        sig = place("sig", [P, 2, SEQ], F32, z_q)
        hf = place("hf", [P, 2, SEQ], F32, z_q + 4096)
        fz = place("fz", [P, SEQ], F32, z_v)
        fe = place("fe", [P, SEQ], F32, z_v + 2048)
        fa = place("fa", [P, SEQ], F32, z_v + 4096)
        fb = place("fb", [P, SEQ], F32, z_v + 6144)
        prob = place("prob", [P, 1280], F32, z_p)
        probT = place("probT", [P, 1280], F32, z_p + 5120)
        ln_g = place("ln_g", [P, D], F32, z_p)
        ln_b = place("ln_b", [P, D], F32, z_p + 4096)
        lsn = place("lsn", [P, TB, P], F32, z_p)
        tri_f = place("tri_f", [P, SEQ], F32, z_p + 5120)
        rot = place("rot", [P, SEQ], F32, z_p + 2048)
        kraw = place("kraw", [P, SEQ], F32, z_p + 7168)
        cos_t = place("cos_t", [P, SEQ], F32, z_q + 4096)
        sin_t = place("sin_t", [P, SEQ], F32, z_q + 6144)
        km = place("km", [P, KC, MEM], F32)
        vs = place("vs", [P, TB, P], F32)
        gate = place("gate", [P, 2, SEQ], F32)
        c_hi = place("c_hi", [P, SEQ], BF16)
        c_mid = place("c_mid", [P, SEQ], BF16)
        c_lo = place("c_lo", [P, SEQ], BF16)
        c_q = place("c_q", [P, SEQ], BF16)
        c_k = place("c_k", [P, SEQ], BF16)
        c_qh = place("c_qh", [P, 2, SEQ], BF16)
        ident = place("ident", [P, P], F32)
        ident_b = place("ident_b", [P, P], BF16)
        swap = place("swap", [P, P], F32)
        mask_s = place("mask_s", [P, WINDOW], BF16)
        mask_0 = place("mask_0", [P, WINDOW], BF16)
        mask_c = place("mask_c", [P, P], BF16)
        pick = place("pick", [P, 6, FOX_HEADS], F32)
        pick_part = place("pick_part", [P, 8], F32)
        pick_head = place("pick_head", [P, FOX_HEADS], F32)
        bias_rows = place("bias_rows", [2 * KC + 1, P], F32)
        b_gate = place("b_gate", [P, 2, KC], F32)
        b_f = place("b_f", [P, 1], F32)
        sinks = place("sinks", [P, SWA_HEADS], F32)
        stats = place("stats", [P, TB, 2, 6], F32)
        mv = place("mv", [P, TB, 2], F32)
        rstd = place("rstd", [P, TB], F32)
        veps = place("veps", [P, TB], F32)
        expo = place("expo", [P, 1], F32)
        top = place("top", [P, 4], F32)
        ntop = place("ntop", [P, 4], F32)
        rsum = place("rsum", [P, 4], F32)
        esink = place("esink", [P, 4], F32)
        rinv = place("rinv", [P, 4], F32)

        ps = [ctx.enter_context(nc.psum_tensor(f"bank{i}", [P, HALF], F32)) for i in range(2)]
        sc = ctx.enter_context(nc.psum_tensor("banks_scores", [P, 3 * HALF], F32))
        ps += [sc[:, HALF * i:HALF * (i + 1)] for i in range(3)]
        ps += [ctx.enter_context(nc.psum_tensor(f"bank{i}", [P, HALF], F32)) for i in range(5, 8)]

        landed = [sem(f"unit_landed{i}") for i in range(RAW)]
        unit_hi = sem("unit_hi")
        unit_lo = sem("unit_lo")
        unit_used = sem("unit_used")
        x_in = [sem(f"x_in{i}") for i in range(TB)]
        mem_in_ok = sem("mem_in_ok")
        small_in, bias_turned, bias_made = sem("small_in"), sem("bias_turned"), sem("bias_made")
        gains_in = sem("gains_in")
        pool_step = sem("pool_step")
        consts = sem("consts")
        zeroed = sem("zeroed")
        dve_consts = sem("dve_consts")
        xt_full, xt_hi, xt_lo = sem("xt_full"), sem("xt_hi"), sem("xt_lo")
        sig_done, gated = sem("sig_done"), sem("gated")
        h_full, h_hi_done, h_lo_done = sem("h_full"), sem("h_hi_done"), sem("h_lo_done")
        scaled = sem("scaled")
        down_full, down_free = sem("down_full"), sem("down_free")
        stats_done, mean_done, eps_added, rstd_done = sem("stats_done"), sem("mean_done"), sem("eps_added"), sem("rstd_done")
        centred, ln_done = sem("centred"), sem("ln_done")
        proj_free = [sem(f"proj_free{i}") for i in range(2)]
        branch_full = sem("branch_full")
        f_act, f_dve = sem("f_act"), sem("f_dve")
        t_full = sem("t_full")
        t_free = [sem(f"t_free{i}") for i in range(2)]
        s_full, top_done, ntop_done, exp_done = sem("s_full"), sem("top_done"), sem("ntop_done"), sem("exp_done")
        sink_added, inverse_done, p_done = sem("sink_added"), sem("inverse_done"), sem("p_done")
        o_full, o_hi, o_lo = sem("o_full"), sem("o_hi"), sem("o_lo")
        c_made, cq_made = sem("c_made"), sem("cq_made")
        angles_in, rope_cos, rope_done, ks_made = sem("angles_in"), sem("rope_cos"), sem("rope_done"), sem("ks_made")
        fox_gated, merged, merged_hi, merged_lo = sem("fox_gated"), sem("merged"), sem("merged_hi"), sem("merged_lo")
        tile_full, tile_free = sem("tile_full"), sem("tile_free")
        vm_done = sem("vm_done")
        mt_full = sem("mt_full")
        mt_free = [sem(f"mt_free{i}") for i in range(2)]
        om_full, om_hi_done, om_lo_done = sem("om_full"), sem("om_hi_done"), sem("om_lo_done")
        spilled, back, stored = sem("spilled"), sem("back"), sem("stored")

        block = ctx.enter_context(nc.Block())

        def proj_is_out(eng, o):
            eng.wait_ge(proj_free[o % 2], o // 2 + 1)

        def t_is_out(eng, n):
            eng.wait_ge(t_free[n % 2], n // 2 + 1)

        def head_uses(H):
            n = T_HEAD[H]
            return range(n, n + (2 if H < SWA_HEADS else 3))

        def p_at(H, q, k):
            return WINDOW * q + P * (k - q + 1) if H < SWA_HEADS else FOX_AT[q][0] + P * k

        def bank(i):
            return ps[i][:, :]

        def turned(i):
            return ps[i][:, :].rearrange("p (c n) -> p c n", n=P)

        def forget_views(n, ring):
            src = raw[:, n % RAW, 0:KC * FOX_HEADS].rearrange("p (k h) -> p k h", k=KC).unsqueeze(2)
            dst = ring[:, n % RING, :].rearrange("p (k r h) -> p k r h", k=KC, h=FOX_HEADS)
            return src.to_broadcast([P, KC, FOX_COPIES, FOX_HEADS]), dst

        @block.sync
        def _(sp):
            def load(n, src, form=None, off=None):
                dst = raw[:, n % RAW, :]
                if form == "columns":
                    dst = dst.rearrange("p (k c) -> p k c", k=KC)
                elif form == "branch":
                    dst = dst.rearrange("p (k c) -> p k c", k=4)
                elif form == "forget":
                    dst = raw[:, n % RAW, 0:KC * FOX_HEADS].rearrange("p (k c) -> p k c", k=KC)
                if off is not None:
                    sp.wait_ge(unit_lo, off + (n - RAW + 1))
                elif n >= RAW:
                    sp.wait_ge(unit_lo, n - RAW + 1)
                sp.dma_start(dst, src).then_inc(landed[n % RAW], 16)

            def columns(w, c0):
                return w.rearrange("(k p) c -> p k c", p=P)[:, :, c0:c0 + P]

            def rows(w, r):
                return w[r * P:(r + 1) * P, :]

            def ffn_units(n0, w_gate, w_up, w_down):
                for m in range(2):
                    load(n0 + 2 * m, columns(w_gate, m * P), "columns")
                    load(n0 + 2 * m + 1, columns(w_up, m * P), "columns")
                g = w_gate.rearrange("(k p) (m c) -> p k m c", p=P, c=P)
                u = w_up.rearrange("(k p) (m c) -> p k m c", p=P, c=P)
                d = w_down.rearrange("(m p) c -> p m c", p=P)
                n = n0 + 4
                with sp.Fori(0, FF_PAIRS - 1) as i:
                    for m in range(2):
                        chunk = bass.ds(i * 2 + (2 + m), 1)
                        load(n + 4 * m, g[:, :, chunk, :].rearrange("p k m c -> p k (m c)"), "columns", i * 6)
                        load(n + 4 * m + 1, u[:, :, chunk, :].rearrange("p k m c -> p k (m c)"), "columns", i * 6)
                        if m == 0:
                            for r in range(2):
                                load(n + 2 + r, d[:, bass.ds(i * 2 + r, 1), :].rearrange("p m c -> p (m c)"), None, i * 6)
                for r in range(2):
                    load(n0 + 6 * FF_PAIRS - 2 + r, rows(w_down, 2 * FF_PAIRS - 2 + r))

            for b in range(TB):
                sp.dma_start(xa[:, b, :], t["x"][b * P:(b + 1) * P, :]).then_inc(x_in[b], 16)
            ffn_units(U_FFN1, t["ffn1_w_gate"], t["ffn1_w_up"], t["ffn1_w_down"])
            for m in range(KC):
                load(U_MK + m, columns(t["mem_w_k"], m * P), "columns")
            w_in = t["mix_w_in"]
            load(U_F, w_in.rearrange("(k p) c -> p k c", p=P)[:, :, C_F:C_F + FOX_HEADS], "forget")
            load(U_KS, columns(w_in, C_KS), "columns")
            load(U_VS, columns(w_in, C_VS), "columns")
            for first, col in ((U_QS, C_QS), (U_QF, C_QF), (U_KF, C_KF), (U_VF, C_VF)):
                for m in range(4):
                    load(first + m, columns(w_in, col + m * P), "columns")
            for g, (first, w) in enumerate(((U_G0, t["mix_w_branch_swa"]), (U_G1, t["mix_w_branch_fox"]))):
                for u in range(4):
                    for e in range(2):
                        load(first + 3 * u + e, columns(w_in, C_G + g * D + (2 * u + e) * P), "columns")
                    load(first + 3 * u + 2, w.rearrange("(k p) c -> p k c", p=P)[:, :, 2 * P * u:2 * P * (u + 1)], "branch")
            for m in range(KC):
                load(U_OUT + m, rows(t["mix_w_out"], m))
            for m in range(KC):
                load(U_MV + m, rows(t["mem_w_v"], m))
            for m in range(KC):
                load(U_MQ + m, columns(t["mem_w_q"], m * P), "columns")
            for m in range(KC):
                load(U_MO + m, rows(t["mem_w_o"], m))
            ffn_units(U_FFN2, t["ffn2_w_gate"], t["ffn2_w_up"], t["ffn2_w_down"])
            for b in range(TB):
                sp.wait_ge(ln_done, 3 * TB + b + 1)
                sp.dma_start(out[b * P:(b + 1) * P, :], xb[:, b, :]).then_inc(stored, 16)
            sp.wait_ge(stored, 16 * TB)

        @block.gpsimd
        def _(pool):
            steps = [0]

            def step(ins):
                steps[0] += 1
                ins.then_inc(pool_step, 1)
                pool.wait_ge(pool_step, steps[0])

            def load_gains(n, after=None):
                pool.dma_start(ln_g[:, :], t[f"ln{n}_g"].to_broadcast([P, D])).then_inc(gains_in, 16)
                pool.dma_start(ln_b[:, :], t[f"ln{n}_b"].to_broadcast([P, D])).then_inc(gains_in, 16)

            def load_mem():
                pool.dma_start(mem_in[:, :, :], t["mem"].rearrange("(b p) d -> p b d", p=P)).then_inc(mem_in_ok, 16)

            def inverse_deviations(n):
                for b in range(TB):
                    pool.wait_ge(mean_done, n * TB + b + 1)
                    nc.gpsimd.tensor_scalar(veps[:, b:b + 1], mv[:, b, 1:2], LN_EPS, None, ALU.add).then_inc(eps_added, 1)
                    pool.wait_ge(eps_added, n * TB + b + 1)
                    nc.gpsimd.tensor_tensor(rstd[:, b:b + 1], veps[:, b:b + 1], expo[:, :], ALU.pow).then_inc(rstd_done, 1)

            step(nc.gpsimd.memset(ident[:, :], 0.0))
            nc.gpsimd.affine_select(out=ident[:, :], in_=ident[:, :], compare_op=ALU.not_equal, fill=1.0, base=0,
                                    pattern=[[-1, P]], channel_multiplier=1).then_inc(consts, 1)
            pool.wait_ge(consts, 1)
            load_mem()
            load_gains(1)
            step(nc.gpsimd.memset(ident_b[:, :], 0.0))
            step(nc.gpsimd.affine_select(out=ident_b[:, :], in_=ident_b[:, :], compare_op=ALU.not_equal, fill=1.0, base=0,
                                         pattern=[[-1, P]], channel_multiplier=1))
            step(nc.gpsimd.memset(expo[:, :], -0.5))
            step(nc.gpsimd.memset(swap[:, :], 0.0))
            halves = swap[:, :].rearrange("p (a b c) -> p a b c", a=2, b=2)
            for b, (sign, first) in enumerate(((-1.0, -HD // 2), (1.0, 0))):
                step(nc.gpsimd.affine_select(out=halves[:, :, b, :], in_=halves[:, :, b, :], compare_op=ALU.not_equal, fill=sign,
                                             base=first, pattern=[[-HD, 2], [-1, HD // 2]], channel_multiplier=1))
            step(nc.gpsimd.memset(mask_s[:, :], NEG))
            step(nc.gpsimd.memset(mask_0[:, :], NEG))
            step(nc.gpsimd.memset(mask_s[0:CHUNK, CHUNK:3 * CHUNK], 0.0))
            step(nc.gpsimd.memset(mask_s[CHUNK:P, 2 * CHUNK:WINDOW], 0.0))
            step(nc.gpsimd.memset(mask_0[0:CHUNK, 2 * CHUNK:3 * CHUNK], 0.0))
            step(nc.gpsimd.memset(mask_0[CHUNK:P, 2 * CHUNK:WINDOW], 0.0))
            step(nc.gpsimd.memset(mask_c[:, :], 0.0))
            step(nc.gpsimd.affine_select(out=mask_c[:, :], in_=mask_c[:, :], compare_op=ALU.is_ge, fill=NEG, base=0,
                                         pattern=[[-1, P]], channel_multiplier=1))
            step(nc.gpsimd.memset(pick[:, :, :], 0.0))
            nc.gpsimd.affine_select(out=pick[:, :, :], in_=pick[:, :, :], compare_op=ALU.not_equal, fill=1.0, base=0,
                                    pattern=[[-FOX_HEADS, 6], [-1, FOX_HEADS]], channel_multiplier=1).then_inc(consts, 1)
            pool.wait_ge(consts, 2)
            pairs = kf[:, :, :].rearrange("p (m e) s -> p m e s", e=2)
            step(nc.gpsimd.memset(pairs[CHUNK:P, :, 0, :], 0.0))
            nc.gpsimd.memset(pairs[0:CHUNK, :, 1, :], 0.0).then_inc(zeroed, 1)
            pool.wait_ge(zeroed, 1)
            inverse_deviations(0)
            for b in range(TB):
                pool.wait_ge(ln_done, b + 1)
                pool.dma_start(x_spill[b * P:(b + 1) * P, :], xa[:, b, :]).then_inc(spilled, 16)
            for angles, row in ((cos_t, 0), (sin_t, 1)):
                pool.dma_start(angles[:, :], t["rope"][row]).then_inc(angles_in, 16)
            step(nc.gpsimd.memset(tri_f[:, :], 1.0))
            nc.gpsimd.affine_select(out=tri_f[:, :], in_=tri_f[:, :], compare_op=ALU.is_ge, fill=0.0, base=0,
                                    pattern=[[1, SEQ]], channel_multiplier=-1).then_inc(zeroed, 1)
            pool.wait_ge(zeroed, 2)
            pool.wait_ge(spilled, 16 * TB)
            pool.wait_ge(xt_full, 20)
            step(nc.gpsimd.memset(ks[CHUNK:P, :, 0, :], 0.0))
            nc.gpsimd.memset(ks[0:CHUNK, :, 1, :], 0.0).then_inc(zeroed, 1)
            pool.wait_ge(zeroed, 3)
            pool.wait_ge(dve_consts, 4)
            pool.wait_ge(c_made, 2)
            for h in range(FOX_HEADS):
                if h >= 2:
                    pool.wait_ge(s_full, SWA_HEADS + h - 1)
                nc.gpsimd.tensor_scalar(c_qh[:, h % 2, :], c_q[:, :], pick_head[:, h:h + 1], None, ALU.mult).then_inc(cq_made, 1)
                pool.wait_ge(cq_made, h + 1)
            pool.wait_ge(s_full, HEADS)
            for b in range(TB):
                pool.dma_start(xb[:, b, :], x_spill[b * P:(b + 1) * P, :]).then_inc(back, 16)
            pool.wait_ge(o_full, HEADS)
            load_mem()
            load_gains(2)
            inverse_deviations(1)
            pool.wait_ge(om_full, KC)
            pool.wait_ge(ln_done, 2 * TB)
            load_gains(3)
            inverse_deviations(2)
            pool.wait_ge(ln_done, 3 * TB)
            load_gains(4)
            inverse_deviations(3)

        @block.tensor
        def _(pe):
            def parts(n):
                return ring_hi[:, n % RING, :], ring_lo[:, n % RING, :]

            def split_product(dst, hi, lo, mhi, mlo, start, stop):
                pe.matmul(dst, hi, mhi, start=start, stop=False)
                pe.matmul(dst, hi, mlo, start=False, stop=False)
                return pe.matmul(dst, lo, mhi, start=False, stop=stop)

            def ready(n, off=None):
                pe.wait_ge(unit_lo, n + 1 if off is None else off + (n + 1))

            def project(n, dst, acts=(xT_hi, xT_lo), width=SEQ):
                hi, lo = (r.rearrange("p (k c) -> p k c", k=KC) for r in parts(n))
                for k in range(KC):
                    mm = split_product(dst, hi[:, k, :], lo[:, k, :], acts[0][:, k, 0:width], acts[1][:, k, 0:width],
                                       k == 0, k == KC - 1)
                mm.then_inc(unit_used, 1)

            def turn(src, dst, c0):
                for c in range(4):
                    mm = pe.transpose(dst[:, c * P:(c + 1) * P], src[:, (c0 + c) * P:(c0 + c + 1) * P], ident[:, :])
                return mm

            def turn_rows(n, src):
                for e in range(2):
                    if n + e >= 2:
                        pe.wait_ge(xt_lo, n + e - 1)
                    turn(src, bank(2 + (n + e) % 2), 4 * e).then_inc(xt_full, 1)

            def ffn(f, n0):
                def gate_up(side, n, chunk, i=None):
                    for m in range(2):
                        ready(n + m, None if i is None else i * 6)
                        if m == 0 and i is not None:
                            pe.wait_ge(h_full, i * 2 + (chunk - 1))
                        elif m == 0 and chunk >= 2:
                            pe.wait_ge(h_full, chunk - 1)
                        project(n + m, bank(2 * side + m))

                def down(n, pair, i=None):
                    ready(n + 1, None if i is None else i * 6)
                    split = 2 * pair + 2
                    pe.wait_ge(h_lo_done, split if i is None else i * 2 + split)
                    for j in range(8):
                        b, half = j // 2, j % 2
                        was = 8 * pair + j - 3
                        if i is None:
                            pe.wait_ge(down_free, was)
                        elif was > 0:
                            pe.wait_ge(down_free, i * 8 + was)
                        elif pair == 0:
                            pe.wait_ge(down_free, i * 8 + max(was, 0))
                        for m in range(2):
                            hi, lo = (r[:, half * HALF:(half + 1) * HALF] for r in parts(n + m))
                            tok = slice(b * P, (b + 1) * P)
                            mm = split_product(bank(4 + j % 4), h_hi[:, m, tok], h_lo[:, m, tok], hi, lo, m == 0, m == 1)
                        if j < 7:
                            mm.then_inc(down_full, 1)
                        else:
                            mm.then_inc(unit_used, 2)

                pair0, chunk0 = FF_PAIRS * f, 2 * FF_PAIRS * f
                for side in range(2):
                    gate_up(side, n0 + 2 * side, chunk0 + side)
                n = n0 + 4
                with pe.Fori(0, FF_PAIRS - 1) as i:
                    gate_up(0, n, chunk0 + 2, i)
                    down(n + 2, pair0, i)
                    gate_up(1, n + 4, chunk0 + 3, i)
                down(n0 + 6 * FF_PAIRS - 2, pair0 + FF_PAIRS - 1)

            def tiles(n0, lhs, chunk_ready, touched):
                def product(j, k):
                    b, half = j // 2, j % 2
                    hi, lo = (r[:, half * HALF:(half + 1) * HALF] for r in parts(n0 + k))
                    a_hi, a_lo = lhs(k)
                    tok = slice(b * P, (b + 1) * P)
                    return split_product(bank(j), a_hi[:, tok], a_lo[:, tok], hi, lo, k == 0, k == KC - 1)

                for k in range(2):
                    ready(n0 + k)
                    chunk_ready(k)
                    for j in range(8):
                        if k == 0:
                            touched(j)
                        mm = product(j, k)
                    mm.then_inc(unit_used, 1)
                for j in range(6):
                    for k in range(2, KC):
                        if j == 0:
                            ready(n0 + k)
                            chunk_ready(k)
                        mm = product(j, k)
                    mm.then_inc(tile_full, 1)
                for k in range(2, KC):
                    product(6, k)
                    product(7, k).then_inc(unit_used, 1)

            pe.wait_ge(consts, 1)
            for b in range(TB):
                pe.wait_ge(x_in[b], 16)
                turn_rows(2 * b, xa[:, b, :])
            pe.wait_ge(mem_in_ok, 16)
            for b in range(MB):
                turn_rows(8 + 2 * b, mem_in[:, b, :])
            pe.wait_ge(small_in, 48)
            pe.transpose(bank(4)[:, 0:2 * KC + 1], bias_rows[:, :], ident[0:2 * KC + 1, 0:2 * KC + 1]).then_inc(bias_turned, 1)
            pe.wait_ge(bias_made, 2)
            pe.wait_ge(xt_lo, 12)
            ffn(0, U_FFN1)
            for m in range(KC):
                ready(U_MK + m)
                if m >= 2:
                    proj_is_out(pe, O_MK + m - 2)
                elif m == 0:
                    pe.wait_ge(h_full, 2 * FF_PAIRS)
                project(U_MK + m, bank((O_MK + m) % 2)[:, 0:MEM], (memT_hi, memT_lo), MEM)
                if m % 2 == 1:
                    b = m // 2
                    pe.wait_ge(ln_done, b + 1)
                    turn_rows(12 + 2 * b, xa[:, b, :])
            pe.wait_ge(xt_lo, 20)

            def project_out(n, o):
                ready(n)
                if o >= 2:
                    proj_is_out(pe, o - 2)
                project(n, bank(o % 2))

            def branch(n, o, b_hi, b_lo):
                ready(n)
                hi, lo = (r.rearrange("p (k c) -> p k c", k=4) for r in parts(n))
                for e in range(2):
                    proj_is_out(pe, o + e - 2)
                    cols = slice(e * P, (e + 1) * P)
                    for k in range(4):
                        mm = split_product(bank((o + e) % 2), hi[:, k, cols], lo[:, k, cols], b_hi[:, k, :], b_lo[:, k, :],
                                           k == 0, k == 3)
                    mm.then_inc(*((branch_full, 1) if e == 0 else (unit_used, 1)))

            def t_bank(n):
                if n >= 2:
                    t_is_out(pe, n - 2)
                return bank(5 + n % 2)

            def scores(H):
                if H >= 1:
                    pe.wait_ge(exp_done, H)
                if H < SWA_HEADS:
                    pe.wait_ge(rope_done, H // 2 + 2)
                    if H == 0:
                        pe.wait_ge(ks_made, 1)
                    for q in range(TB):
                        at = sc[:, WINDOW * q:WINDOW * (q + 1)]
                        pe.matmul(at, ident_b[:, :], (mask_s if q else mask_0)[:, :], start=True, stop=False)
                        k0 = P * max(q - 1, 0)
                        mm = pe.matmul(at[:, WINDOW - (P * (q + 1) - k0):], qs[:, H // 2, q * P:(q + 1) * P],
                                       ks[:, H // 4, H % 2, k0:P * (q + 1)], start=False, stop=True)
                else:
                    h = H - SWA_HEADS
                    pe.wait_ge(cq_made, h + 1)
                    for q in (3, 2, 0, 1):
                        c0, w = FOX_AT[q]
                        tok = slice(q * P, (q + 1) * P)
                        pe.matmul(sc[:, c0:c0 + w], c_qh[:, h % 2, tok], c_k[:, 0:w], start=True, stop=False)
                        pe.matmul(sc[:, c0:c0 + w], qf[:, h // 2, tok], kf[:, h, 0:w], start=False, stop=False)
                        mm = pe.matmul(sc[:, c0 + w - P:c0 + w], ident_b[:, :], mask_c[:, :], start=False, stop=True)
                mm.then_inc(s_full, 1)

            def transposed_probs(H):
                pe.wait_ge(p_done, H + 1)
                for b, (n, blocks) in enumerate(zip(head_uses(H), swa_transposes() if H < SWA_HEADS else fox_transposes())):
                    dst = t_bank(n)
                    for q, k, col in blocks:
                        src = p_at(H, q, k)
                        mm = pe.transpose(dst[:, col - HALF * b:col - HALF * b + P], prob[:, src:src + P], ident[:, :])
                    mm.then_inc(t_full, 1)

            def values(H):
                for n in head_uses(H):
                    t_is_out(pe, n)
                if H % 2 == 0 and H >= 2:
                    pe.wait_ge(o_lo, H // 2)
                dst = ps[7][HD * (H % 2):HD * (H % 2 + 1), :]
                for k in range(TB):
                    if H < SWA_HEADS:
                        v = vs[:, k, HD * (H // 4):HD * (H // 4 + 1)]
                        end, src = min(SEQ, P * k + WINDOW), SWA_T[k]
                    else:
                        h = H - SWA_HEADS
                        v = vf[:, k, HD * h:HD * (h + 1)]
                        end, src = SEQ, FOX_T[k]
                    mm = pe.matmul(dst[:, P * k:end], v, probT[:, src:src + end - P * k], start=k == 0, stop=k == TB - 1,
                                   skip_group_check=True)
                mm.then_inc(o_full, 1)

            def swapped(n, src, o):
                proj_is_out(pe, o)
                pe.matmul(t_bank(n), swap[:, :], src, start=True, stop=True).then_inc(t_full, 1)

            project_out(U_F, O_F)
            project_out(U_KS, O_KS)
            pe.wait_ge(f_dve, 2)
            turn(fe, t_bank(T_F), 0).then_inc(t_full, 1)
            project_out(U_VS, O_VS)
            swapped(T_KS, kraw[:, :], O_KS)
            t_is_out(pe, T_F)
            pe.wait_ge(zeroed, 2)
            dst = t_bank(T_C)
            for k in range(TB):
                mm = pe.matmul(dst[:, k * P:], lsn[:, k, :], tri_f[:, 0:SEQ - k * P], start=k == 0, stop=k == TB - 1)
            mm.then_inc(t_full, 1)
            project_out(U_QS, O_QS)
            proj_is_out(pe, O_VS)
            turn(gate[:, 0, :], t_bank(T_VS), 0).then_inc(t_full, 1)
            for m in range(1, 4):
                project_out(U_QS + m, O_QS + m)
                swapped(T_QS + m - 1, qs[:, m - 1, :], O_QS + m - 1)
            pe.wait_ge(zeroed, 3)
            pe.wait_ge(consts, 2)
            for H in range(HEADS):
                for u in fill(H % 8):
                    if H < SWA_HEADS:
                        project_out(U_QF + u, O_QF + u)
                    elif u % 3 < 2:
                        project_out(U_G0 + u, O_G0 + 4 * (u // 3) + u % 3)
                    else:
                        pe.wait_ge(o_lo, SWA_HEADS // 2)
                        branch(U_G0 + u, O_G0 + 4 * (u // 3) + 2, os_hi, os_lo)
                if H == 0:
                    swapped(T_QS + 3, qs[:, 3, :], O_QS + 3)
                if H >= 1:
                    transposed_probs(H - 1)
                if H < SWA_HEADS:
                    for u in fill(H):
                        if u >= 8:
                            proj_is_out(pe, O_VF + u - 8)
                            turn(gate[:, (u - 7) % 2, :], t_bank(T_VF[u - 8]), 0).then_inc(t_full, 1)
                if H == SWA_HEADS:
                    for o in range(O_QF, O_VF):
                        proj_is_out(pe, o)
                    pe.wait_ge(c_made, 4)
                scores(H)
                if H >= 1:
                    values(H - 1)
            for u in range(12):
                o = O_G1 + 4 * (u // 3) + u % 3
                if u % 3 < 2:
                    project_out(U_G1 + u, o)
                else:
                    pe.wait_ge(o_lo, HEADS // 2)
                    branch(U_G1 + u, o, of_hi, of_lo)
                if u == 0:
                    transposed_probs(HEADS - 1)
                    values(HEADS - 1)
            pe.wait_ge(mem_in_ok, 32)
            for b in range(MB):
                turn_rows(20 + 2 * b, mem_in[:, b, :])

            def merged_chunk(k):
                hi, lo = (m0_hi, m0_lo) if k < 4 else (m1_hi, m1_lo)
                return hi[:, k % 4, :], lo[:, k % 4, :]

            def mixer_touched(j):
                if j < 2:
                    proj_is_out(pe, O_MQ - 2 + (O_MQ + j) % 2)
                elif j < 4:
                    pe.wait_ge(xt_lo, 21 + j)
                elif j == 4:
                    pe.wait_ge(exp_done, HEADS)
                elif j < 7:
                    t_is_out(pe, T_END - 2 + (T_END + j - 5) % 2)
                else:
                    pe.wait_ge(o_lo, HEADS // 2)

            tiles(U_OUT, merged_chunk, lambda k: pe.wait_ge(merged_lo, k + 1), mixer_touched)

            pe.wait_ge(tile_free, 4)
            for b in range(2):
                pe.wait_ge(ln_done, TB + b + 1)
                turn_rows(24 + 2 * b, xb[:, b, :])
            for k in range(KC):
                ready(U_MV + k)
                for b in range(MB):
                    for half in range(2):
                        if k == 0:
                            pe.wait_ge(tile_free, 5 + 2 * b + half)
                        hi, lo = (r[:, half * HALF:(half + 1) * HALF] for r in parts(U_MV + k))
                        mm = split_product(bank(4 + 2 * b + half), memT_hi[:, k, b * P:(b + 1) * P],
                                           memT_lo[:, k, b * P:(b + 1) * P], hi, lo, k == 0, k == KC - 1)
                mm.then_inc(unit_used, 1)
                if k in (1, 4):
                    b = 2 + (k == 4)
                    pe.wait_ge(ln_done, TB + b + 1)
                    turn_rows(24 + 2 * b, xb[:, b, :])
            pe.wait_ge(xt_lo, 32)

            def mem_scores(h):
                for m in range(2):
                    proj_is_out(pe, O_MQ + 2 * h + m)
                pe.wait_ge(exp_done, HEADS + h)
                for b in range(TB):
                    for m in range(2):
                        mm = pe.matmul(sc[:, b * MEM:(b + 1) * MEM], qm[:, 2 * h + m, b * P:(b + 1) * P], km[:, 2 * h + m, :],
                                       start=m == 0, stop=m == 1)
                mm.then_inc(s_full, 1)

            def mem_transposed_probs(h):
                pe.wait_ge(p_done, HEADS + h + 1)
                for m in range(MB):
                    if h >= 1:
                        pe.wait_ge(mt_free[m], h)
                    elif m == 0:
                        pe.wait_ge(vm_done, 4)
                    for b in range(TB):
                        mm = pe.transpose(bank(4 + m)[:, b * P:(b + 1) * P], prob[:, MEM * b + P * m:MEM * b + P * (m + 1)],
                                          ident[:, :])
                    mm.then_inc(mt_full, 1)

            def mem_values(h):
                for m in range(MB):
                    pe.wait_ge(mt_free[m], h + 1)
                for e in range(2):
                    if h >= 1:
                        pe.wait_ge(om_lo_done, 2 * h + e - 1)
                    for m in range(MB):
                        c0 = 2 * P * h + P * e
                        mm = pe.matmul(bank(6 + e), vm[:, m, c0:c0 + P], probT[:, HALF * m:HALF * (m + 1)],
                                       start=m == 0, stop=m == MB - 1)
                    mm.then_inc(om_full, 1)

            for h in range(MEM_HEADS + 1):
                if h < MEM_HEADS:
                    for m in range(2):
                        project_out(U_MQ + 2 * h + m, O_MQ + 2 * h + m)
                if h >= 1:
                    mem_transposed_probs(h - 1)
                if h < MEM_HEADS:
                    mem_scores(h)
                if h >= 1:
                    mem_values(h - 1)

            def memory_touched(j):
                if j < 2:
                    proj_is_out(pe, O_END - 2 + (O_END + j) % 2)
                elif j < 4:
                    pe.wait_ge(exp_done, HEADS + MEM_HEADS)
                elif j < 6:
                    pe.wait_ge(mt_free[j - 4], MEM_HEADS)
                else:
                    pe.wait_ge(om_lo_done, j + 1)

            tiles(U_MO, lambda k: (om_hi[:, k, :], om_lo[:, k, :]), lambda k: pe.wait_ge(om_lo_done, k + 1), memory_touched)
            pe.wait_ge(tile_free, 12)
            for b in range(TB):
                pe.wait_ge(ln_done, 2 * TB + b + 1)
                turn_rows(32 + 2 * b, xb[:, b, :])
            pe.wait_ge(xt_lo, 40)
            pe.wait_ge(tile_free, 16)
            ffn(1, U_FFN2)

        @block.scalar
        def _(act):
            copy = ACT.Copy

            def prep(n, i=None):
                if i is None:
                    act.wait_ge(landed[n % RAW], 16 * (n // RAW + 1))
                    if n >= RING:
                        act.wait_ge(unit_used, n - RING + 1)
                else:
                    act.wait_ge(landed[n % RAW], i * 32 + 16 * (n // RAW + 1))
                    act.wait_ge(unit_used, i * 6 + max(n - RING + 1, 0))
                src, dst = raw[:, n % RAW, :], ring_hi[:, n % RING, :]
                if n == U_F:
                    src, dst = forget_views(n, ring_hi)
                nc.scalar.activation(dst, src, copy).then_inc(unit_hi, 1)

            def high(dst, src, done):
                nc.scalar.activation(dst, src, copy).then_inc(done, 1)

            def turned_high(n, dst, b):
                act.wait_ge(xt_full, n + 1)
                e = n % 2
                high(dst[:, 4 * e:4 * e + 4, b * P:(b + 1) * P], turned(2 + e), xt_hi)

            def ffn(f, n0):
                chunk0 = 2 * FF_PAIRS * f

                def sigmoid(side, n, chunk, i=None):
                    if i is None:
                        act.wait_ge(unit_used, n + 1)
                        if chunk >= 2:
                            act.wait_ge(gated, chunk - 1)
                    else:
                        act.wait_ge(unit_used, i * 6 + (n + 1))
                        act.wait_ge(gated, i * 2 + (chunk - 1))
                    nc.scalar.activation(sig[:, side, :], bank(2 * side), ACT.Sigmoid).then_inc(sig_done, 1)

                def hidden_high(side, chunk, used, i=None):
                    act.wait_ge(h_full, chunk + 1 if i is None else i * 2 + (chunk + 1))
                    act.wait_ge(unit_used, used if i is None else i * 6 + used)
                    high(h_hi[:, side, :], hf[:, side, :], h_hi_done)

                sigmoid(0, n0, chunk0)
                for k in range(3, 6):
                    prep(n0 + k)
                hidden_high(0, chunk0, n0 + 1)
                sigmoid(1, n0 + 2, chunk0 + 1)
                n = n0 + 4
                with act.Fori(0, FF_PAIRS - 1) as i:
                    prep(n + 2, i)
                    prep(n + 3, i)
                    prep(n + 4, i)
                    hidden_high(1, chunk0 + 1, n - 2, i)
                    prep(n + 5, i)
                    sigmoid(0, n, chunk0 + 2, i)
                    prep(n + 6, i)
                    prep(n + 7, i)
                    hidden_high(0, chunk0 + 2, n + 4, i)
                    sigmoid(1, n + 4, chunk0 + 3, i)
                hidden_high(1, chunk0 + 2 * FF_PAIRS - 1, n0 + 6 * FF_PAIRS - 6 + 2)

            act.dma_start(bias_rows[0:2 * KC, :], t["mix_b_gate"].rearrange("g (m p) -> (g m) p", p=P)).then_inc(small_in, 16)
            act.dma_start(bias_rows[2 * KC:2 * KC + 1, :].rearrange("a (r h) -> a r h", h=FOX_HEADS),
                          t["mix_b_forget"].unsqueeze(1).to_broadcast([1, FOX_COPIES, FOX_HEADS])).then_inc(small_in, 16)
            act.dma_start(sinks[:, :], t["swa_sinks"].to_broadcast([P, SWA_HEADS])).then_inc(small_in, 16)
            for n in range(8):
                turned_high(n, xT_hi, n // 2)
                if n in (3, 5, 7):
                    prep((n - 3) // 2)
            for n in range(8, 12):
                turned_high(n, memT_hi, n // 2 - 4)
            ffn(0, U_FFN1)
            for n in range(U_MK, U_MK + 4):
                prep(n)
            for m in range(KC):
                prep(U_MK + m + 4)
                act.wait_ge(unit_used, U_MK + m + 1)
                nc.scalar.activation(km[:, m, :], bank((O_MK + m) % 2)[:, 0:MEM], copy).then_inc(proj_free[(O_MK + m) % 2], 1)
                if m % 2 == 1:
                    for e in range(2):
                        turned_high(12 + m - 1 + e, xT_hi, m // 2)

            def output(n, o):
                act.wait_ge(unit_used, n + 1)
                return bank(o % 2)

            prep(U_F + 4)
            act.wait_ge(bias_made, 2)
            nc.scalar.activation(fz[:, :], output(U_F, O_F), ACT.Identity, bias=b_f[:, 0:1]).then_inc(proj_free[O_F % 2], 1)
            act.wait_ge(f_dve, 1)
            nc.scalar.activation(fa[:, :], fe[:, :], ACT.Exp, scale=-1.0).then_inc(f_act, 1)
            act.wait_ge(f_act, 1)
            nc.scalar.activation(fb[:, :], fa[:, :], ACT.Ln, bias=1.0).then_inc(f_act, 1)
            prep(U_KS + 4)
            nc.scalar.activation(kraw[:, :], output(U_KS, O_KS), copy).then_inc(proj_free[O_KS % 2], 1)
            prep(U_VS + 4)
            nc.scalar.activation(gate[:, 0, :], output(U_VS, O_VS), copy).then_inc(proj_free[O_VS % 2], 1)
            act.wait_ge(spilled, 16 * TB)
            act.wait_ge(rope_done, 1)
            for kv in range(2):
                for e in range(2):
                    ins = nc.scalar.activation(ks[HD * e:HD * (e + 1), kv, e, :], kraw[HD * kv:HD * (kv + 1), :], copy)
            ins.then_inc(ks_made, 1)
            for m in range(4):
                prep(U_QS + m + 4)
                nc.scalar.activation(qs[:, m, :], output(U_QS + m, O_QS + m), copy, scale=QK_SCALE)\
                    .then_inc(proj_free[(O_QS + m) % 2], 1)

            def copied_probs(H):
                for e, n in enumerate(head_uses(H)):
                    if e != 1:
                        act.wait_ge(t_full, n + 1)
                        w = HALF if e == 0 else 2 * P
                        nc.scalar.activation(probT[:, HALF * e:HALF * e + w], bank(5 + n % 2)[:, 0:w], copy)\
                            .then_inc(t_free[n % 2], 1)

            def exponentials(H, at, sink=None):
                act.wait_ge(ntop_done, H + 1)
                if sink is not None:
                    nc.scalar.activation(esink[:, :], ntop[:, :], ACT.Exp, bias=sinks[:, sink:sink + 1])
                for q, (c0, w) in sorted(at.items()):
                    ins = nc.scalar.activation(prob[:, c0:c0 + w], sc[:, c0:c0 + w], ACT.Exp, bias=ntop[:, q:q + 1],
                                               accum_out=rsum[:, q:q + 1])
                ins.then_inc(exp_done, 1)

            def pair_high(H):
                act.wait_ge(o_full, H + 1)
                m = H // 2
                high((os_hi if m < 4 else of_hi)[:, m % 4, :], bank(7), o_hi)

            def gate_tanh(n, o, g, m):
                nc.scalar.activation(gate[:, m % 2, :], output(n, o), ACT.Tanh, bias=b_gate[:, g, m:m + 1], scale=0.5)\
                    .then_inc(proj_free[o % 2], 1)

            at_swa = {q: (WINDOW * q, WINDOW) for q in range(TB)}
            act.wait_ge(small_in, 48)
            for H in range(HEADS):
                for u in fill(H % 8):
                    if H < SWA_HEADS:
                        n, o = U_QF + u, O_QF + u
                        prep(n + 4)
                        if u == 2:
                            act.wait_ge(rope_done, 5)
                        if u < 4:
                            nc.scalar.activation(qf[:, u, :], output(n, o), copy, scale=QK_SCALE).then_inc(proj_free[o % 2], 1)
                        elif u >= 8:
                            v = u - 8
                            act.wait_ge(t_full, (T_VF[v - 2] if v >= 2 else T_VS) + 1)
                            nc.scalar.activation(gate[:, (v + 1) % 2, :], output(n, o), copy).then_inc(proj_free[o % 2], 1)
                    else:
                        n = U_G0 + u
                        prep(n + 4)
                        if u % 3 < 2:
                            o, m = O_G0 + 4 * (u // 3) + u % 3, 2 * (u // 3) + u % 3
                            if m >= 2:
                                proj_is_out(act, o - 2)
                            else:
                                act.wait_ge(t_full, T_VF[3] + 1)
                            gate_tanh(n, o, 0, m)
                if H >= 1:
                    copied_probs(H - 1)
                exponentials(H, at_swa if H < SWA_HEADS else FOX_AT, H if H < SWA_HEADS else None)
                if H >= 2 and H % 2 == 0:
                    pair_high(H - 1)

            def merged_high(m):
                act.wait_ge(merged, m + 1)
                if m >= 4:
                    act.wait_ge(unit_used, U_G1 + 11)
                hi = (m0_hi if m < 4 else m1_hi)[:, m % 4, :]
                nc.scalar.activation(hi, part[:, m, :], copy, scale=0.5).then_inc(merged_hi, 1)

            for u in range(12):
                n = U_G1 + u
                prep(n + 4)
                if u % 3 < 2:
                    o, m = O_G1 + 4 * (u // 3) + u % 3, 2 * (u // 3) + u % 3
                    if m >= 2:
                        act.wait_ge(merged, m - 1)
                    else:
                        proj_is_out(act, O_G1 - 2 + m)
                    gate_tanh(n, o, 1, m)
                if u == 0:
                    copied_probs(HEADS - 1)
                    pair_high(HEADS - 1)
                if u in (3, 6):
                    for m in (0, 1) if u == 3 else (2, 3):
                        merged_high(m)
            for m in range(4, KC):
                merged_high(m)
            for n in range(20, 24):
                turned_high(n, memT_hi, n // 2 - 10)
            for m in range(4, KC + 4):
                prep(U_OUT + m)
            for b in range(2):
                for e in range(2):
                    turned_high(24 + 2 * b + e, xT_hi, b)
            for k in range(KC):
                prep(U_MV + k + 4)
                if k in (1, 4):
                    b = 2 + (k == 4)
                    for e in range(2):
                        turned_high(24 + 2 * b + e, xT_hi, b)
            act.wait_ge(unit_used, U_MV + KC)
            for b in range(MB):
                for half in range(2):
                    nc.scalar.activation(vm[:, b, half * HALF:(half + 1) * HALF], bank(4 + 2 * b + half), copy).then_inc(vm_done, 1)
            for h in range(MEM_HEADS + 1):
                if h < MEM_HEADS:
                    for m in range(2):
                        n, o = U_MQ + 2 * h + m, O_MQ + 2 * h + m
                        prep(n + 4)
                        nc.scalar.activation(qm[:, 2 * h + m, :], output(n, o), copy, scale=MEM_SCALE).then_inc(proj_free[o % 2], 1)
                if h >= 1:
                    act.wait_ge(mt_full, 2 * h - 1)
                    nc.scalar.activation(probT[:, 0:HALF], bank(4), copy).then_inc(mt_free[0], 1)
                if h < MEM_HEADS:
                    exponentials(HEADS + h, at_swa)
                if h >= 1:
                    for e in range(2):
                        m = 2 * (h - 1) + e
                        act.wait_ge(om_full, m + 1)
                        high(om_hi[:, m, :], bank(6 + e), om_hi_done)
            for m in range(4, KC + 3):
                prep(U_MO + m)
            for n in range(32, 40):
                turned_high(n, xT_hi, n // 2 - 16)
            ffn(1, U_FFN2)

        @block.vector
        def _(dve):
            def low(dst, src, hi, done):
                nc.vector.tensor_tensor(dst, src, hi.bitcast(F32), ALU.subtract).then_inc(done, 1)

            def split(n, i=None):
                dve.wait_ge(unit_hi, n + 1 if i is None else i * 6 + (n + 1))
                src, dst, hi = raw[:, n % RAW, :], ring_lo[:, n % RING, :], ring_hi[:, n % RING, :]
                if n == U_F:
                    src, dst = forget_views(n, ring_lo)
                    hi = forget_views(n, ring_hi)[1]
                low(dst, src, hi, unit_lo)

            def turned_low(n, hi, lo, b):
                dve.wait_ge(xt_hi, n + 1)
                e = n % 2
                at = (slice(None), slice(4 * e, 4 * e + 4), slice(b * P, (b + 1) * P))
                low(lo[at], turned(2 + e), hi[at], xt_lo)

            def scale_residual(x, blocks, turned_uses=None):
                for b in blocks:
                    if turned_uses is not None:
                        dve.wait_ge(xt_full, turned_uses + 2 * b + 2)
                    nc.vector.tensor_scalar(x[:, b, :], x[:, b, :], ALPHA, None, ALU.mult).then_inc(scaled, 1)

            def add_tile(x, j, src, done):
                at = (slice(None), j // 2, slice(HALF * (j % 2), HALF * (j % 2 + 1)))
                nc.vector.tensor_tensor(x[at], x[at], src, ALU.add).then_inc(done, 1)

            def block_stats(n, x, b, done, count):
                dve.wait_ge(done, count)
                for e in range(2):
                    nc.vector.bn_stats(stats[:, b, e, :], x[:, b, HALF * e:HALF * (e + 1)]).then_inc(stats_done, 1)
                dve.wait_ge(stats_done, 2 * (n * TB + b) + 2)
                nc.vector.bn_aggr(mv[:, b, :], stats[:, b, :, :]).then_inc(mean_done, 1)

            def normalize(n, x, b):
                if b == 0:
                    dve.wait_ge(gains_in, 32 * (n + 1))
                dve.wait_ge(mean_done, n * TB + b + 1)
                nc.vector.scalar_tensor_tensor(out=x[:, b, :], in0=x[:, b, :], scalar=mv[:, b, 0:1], in1=ln_g[:, :],
                                               op0=ALU.subtract, op1=ALU.mult).then_inc(centred, 1)
                dve.wait_ge(rstd_done, n * TB + b + 1)
                dve.wait_ge(centred, n * TB + b + 1)
                nc.vector.scalar_tensor_tensor(out=x[:, b, :], in0=x[:, b, :], scalar=rstd[:, b:b + 1], in1=ln_b[:, :],
                                               op0=ALU.mult, op1=ALU.add).then_inc(ln_done, 1)

            def ffn(f, n0, x):
                chunk0, pair0 = 2 * FF_PAIRS * f, FF_PAIRS * f

                def hidden(side, n, chunk, i=None):
                    dve.wait_ge(sig_done, chunk + 1 if i is None else i * 2 + (chunk + 1))
                    nc.vector.tensor_tensor(hf[:, side, :], sig[:, side, :], bank(2 * side), ALU.mult).then_inc(gated, 1)
                    dve.wait_ge(unit_used, n + 1 if i is None else i * 6 + (n + 1))
                    dve.wait_ge(gated, chunk + 1 if i is None else i * 2 + (chunk + 1))
                    nc.vector.scalar_tensor_tensor(out=hf[:, side, :], in0=hf[:, side, :], scalar=0.5, in1=bank(2 * side + 1),
                                                   op0=ALU.mult, op1=ALU.mult).then_inc(h_full, 1)

                def hidden_low(side, chunk, i=None):
                    dve.wait_ge(h_hi_done, chunk + 1 if i is None else i * 2 + (chunk + 1))
                    low(h_lo[:, side, :], hf[:, side, :], h_hi[:, side, :], h_lo_done)

                def add_down(js, n, pair, i=None):
                    for j in js:
                        if j < 7:
                            full = 7 * pair + j + 1
                            dve.wait_ge(down_full, full if i is None else i * 7 + full)
                        else:
                            dve.wait_ge(unit_used, n + 1 if i is None else i * 6 + (n + 1))
                        was = 8 * pair + j - 7
                        if i is None:
                            dve.wait_ge(down_free, was)
                        elif was > 0:
                            dve.wait_ge(down_free, i * 8 + was)
                        else:
                            dve.wait_ge(down_free, i * 8 + max(was, 0))
                        add_tile(x, j, bank(4 + j % 4), down_free)

                split(n0 + 3)
                hidden(0, n0 + 1, chunk0)
                split(n0 + 4)
                split(n0 + 5)
                hidden_low(0, chunk0)
                dve.wait_ge(scaled, TB * (1 + 3 * f))
                n = n0 + 4
                with dve.Fori(0, FF_PAIRS - 1) as i:
                    hidden(1, n - 1, chunk0 + 1, i)
                    split(n + 2, i)
                    split(n + 3, i)
                    split(n + 4, i)
                    hidden_low(1, chunk0 + 1, i)
                    split(n + 5, i)
                    split(n + 6, i)
                    hidden(0, n + 1, chunk0 + 2, i)
                    add_down((0, 1), n + 3, pair0, i)
                    split(n + 7, i)
                    add_down(range(2, 8), n + 3, pair0, i)
                    hidden_low(0, chunk0 + 2, i)
                last = n0 + 6 * FF_PAIRS - 1
                hidden(1, last - 2, chunk0 + 2 * FF_PAIRS - 1)
                hidden_low(1, chunk0 + 2 * FF_PAIRS - 1)
                for b in range(TB):
                    add_down((2 * b, 2 * b + 1), last, pair0 + FF_PAIRS - 1)
                    block_stats(3 * f, x, b, down_free, 8 * (pair0 + FF_PAIRS - 1) + 2 * b + 2)
                    if b >= 1:
                        normalize(3 * f, x, b - 1)
                    if f == 0:
                        split(U_MK + b)
                normalize(3 * f, x, TB - 1)
                if f == 0:
                    split(U_MK + TB)

            for n in range(8):
                turned_low(n, xT_hi, xT_lo, n // 2)
                if n in (3, 5, 7):
                    split((n - 3) // 2)
            for n in range(8, 12):
                turned_low(n, memT_hi, memT_lo, n // 2 - 4)
            scale_residual(xa, range(TB), 0)
            dve.wait_ge(bias_turned, 1)
            nc.vector.tensor_scalar(b_gate[:, :, :].rearrange("p g m -> p (g m)"), bank(4)[:, 0:2 * KC], 0.5, None, ALU.mult)\
                .then_inc(bias_made, 1)
            nc.vector.tensor_copy(b_f[:, :], bank(4)[:, 2 * KC:2 * KC + 1]).then_inc(bias_made, 1)
            dve.wait_ge(consts, 2)
            nc.vector.tensor_reduce(pick_part[:, 0:6], pick[:, :, :], AX.X, ALU.add).then_inc(dve_consts, 1)
            dve.wait_ge(dve_consts, 1)
            nc.vector.tensor_reduce(pick_part[:, 6:8], pick_part[:, 0:6].rearrange("p (a b) -> p a b", a=2), AX.X, ALU.add)\
                .then_inc(dve_consts, 1)
            nc.vector.tensor_reduce(pick_head[:, :], pick[:, :, :].rearrange("p k h -> p h k"), AX.X, ALU.add)\
                .then_inc(dve_consts, 1)
            dve.wait_ge(dve_consts, 2)
            nc.vector.tensor_scalar(pick_part[:, 0:3], pick_part[:, 0:3], -1.0, None, ALU.mult).then_inc(dve_consts, 1)
            ffn(0, U_FFN1, xa)
            for m in range(KC):
                if m >= 1:
                    split(U_MK + m + 4)
                if m % 2 == 1:
                    for e in range(2):
                        turned_low(12 + m - 1 + e, xT_hi, xT_lo, m // 2)

            ropes = [0]

            def rotate(x, n):
                if ropes[0]:
                    dve.wait_ge(rope_done, ropes[0])
                ropes[0] += 1
                dve.wait_ge(t_full, n + 1)
                nc.vector.tensor_tensor(rot[:, :], bank(5 + n % 2), sin_t[:, :], ALU.mult).then_inc(t_free[n % 2], 1)
                nc.vector.tensor_tensor(x, x, cos_t[:, :], ALU.mult).then_inc(rope_cos, 1)
                t_is_out(dve, n)
                dve.wait_ge(rope_cos, ropes[0])
                nc.vector.tensor_tensor(x, x, rot[:, :], ALU.add).then_inc(rope_done, 1)

            split(U_F + 4)
            proj_is_out(dve, O_F)
            nc.vector.scalar_tensor_tensor(out=fe[:, :], in0=fz[:, :], scalar=-1.0, in1=fz[:, :], op0=ALU.mult,
                                           op1=ALU.max).then_inc(f_dve, 1)
            dve.wait_ge(f_act, 2)
            nc.vector.scalar_tensor_tensor(out=fe[:, :], in0=fz[:, :], scalar=0.0, in1=fb[:, :], op0=ALU.min,
                                           op1=ALU.subtract).then_inc(f_dve, 1)
            split(U_KS + 4)
            dve.wait_ge(t_full, T_F + 1)
            nc.vector.tensor_copy(lsn[:, :, :].rearrange("p k c -> p (k c)"), bank(5 + T_F % 2)).then_inc(t_free[T_F % 2], 1)
            split(U_VS + 4)
            dve.wait_ge(angles_in, 32)
            rotate(kraw[:, :], T_KS)
            dve.wait_ge(t_full, T_C + 1)
            c = bank(5 + T_C % 2)
            nc.vector.tensor_copy(c_hi[:, :], c).then_inc(f_dve, 1)
            dve.wait_ge(f_dve, 3)
            nc.vector.tensor_tensor(fz[:, :], c, c_hi[:, :], ALU.subtract).then_inc(t_free[T_C % 2], 1)
            t_is_out(dve, T_C)
            nc.vector.tensor_copy(c_mid[:, :], fz[:, :]).then_inc(f_dve, 1)
            dve.wait_ge(f_dve, 4)
            nc.vector.tensor_tensor(fe[:, :], fz[:, :], c_mid[:, :], ALU.subtract).then_inc(f_dve, 1)
            dve.wait_ge(f_dve, 5)
            nc.vector.tensor_copy(c_lo[:, :], fe[:, :]).then_inc(f_dve, 1)
            dve.wait_ge(f_dve, 6)
            dve.wait_ge(dve_consts, 4)
            for side, (first, acc, dst) in enumerate(((3, fa, c_q), (0, fb, c_k))):
                nc.vector.tensor_scalar(acc[:, :], c_hi[:, :], pick_part[:, first:first + 1], pick_part[:, 6 + side:7 + side],
                                        ALU.mult, ALU.add).then_inc(f_dve, 1)
                dve.wait_ge(f_dve, 7 + side)
                nc.vector.scalar_tensor_tensor(out=acc[:, :], in0=c_mid[:, :], scalar=pick_part[:, first + 1:first + 2],
                                               in1=acc[:, :], op0=ALU.mult, op1=ALU.add).then_inc(c_made, 1)
                dve.wait_ge(c_made, 1 + 2 * side)
                nc.vector.scalar_tensor_tensor(out=dst[:, :], in0=c_lo[:, :], scalar=pick_part[:, first + 2:first + 3],
                                               in1=acc[:, :], op0=ALU.mult, op1=ALU.add).then_inc(c_made, 1)
            split(U_QS + 4)
            dve.wait_ge(t_full, T_VS + 1)
            nc.vector.tensor_copy(vs[:, :, :].rearrange("p k c -> p (k c)"), bank(5 + T_VS % 2)).then_inc(t_free[T_VS % 2], 1)
            for m in range(1, 4):
                split(U_QS + m + 4)
                rotate(qs[:, m - 1, :], T_QS + m - 1)

            def copied_probs(H):
                n = head_uses(H)[1]
                dve.wait_ge(t_full, n + 1)
                w = 3 * P if H < SWA_HEADS else HALF
                nc.vector.tensor_copy(probT[:, HALF:HALF + w], bank(5 + n % 2)[:, 0:w]).then_inc(t_free[n % 2], 1)

            def maxima(H, at, sink=None):
                if H == 0:
                    dve.wait_ge(small_in, 48)
                dve.wait_ge(s_full, H + 1)
                if len({w for _, w in at.values()}) == 1:
                    nc.vector.tensor_reduce(top[:, :], sc[:, 0:TB * WINDOW].rearrange("p (q k) -> p q k", q=TB), AX.X, ALU.max)\
                        .then_inc(top_done, 1)
                else:
                    for q, (c0, w) in at.items():
                        ins = nc.vector.tensor_reduce(top[:, q:q + 1], sc[:, c0:c0 + w], AX.X, ALU.max)
                    ins.then_inc(top_done, 1)
                dve.wait_ge(top_done, H + 1)
                if sink is None:
                    nc.vector.tensor_scalar(ntop[:, :], top[:, :], -1.0, None, ALU.mult).then_inc(ntop_done, 1)
                else:
                    nc.vector.tensor_scalar(ntop[:, :], top[:, :], sinks[:, sink:sink + 1], -1.0, ALU.max, ALU.mult)\
                        .then_inc(ntop_done, 1)

            def normalize_probs(H, at, sink=None):
                dve.wait_ge(exp_done, H + 1)
                if sink is not None:
                    nc.vector.tensor_tensor(rsum[:, :], rsum[:, :], esink[:, :], ALU.add).then_inc(sink_added, 1)
                    dve.wait_ge(sink_added, sink + 1)
                nc.vector.reciprocal(rinv[:, :], rsum[:, :]).then_inc(inverse_done, 1)
                dve.wait_ge(inverse_done, H + 1)
                for q, (c0, w) in sorted(at.items()):
                    ins = nc.vector.tensor_scalar(prob[:, c0:c0 + w], prob[:, c0:c0 + w], rinv[:, q:q + 1], None, ALU.mult)
                ins.then_inc(p_done, 1)

            def pair_low(H):
                m = H // 2
                dve.wait_ge(o_hi, m + 1)
                hi, lo = (os_hi, os_lo) if m < 4 else (of_hi, of_lo)
                low(lo[:, m % 4, :], bank(7), hi[:, m % 4, :], o_lo)

            def branch_output(n, o, e):
                if e == 0:
                    dve.wait_ge(branch_full, branches[0] + 1)
                    branches[0] += 1
                else:
                    dve.wait_ge(unit_used, n + 1)
                return bank((o + e) % 2)

            branches = [0]
            at_swa = {q: (WINDOW * q, WINDOW) for q in range(TB)}
            for H in range(HEADS):
                for u in fill(H % 8):
                    n = (U_QF if H < SWA_HEADS else U_G0) + u
                    split(n + 4)
                    if H < SWA_HEADS and 4 <= u < 8:
                        m, o = u - 4, O_QF + u
                        dve.wait_ge(unit_used, n + 1)
                        nc.vector.tensor_copy(kf[0:HD, 2 * m, :], bank(o % 2)[0:HD, :])
                        nc.vector.tensor_copy(kf[HD:P, 2 * m + 1, :], bank(o % 2)[HD:P, :]).then_inc(proj_free[o % 2], 1)
                    elif H >= SWA_HEADS and u % 3 == 2:
                        o = O_G0 + 4 * (u // 3) + 2
                        for e in range(2):
                            m = 2 * (u // 3) + e
                            proj_is_out(dve, o + e - 2)
                            nc.vector.scalar_tensor_tensor(out=part[:, m, :], in0=gate[:, e, :], scalar=1.0,
                                                           in1=branch_output(n, o, e), op0=ALU.add, op1=ALU.mult)\
                                .then_inc(proj_free[(o + e) % 2], 1)
                if H == 0:
                    rotate(qs[:, 3, :], T_QS + 3)
                if H >= 1:
                    copied_probs(H - 1)
                if H < SWA_HEADS:
                    for u in fill(H):
                        if u >= 8:
                            v, use = u - 8, T_VF[u - 8]
                            dve.wait_ge(t_full, use + 1)
                            nc.vector.tensor_copy(vf[:, :, v * P:(v + 1) * P], turned(5 + use % 2)).then_inc(t_free[use % 2], 1)
                at, sink = (at_swa, H) if H < SWA_HEADS else (FOX_AT, None)
                maxima(H, at, sink)
                if H >= 2 and H % 2 == 0:
                    pair_low(H - 1)
                normalize_probs(H, at, sink)

            def merged_low_part(m):
                dve.wait_ge(merged_hi, m + 1)
                hi, lo = (m0_hi, m0_lo) if m < 4 else (m1_hi, m1_lo)
                nc.vector.scalar_tensor_tensor(out=lo[:, m % 4, :], in0=part[:, m, :], scalar=0.5,
                                               in1=hi[:, m % 4, :].bitcast(F32), op0=ALU.mult, op1=ALU.subtract)\
                    .then_inc(merged_lo, 1)

            for u in range(12):
                n = U_G1 + u
                split(n + 4)
                if u == 0:
                    copied_probs(HEADS - 1)
                    pair_low(HEADS - 1)
                if u % 3 == 2:
                    o = O_G1 + 4 * (u // 3) + 2
                    for e in range(2):
                        m = 2 * (u // 3) + e
                        proj_is_out(dve, o + e - 2)
                        nc.vector.scalar_tensor_tensor(out=gate[:, e, :], in0=gate[:, e, :], scalar=1.0,
                                                       in1=branch_output(n, o, e), op0=ALU.add, op1=ALU.mult)\
                            .then_inc(proj_free[(o + e) % 2], 1)
                        proj_is_out(dve, o + e)
                        nc.vector.tensor_tensor(part[:, m, :], part[:, m, :], gate[:, e, :], ALU.add).then_inc(merged, 1)
                if u in (3, 6):
                    for m in (0, 1) if u == 3 else (2, 3):
                        merged_low_part(m)
            for m in range(4, KC):
                merged_low_part(m)
            for n in range(20, 24):
                turned_low(n, memT_hi, memT_lo, n // 2 - 10)
            dve.wait_ge(back, 16 * TB)
            scale_residual(xb, range(TB))

            def project_tiles(s, ln, n0, splits):
                dve.wait_ge(scaled, TB * (s + 2))
                for b in range(TB):
                    for n in splits[b]:
                        split(n)
                    for e in range(2):
                        j = 2 * b + e
                        if j < 6:
                            dve.wait_ge(tile_full, 6 * s + j + 1)
                        else:
                            dve.wait_ge(unit_used, n0 + KC)
                        add_tile(xb, j, bank(j), tile_free)
                    block_stats(ln, xb, b, tile_free, 8 * s + 2 * b + 2)
                    if b >= 1:
                        normalize(ln, xb, b - 1)
                normalize(ln, xb, TB - 1)

            u = U_OUT
            project_tiles(0, 1, u, (range(u + 4, u + 8), (), (), range(u + 8, u + 11)))
            split(u + 11)
            for b in range(2):
                for e in range(2):
                    turned_low(24 + 2 * b + e, xT_hi, xT_lo, b)
            for k in range(KC):
                split(U_MV + k + 4)
                if k in (1, 4):
                    b = 2 + (k == 4)
                    for e in range(2):
                        turned_low(24 + 2 * b + e, xT_hi, xT_lo, b)
            scale_residual(xb, range(TB), 24)
            for h in range(MEM_HEADS + 1):
                if h < MEM_HEADS:
                    for m in range(2):
                        split(U_MQ + 2 * h + m + 4)
                if h >= 1:
                    dve.wait_ge(mt_full, 2 * h)
                    nc.vector.tensor_copy(probT[:, HALF:2 * HALF], bank(5)).then_inc(mt_free[1], 1)
                if h < MEM_HEADS:
                    maxima(HEADS + h, at_swa)
                    normalize_probs(HEADS + h, at_swa)
                if h >= 1:
                    for e in range(2):
                        m = 2 * (h - 1) + e
                        dve.wait_ge(om_hi_done, m + 1)
                        low(om_lo[:, m, :], bank(6 + e), om_hi[:, m, :], om_lo_done)
            u = U_MO
            project_tiles(1, 2, u, (range(u + 4, u + 8), (), (), range(u + 8, u + 11)))
            for n in range(32, 40):
                turned_low(n, xT_hi, xT_lo, n // 2 - 16)
            scale_residual(xb, range(TB), 32)
            ffn(1, U_FFN2, xb)


_INS = ["x", "mem", "ffn1_w_gate", "ffn1_w_up", "ffn1_w_down", "ln1_g", "ln1_b", "mix_w_in", "mix_b_gate",
        "mix_b_forget", "swa_sinks", "mix_w_branch_swa", "mix_w_branch_fox", "mix_w_out", "ln2_g", "ln2_b",
        "mem_w_q", "mem_w_k", "mem_w_v", "mem_w_o", "ln3_g", "ln3_b", "ffn2_w_gate", "ffn2_w_up", "ffn2_w_down",
        "ln4_g", "ln4_b"]


def kernel(**inputs):
    import numpy as _np
    import concourse.bacc as _bacc
    from concourse.bass_utils import run_bass_kernel_spmd as _run

    nc = _bacc.Bacc("TRN2", target_bir_lowering=False, num_devices=1)
    arrays, tensors = {}, {}
    for name in _INS:
        a = _np.ascontiguousarray(inputs[name])
        arrays[f"in_{name}"] = a
        ap = nc.dram_tensor(f"in_{name}", a.shape, F32, kind="ExternalInput").ap()
        if len(a.shape) == 3:
            ap = ap[0]
        tensors[name] = ap
    half = HD // 2
    freq = _np.float32(ROPE_THETA) ** (-_np.arange(half, dtype=_np.float32) / half)
    angle = _np.arange(SEQ, dtype=_np.float32)[None, :] * _np.tile(freq, P // half)[:, None]
    arrays["in_rope"] = _np.stack([_np.cos(angle), _np.sin(angle)])
    tensors["rope"] = nc.dram_tensor("in_rope", (2, P, SEQ), F32, kind="ExternalInput").ap()
    out = nc.dram_tensor("out", (1, SEQ, D), F32, kind="ExternalOutput").ap()
    spill = nc.dram_tensor("x_spill", (SEQ, D), F32, kind="Internal").ap()
    program(nc, tensors, out[0], spill)
    r = _run(nc, [arrays], core_ids=[0])
    return r.results[0]["out"]
```

```python
from contextlib import ExitStack

import concourse.bass as bass
from concourse import mybir

F32 = mybir.dt.float32
F32R = mybir.dt.float32r
BF16 = mybir.dt.bfloat16
ACT = mybir.ActivationFunctionType
ALU = mybir.AluOpType
AX = mybir.AxisListType

P = 128
D = 1024
SEQ = 512
TB = SEQ // P
KC = D // P
HALF = 512
HD = 64
SWA_HEADS, SWA_KV, FOX_HEADS = 8, 2, 8
WINDOW = 256
CHUNK = 64
MEM = 256
MB = MEM // P
MEM_HEADS = 4
D_FF = 2816
FF_PAIRS = D_FF // P // 2
ALPHA = 2.0 ** 0.25
LN_EPS = 1e-5
ROPE_THETA = 10000.0
NEG = -1e30
QK_SCALE = HD ** -0.5
MEM_SCALE = (D // MEM_HEADS) ** -0.5

C_QS = 0
C_KS = C_QS + SWA_HEADS * HD
C_VS = C_KS + SWA_KV * HD
C_QF = C_VS + SWA_KV * HD
C_KF = C_QF + FOX_HEADS * HD
C_VF = C_KF + FOX_HEADS * HD
C_F = C_VF + FOX_HEADS * HD
C_G = C_F + FOX_HEADS

U_FFN1 = 0
U_MK = U_FFN1 + 6 * FF_PAIRS
U_F = U_MK + KC
U_KS = U_F + 1
U_VS = U_KS + 1
U_QS = U_VS + 1
U_QF = U_QS + 4
U_KF = U_QF + 4
U_VF = U_KF + 4
U_G0 = U_VF + 4
U_G1 = U_G0 + 12
U_OUT = U_G1 + 12
U_MV = U_OUT + KC
U_MQ = U_MV + KC
U_MO = U_MQ + KC
U_FFN2 = U_MO + KC
U_END = U_FFN2 + 6 * FF_PAIRS
T_MEM = 2 * TB
T_X1 = T_MEM + 2 * MB
T_MEM2 = T_X1 + 2 * TB
T_X2 = T_MEM2 + 2 * MB
T_X3 = T_X2 + 2 * TB
FOX_COPIES = P // FOX_HEADS
AFTER_MK = (1, 3, 4, 5)
RAW = 3
RING = 6
AHEAD = 3

O_MK = 0
O_F = O_MK + KC
O_KS = O_F + 1
O_VS = O_KS + 1
O_QS = O_VS + 1
O_QF = O_QS + 4
O_KF = O_QF + 4
O_VF = O_KF + 4
O_G0 = O_VF + 4
O_G1 = O_G0 + 16
O_MQ = O_G1 + 16
O_END = O_MQ + KC

HEADS = SWA_HEADS + FOX_HEADS

T_F, T_KS, T_C, T_VS, T_QS = 0, 1, 2, 3, 4


def fill(slot):
    first = 3 * (slot // 2) + (slot % 2)
    return range(first, first + 1 + slot % 2)


def t_uses():
    n, heads, values = T_QS + 4, [], {}
    for slot in range(HEADS + 1):
        if slot >= 1:
            heads.append(n)
            n += 2 if slot - 1 < SWA_HEADS else 3
        if slot < SWA_HEADS:
            for u in fill(slot):
                if u >= 8:
                    values[u - 8] = n
                    n += 1
    return heads, values, n


T_HEAD, T_VF, T_END = t_uses()

FOX_AT = {3: (0, 512), 2: (512, 384), 0: (896, 128), 1: (1024, 256)}
FOX_T = {0: 0, 1: 512, 2: 1024, 3: 896}
SWA_T = {0: 0, 1: 256, 2: 512, 3: 768}


def fox_transposes():
    every = [(q, k, FOX_T[k] + P * (q - k)) for k in range(TB) for q in range(k, TB)]
    return [[x for x in every if x[2] // HALF == b] for b in range(3)]


def swa_transposes():
    every = [(q, k, SWA_T[k] + P * (q - k)) for k in range(TB) for q in (k, k + 1) if q < TB]
    return [[x for x in every if x[2] // HALF == b] for b in range(2)]


def program(nc, t, out, x_spill):
    ctx = ExitStack()
    with ctx:
        base = [(nc.sbuf_base + 63) // 64 * 64]

        def place(name, shape, dt, at=None):
            size = 2 if dt == BF16 else 4
            for n in shape[1:]:
                size *= n
            where = base[0] if at is None else at
            if at is None:
                base[0] += (size + 31) // 32 * 32
            return nc.alloc_sbuf_tensor_at(name, shape, dt, offset=where)

        def zone(kib):
            where = base[0]
            base[0] += kib * 1024
            return where

        def sem(name):
            return ctx.enter_context(nc.semaphore(name))

        ring_hi = place("ring_hi", [P, RING, D], F32R)
        ring_lo = place("ring_lo", [P, RING, D], F32R)
        z_xh, z_xl, z_r = zone(16), zone(16), zone(32)
        xT_hi = place("xT_hi", [P, KC, SEQ], F32R, z_xh)
        xT_lo = place("xT_lo", [P, KC, SEQ], F32R, z_xl)
        h_hi = place("h_hi", [P, 2, SEQ], F32R, z_r)
        h_lo = place("h_lo", [P, 2, SEQ], F32R, z_r + 4096)
        os_hi = place("os_hi", [P, 4, SEQ], F32R, z_r)
        os_lo = place("os_lo", [P, 4, SEQ], F32R, z_r + 8192)
        of_hi = place("of_hi", [P, 4, SEQ], F32R, z_r + 16384)
        of_lo = place("of_lo", [P, 4, SEQ], F32R, z_r + 24576)
        memT_hi = place("memT_hi", [P, KC, MEM], F32R, z_r + 16384)
        memT_lo = place("memT_lo", [P, KC, MEM], F32R, z_r + 24576)
        m0_hi = place("m0_hi", [P, 4, SEQ], F32R, z_r)
        m0_lo = place("m0_lo", [P, 4, SEQ], F32R, z_r + 8192)
        m1_hi = place("m1_hi", [P, 4, SEQ], F32R, z_xh)
        m1_lo = place("m1_lo", [P, 4, SEQ], F32R, z_xl)
        om_hi = place("om_hi", [P, KC, SEQ], F32R, z_r)
        om_lo = place("om_lo", [P, KC, SEQ], F32R, z_r + 16384)

        raw = place("raw", [P, RAW, D], F32)
        z_a, z_b, z_q, z_v = zone(16), zone(16), zone(8), zone(8)
        z_p = zone(10)
        xa = place("xa", [P, TB, D], F32, z_a)
        xb = place("xb", [P, TB, D], F32, z_b)
        part = place("part", [P, KC, SEQ], F32, z_a)
        qm = place("qm", [P, KC, SEQ], F32, z_a)
        qs = place("qs", [P, 4, SEQ], F32, z_a)
        ks_hh = place("ks_hh", [P, SWA_KV, SEQ], F32R, z_a + 8192)
        ks_ll = place("ks_ll", [P, SWA_KV, SEQ], F32R, z_a + 12288)
        kf = place("kf", [P, 4, SEQ], F32, z_b)
        q_st = place("q_st", [P, 2, SEQ], F32R, z_b + 8192)
        k_hh = place("k_hh", [P, 2, SEQ], F32R, z_b + 12288)
        k_low = place("k_low", [P, 2, SEQ], F32R)
        qf = place("qf", [P, 4, SEQ], F32, z_q)
        vf = place("vf", [P, TB, FOX_HEADS * HD], F32, z_v)
        vm = place("vm", [P, MB, D], F32, z_q)
        mem_in = place("mem_in", [P, MB, D], F32, z_v)
        sig = place("sig", [P, 2, SEQ], F32, z_q)
        hf = place("hf", [P, 2, SEQ], F32, z_q + 4096)
        fz = place("fz", [P, SEQ], F32, z_v)
        fe = place("fe", [P, SEQ], F32, z_v + 2048)
        fa = place("fa", [P, SEQ], F32, z_v + 4096)
        fb = place("fb", [P, SEQ], F32, z_v + 6144)
        prob = place("prob", [P, 1280], F32, z_p)
        probT = place("probT", [P, 1280], F32, z_p + 5120)
        ln_g = place("ln_g", [P, D], F32, z_p)
        ln_b = place("ln_b", [P, D], F32, z_p + 4096)
        lsn = place("lsn", [P, TB, P], F32, z_p)
        tri_f = place("tri_f", [P, SEQ], F32, z_p + 5120)
        rot = place("rot", [P, SEQ], F32, z_p + 2048)
        kraw = place("kraw", [P, SEQ], F32, z_p + 7168)
        cos_t = place("cos_t", [P, SEQ], F32, z_q + 4096)
        sin_t = place("sin_t", [P, SEQ], F32, z_q + 6144)
        km = place("km", [P, KC, MEM], F32)
        vs = place("vs", [P, TB, P], F32)
        gate = place("gate", [P, 2, SEQ], F32)
        c_hi = place("c_hi", [P, SEQ], BF16, z_p + 4096)
        c_mid = place("c_mid", [P, SEQ], BF16, z_p)
        c_lo = place("c_lo", [P, SEQ], BF16, z_p + 1024)
        c_q = place("c_q", [P, SEQ], BF16)
        c_k = place("c_k", [P, SEQ], BF16)
        c_qh = place("c_qh", [P, 2, SEQ], BF16)
        ident = place("ident", [P, P], F32)
        ident_b = place("ident_b", [P, P], BF16)
        swap = place("swap", [P, P], F32)
        mask_s = place("mask_s", [P, WINDOW], BF16)
        mask_0 = place("mask_0", [P, WINDOW], BF16)
        mask_c = place("mask_c", [P, P], BF16)
        pick = place("pick", [P, 6, FOX_HEADS], F32)
        pick_part = place("pick_part", [P, 8], F32)
        pick_head = place("pick_head", [P, FOX_HEADS], F32)
        bias_rows = place("bias_rows", [2 * KC + 1, P], F32, z_p + 8192)
        b_gate = place("b_gate", [P, 2, KC], F32)
        b_f = place("b_f", [P, 1], F32)
        sinks = place("sinks", [P, SWA_HEADS], F32)
        stats = place("stats", [P, TB, 2, 6], F32)
        mv = place("mv", [P, TB, 2], F32)
        rstd = place("rstd", [P, TB], F32)
        neg_mean = place("neg_mean", [P, TB], F32)
        shift = place("shift", [P, TB], F32)
        veps = place("veps", [P, TB], F32)
        expo = place("expo", [P, 1], F32)
        top = place("top", [P, 4], F32)
        ntop = place("ntop", [P, 4], F32)
        rsum = place("rsum", [P, 4], F32)
        esink = place("esink", [P, 4], F32)
        rinv = place("rinv", [P, 4], F32)

        ps = [ctx.enter_context(nc.psum_tensor(f"bank{i}", [P, HALF], F32)) for i in range(2)]
        sc = ctx.enter_context(nc.psum_tensor("banks_scores", [P, 3 * HALF], F32))
        ps += [sc[:, HALF * i:HALF * (i + 1)] for i in range(3)]
        ps += [ctx.enter_context(nc.psum_tensor(f"bank{i}", [P, HALF], F32)) for i in range(5, 8)]

        landed = [sem(f"unit_landed{i}") for i in range(RAW)]
        unit_hi = sem("unit_hi")
        unit_lo = sem("unit_lo")
        unit_used = sem("unit_used")
        x_in = [sem(f"x_in{i}") for i in range(TB)]
        mem_in_ok = sem("mem_in_ok")
        small_in, bias_turned, bias_made = sem("small_in"), sem("bias_turned"), sem("bias_made")
        gains_in = sem("gains_in")
        pool_step = sem("pool_step")
        consts = sem("consts")
        zeroed = sem("zeroed")
        dve_consts = sem("dve_consts")
        xt_full, xt_hi, xt_lo = sem("xt_full"), sem("xt_hi"), sem("xt_lo")
        sig_done, gated = sem("sig_done"), sem("gated")
        h_full, h_hi_done, h_lo_done = sem("h_full"), sem("h_hi_done"), sem("h_lo_done")
        scaled = sem("scaled")
        down_full, down_free = sem("down_full"), sem("down_free")
        stats_done, mean_done, eps_added, rstd_done = sem("stats_done"), sem("mean_done"), sem("eps_added"), sem("rstd_done")
        shift_done = sem("shift_done")
        standard = sem("standard")
        gained, ln_done = sem("gained"), sem("ln_done")
        last_done = sem("last_done")
        proj_free = [sem(f"proj_free{i}") for i in range(2)]
        branch_full = sem("branch_full")
        f_act, f_dve = sem("f_act"), sem("f_dve")
        t_full = sem("t_full")
        t_free = [sem(f"t_free{i}") for i in range(2)]
        s_full, top_done, ntop_done, exp_done = sem("s_full"), sem("top_done"), sem("ntop_done"), sem("exp_done")
        sink_added, inverse_done, p_done = sem("sink_added"), sem("inverse_done"), sem("p_done")
        o_full, o_hi, o_lo = sem("o_full"), sem("o_hi"), sem("o_lo")
        ks_split = sem("ks_split")
        stack_hi, stack_lo = sem("stack_hi"), sem("stack_lo")
        c_made, cq_made = sem("c_made"), sem("cq_made")
        angles_in, rope_cos, rope_done, ks_made = sem("angles_in"), sem("rope_cos"), sem("rope_done"), sem("ks_made")
        fox_gated, merged, merged_hi, merged_lo = sem("fox_gated"), sem("merged"), sem("merged_hi"), sem("merged_lo")
        tile_full, tile_free = sem("tile_full"), sem("tile_free")
        vm_done = sem("vm_done")
        mt_full = sem("mt_full")
        mt_free = [sem(f"mt_free{i}") for i in range(2)]
        om_full, om_hi_done, om_lo_done = sem("om_full"), sem("om_hi_done"), sem("om_lo_done")
        spilled, back, stored = sem("spilled"), sem("back"), sem("stored")

        block = ctx.enter_context(nc.Block())

        def rows_of(H):
            own, other = slice(HD * (H % 2), HD * (H % 2 + 1)), slice(HD * (1 - H % 2), HD * (2 - H % 2))
            return own, other

        def query_key(H):
            if H < SWA_HEADS:
                return qs[:, H // 2, :], None
            m = (H - SWA_HEADS) // 2
            return qf[:, m, :], kf[:, m, :]

        def proj_is_out(eng, o):
            eng.wait_ge(proj_free[o % 2], o // 2 + 1)

        def t_is_out(eng, n):
            eng.wait_ge(t_free[n % 2], n // 2 + 1)

        def head_uses(H):
            n = T_HEAD[H]
            return range(n, n + (2 if H < SWA_HEADS else 3))

        def p_at(H, q, k):
            return WINDOW * q + P * (k - q + 1) if H < SWA_HEADS else FOX_AT[q][0] + P * k

        def bank(i):
            return ps[i][:, :]

        def xt_bank(n):
            if n < T_MEM:
                return n
            if n < T_X1:
                return 4 + (n - T_MEM)
            if n < T_MEM2:
                return 2 + n % 2
            if n < T_X2:
                return (2, 3, 4, 7)[n - T_MEM2]
            if n < T_X3:
                return (n - T_X2) % 4
            return n - T_X3

        def halves(n, b):
            if n == 3 and b == TB - 1:
                return slice(0, HALF), slice(HALF, D)
            return (slice(0, D),)

        def turned(i):
            return ps[i][:, :].rearrange("p (c n) -> p c n", n=P)

        def forget_views(n, ring):
            src = raw[:, n % RAW, 0:KC * FOX_HEADS].rearrange("p (k h) -> p k h", k=KC).unsqueeze(2)
            dst = ring[:, n % RING, :].rearrange("p (k r h) -> p k r h", k=KC, h=FOX_HEADS)
            return src.to_broadcast([P, KC, FOX_COPIES, FOX_HEADS]), dst

        @block.sync
        def _(sp):
            def load(n, src, form=None, off=None):
                dst = raw[:, n % RAW, :]
                if form == "columns":
                    dst = dst.rearrange("p (k c) -> p k c", k=KC)
                elif form == "branch":
                    dst = dst.rearrange("p (k c) -> p k c", k=4)
                elif form == "forget":
                    dst = raw[:, n % RAW, 0:KC * FOX_HEADS].rearrange("p (k c) -> p k c", k=KC)
                if off is not None:
                    sp.wait_ge(unit_lo, off + (n - RAW + 1))
                elif n >= RAW:
                    sp.wait_ge(unit_lo, n - RAW + 1)
                sp.dma_start(dst, src).then_inc(landed[n % RAW], 16)

            def columns(w, c0):
                return w.rearrange("(k p) c -> p k c", p=P)[:, :, c0:c0 + P]

            def rows(w, r):
                return w[r * P:(r + 1) * P, :]

            def load_x(blocks):
                for b in blocks:
                    sp.dma_start(xa[:, b, :], t["x"][b * P:(b + 1) * P, :]).then_inc(x_in[b], 16)

            def ffn_units(n0, w_gate, w_up, w_down):
                for m in range(2):
                    load(n0 + 2 * m, columns(w_gate, m * P), "columns")
                    load(n0 + 2 * m + 1, columns(w_up, m * P), "columns")
                    if n0 == U_FFN1 and m == 0:
                        load_x((2, 3))
                g = w_gate.rearrange("(k p) (m c) -> p k m c", p=P, c=P)
                u = w_up.rearrange("(k p) (m c) -> p k m c", p=P, c=P)
                d = w_down.rearrange("(m p) c -> p m c", p=P)
                n = n0 + 4
                with sp.Fori(0, FF_PAIRS - 1) as i:
                    for m in range(2):
                        chunk = bass.ds(i * 2 + (2 + m), 1)
                        load(n + 4 * m, g[:, :, chunk, :].rearrange("p k m c -> p k (m c)"), "columns", i * 6)
                        load(n + 4 * m + 1, u[:, :, chunk, :].rearrange("p k m c -> p k (m c)"), "columns", i * 6)
                        if m == 0:
                            for r in range(2):
                                load(n + 2 + r, d[:, bass.ds(i * 2 + r, 1), :].rearrange("p m c -> p (m c)"), None, i * 6)
                for r in range(2):
                    load(n0 + 6 * FF_PAIRS - 2 + r, rows(w_down, 2 * FF_PAIRS - 2 + r))

            load_x((0, 1))
            ffn_units(U_FFN1, t["ffn1_w_gate"], t["ffn1_w_up"], t["ffn1_w_down"])
            for m in range(KC):
                load(U_MK + m, columns(t["mem_w_k"], m * P), "columns")
            w_in = t["mix_w_in"]
            load(U_F, w_in.rearrange("(k p) c -> p k c", p=P)[:, :, C_F:C_F + FOX_HEADS], "forget")
            load(U_KS, columns(w_in, C_KS), "columns")
            load(U_VS, columns(w_in, C_VS), "columns")
            for first, col in ((U_QS, C_QS), (U_QF, C_QF), (U_KF, C_KF), (U_VF, C_VF)):
                for m in range(4):
                    load(first + m, columns(w_in, col + m * P), "columns")
            for g, (first, w) in enumerate(((U_G0, t["mix_w_branch_swa"]), (U_G1, t["mix_w_branch_fox"]))):
                for u in range(4):
                    for e in range(2):
                        load(first + 3 * u + e, columns(w_in, C_G + g * D + (2 * u + e) * P), "columns")
                    load(first + 3 * u + 2, w.rearrange("(k p) c -> p k c", p=P)[:, :, 2 * P * u:2 * P * (u + 1)], "branch")
            for m in range(KC):
                load(U_OUT + m, rows(t["mix_w_out"], m))
            for m in range(KC):
                load(U_MV + m, rows(t["mem_w_v"], m))
            for m in range(KC):
                load(U_MQ + m, columns(t["mem_w_q"], m * P), "columns")
            for m in range(KC):
                load(U_MO + m, rows(t["mem_w_o"], m))
            ffn_units(U_FFN2, t["ffn2_w_gate"], t["ffn2_w_up"], t["ffn2_w_down"])
            for b in range(TB - 1):
                sp.wait_ge(ln_done, 3 * TB + b + 1)
                sp.dma_start(out[b * P:(b + 1) * P, :], xb[:, b, :]).then_inc(stored, 16)
            for e in range(2):
                sp.wait_ge(last_done, e + 1)
                sp.dma_start(out[(TB - 1) * P:, e * HALF:(e + 1) * HALF], xb[:, TB - 1, e * HALF:(e + 1) * HALF])\
                    .then_inc(stored, 16)
            sp.wait_ge(stored, 16 * (TB + 1))

        @block.gpsimd
        def _(pool):
            steps = [0]

            def step(ins):
                steps[0] += 1
                ins.then_inc(pool_step, 1)
                pool.wait_ge(pool_step, steps[0])

            def load_gains(n, after=None):
                pool.dma_start(ln_g[:, :], t[f"ln{n}_g"].to_broadcast([P, D])).then_inc(gains_in, 16)
                pool.dma_start(ln_b[:, :], t[f"ln{n}_b"].to_broadcast([P, D])).then_inc(gains_in, 16)

            def load_mem():
                pool.dma_start(mem_in[:, :, :], t["mem"].rearrange("(b p) d -> p b d", p=P)).then_inc(mem_in_ok, 16)

            def inverse_deviation(n, b):
                count, col = n * TB + b + 1, slice(b, b + 1)
                pool.wait_ge(mean_done, count)
                nc.gpsimd.tensor_scalar(veps[:, col], mv[:, b, 1:2], LN_EPS, None, ALU.add).then_inc(eps_added, 1)
                nc.gpsimd.tensor_scalar(neg_mean[:, col], mv[:, b, 0:1], -1.0, None, ALU.mult).then_inc(eps_added, 1)
                pool.wait_ge(eps_added, 2 * count)
                nc.gpsimd.tensor_tensor(rstd[:, col], veps[:, col], expo[:, :], ALU.pow).then_inc(rstd_done, 1)
                pool.wait_ge(rstd_done, count)
                nc.gpsimd.tensor_tensor(shift[:, col], neg_mean[:, col], rstd[:, col], ALU.mult).then_inc(shift_done, 1)

            def add_bias(n, x, b):
                if b == 0:
                    pool.wait_ge(gains_in, 32 * (n + 1))
                pool.wait_ge(gained, n * TB + b + 1)
                nc.gpsimd.tensor_tensor(x[:, b, :], x[:, b, :], ln_b[:, :], ALU.add).then_inc(ln_done, 1)

            def layer_norm(n, x, lag):
                for b in range(TB + lag):
                    if b < TB:
                        inverse_deviation(n, b)
                    if 0 <= b - lag < TB - 1:
                        add_bias(n, x, b - lag)

            step(nc.gpsimd.memset(ident[:, :], 0.0))
            nc.gpsimd.affine_select(out=ident[:, :], in_=ident[:, :], compare_op=ALU.not_equal, fill=1.0, base=0,
                                    pattern=[[-1, P]], channel_multiplier=1).then_inc(consts, 1)
            pool.wait_ge(consts, 1)
            step(nc.gpsimd.memset(ident_b[:, :], 0.0))
            step(nc.gpsimd.affine_select(out=ident_b[:, :], in_=ident_b[:, :], compare_op=ALU.not_equal, fill=1.0, base=0,
                                         pattern=[[-1, P]], channel_multiplier=1))
            step(nc.gpsimd.memset(expo[:, :], -0.5))
            step(nc.gpsimd.memset(swap[:, :], 0.0))
            halves = swap[:, :].rearrange("p (a b c) -> p a b c", a=2, b=2)
            for b, (sign, first) in enumerate(((-1.0, -HD // 2), (1.0, 0))):
                step(nc.gpsimd.affine_select(out=halves[:, :, b, :], in_=halves[:, :, b, :], compare_op=ALU.not_equal, fill=sign,
                                             base=first, pattern=[[-HD, 2], [-1, HD // 2]], channel_multiplier=1))
            step(nc.gpsimd.memset(mask_s[:, :], NEG))
            step(nc.gpsimd.memset(mask_0[:, :], NEG))
            step(nc.gpsimd.memset(mask_s[0:CHUNK, CHUNK:3 * CHUNK], 0.0))
            step(nc.gpsimd.memset(mask_s[CHUNK:P, 2 * CHUNK:WINDOW], 0.0))
            step(nc.gpsimd.memset(mask_0[0:CHUNK, 2 * CHUNK:3 * CHUNK], 0.0))
            step(nc.gpsimd.memset(mask_0[CHUNK:P, 2 * CHUNK:WINDOW], 0.0))
            step(nc.gpsimd.memset(mask_c[:, :], 0.0))
            step(nc.gpsimd.affine_select(out=mask_c[:, :], in_=mask_c[:, :], compare_op=ALU.is_ge, fill=NEG, base=0,
                                         pattern=[[-1, P]], channel_multiplier=1))
            step(nc.gpsimd.memset(pick[:, :, :], 0.0))
            nc.gpsimd.affine_select(out=pick[:, :, :], in_=pick[:, :, :], compare_op=ALU.not_equal, fill=1.0, base=0,
                                    pattern=[[-FOX_HEADS, 6], [-1, FOX_HEADS]], channel_multiplier=1).then_inc(consts, 1)
            pool.wait_ge(consts, 2)
            pool.wait_ge(x_in[TB - 1], 16)
            load_mem()
            pool.wait_ge(unit_used, 1)
            load_gains(1)
            layer_norm(0, xa, 1)
            for b in range(TB):
                pool.wait_ge(ln_done, b + 1)
                pool.dma_start(x_spill[b * P:(b + 1) * P, :], xa[:, b, :]).then_inc(spilled, 16)
            for angles, row in ((cos_t, 0), (sin_t, 1)):
                pool.dma_start(angles[:, :], t["rope"][row]).then_inc(angles_in, 16)
            step(nc.gpsimd.memset(tri_f[:, :], 1.0))
            nc.gpsimd.affine_select(out=tri_f[:, :], in_=tri_f[:, :], compare_op=ALU.is_ge, fill=0.0, base=0,
                                    pattern=[[1, SEQ]], channel_multiplier=-1).then_inc(zeroed, 1)
            pool.wait_ge(zeroed, 1)
            pool.wait_ge(dve_consts, 4)
            pool.wait_ge(c_made, 2)
            for h in range(FOX_HEADS):
                if h >= 2:
                    pool.wait_ge(s_full, SWA_HEADS + h - 1)
                nc.gpsimd.tensor_scalar(c_qh[:, h % 2, :], c_q[:, :], pick_head[:, h:h + 1], None, ALU.mult).then_inc(cq_made, 1)
                pool.wait_ge(cq_made, h + 1)
            pool.wait_ge(s_full, HEADS)
            for b in range(TB):
                pool.dma_start(xb[:, b, :], x_spill[b * P:(b + 1) * P, :]).then_inc(back, 16)
            pool.wait_ge(o_full, HEADS)
            load_mem()
            load_gains(2)
            layer_norm(1, xb, 0)
            pool.wait_ge(om_full, KC)
            pool.wait_ge(ln_done, 2 * TB)
            load_gains(3)
            layer_norm(2, xb, 0)
            pool.wait_ge(ln_done, 3 * TB)
            load_gains(4)
            layer_norm(3, xb, 1)

        @block.tensor
        def _(pe):
            def parts(n):
                return ring_hi[:, n % RING, :], ring_lo[:, n % RING, :]

            def split_product(dst, hi, lo, mhi, mlo, start, stop):
                pe.matmul(dst, hi, mhi, start=start, stop=False)
                pe.matmul(dst, hi, mlo, start=False, stop=False)
                return pe.matmul(dst, lo, mhi, start=False, stop=stop)

            def ready(n, off=None):
                pe.wait_ge(unit_lo, n + 1 if off is None else off + (n + 1))

            def project(n, dst, acts=(xT_hi, xT_lo), width=SEQ):
                hi, lo = (r.rearrange("p (k c) -> p k c", k=KC) for r in parts(n))
                for k in range(KC):
                    mm = split_product(dst, hi[:, k, :], lo[:, k, :], acts[0][:, k, 0:width], acts[1][:, k, 0:width],
                                       k == 0, k == KC - 1)
                mm.then_inc(unit_used, 1)

            def turn(src, dst, c0):
                for c in range(4):
                    mm = pe.transpose(dst[:, c * P:(c + 1) * P], src[:, (c0 + c) * P:(c0 + c + 1) * P], ident[:, :])
                return mm

            def turn_rows(n, src):
                for e in range(2):
                    if T_X1 <= n + e < T_MEM2:
                        pe.wait_ge(xt_lo, n + e - 1)
                    elif T_X2 + 4 <= n + e < T_X3:
                        pe.wait_ge(xt_lo, n + e - 3)
                    turn(src, bank(xt_bank(n + e)), 4 * e).then_inc(xt_full, 1)

            def ffn(f, n0):
                def gate_up(side, n, chunk, i=None):
                    for m in range(2):
                        ready(n + m, None if i is None else i * 6)
                        if m == 0 and i is not None:
                            pe.wait_ge(h_full, i * 2 + (chunk - 1))
                        elif m == 0 and chunk >= 2:
                            pe.wait_ge(h_full, chunk - 1)
                        project(n + m, bank(2 * side + m))

                def half_units(n, side, part):
                    toks = slice(SEQ // 2 * part, SEQ // 2 * (part + 1))
                    for m in range(2):
                        ready(n + m)
                        hi, lo = (r.rearrange("p (k c) -> p k c", k=KC) for r in parts(n + m))
                        for k in range(KC):
                            mm = split_product(bank(2 * side + m)[:, toks], hi[:, k, :], lo[:, k, :], xT_hi[:, k, toks],
                                               xT_lo[:, k, toks], k == 0, k == KC - 1)
                        if part == 1:
                            mm.then_inc(unit_used, 1)

                def first_units():
                    for b in range(TB):
                        pe.wait_ge(x_in[b], 16)
                        if b == TB - 1:
                            pe.wait_ge(bias_made, 2)
                        turn_rows(2 * b, xa[:, b, :])
                        if b == 1:
                            pe.wait_ge(small_in, 48)
                            pe.transpose(bank(7)[:, 0:2 * KC + 1], bias_rows[:, :], ident[0:2 * KC + 1, 0:2 * KC + 1])\
                                .then_inc(bias_turned, 1)
                        if b % 2:
                            pe.wait_ge(xt_lo, 2 * b + 2)
                            half_units(n0, 0, b // 2)
                    pe.wait_ge(mem_in_ok, 16)
                    for b in range(MB):
                        turn_rows(T_MEM + 2 * b, mem_in[:, b, :])
                    gate_up(1, n0 + 2, chunk0 + 1)

                def first_units_2():
                    pe.wait_ge(xt_lo, T_X3 + 4)
                    half_units(n0, 0, 0)
                    pe.wait_ge(ln_done, 2 * TB + 3)
                    turn_rows(T_X3 + 4, xb[:, 2, :])
                    half_units(n0 + 2, 1, 0)
                    pe.wait_ge(tile_free, 16)
                    pe.wait_ge(ln_done, 3 * TB)
                    turn_rows(T_X3 + 6, xb[:, 3, :])
                    pe.wait_ge(xt_lo, T_X3 + 8)
                    for side in range(2):
                        half_units(n0 + 2 * side, side, 1)

                def last_down(n, pair):
                    for m in range(2):
                        ready(n + m)
                        pe.wait_ge(h_lo_done, 2 * pair + 1 + m)
                        for j in range(4):
                            if m == 0:
                                pe.wait_ge(down_free, 8 * pair + j - 3)
                            mm = down_product(n, j, m)
                            if m == 1:
                                mm.then_inc(down_full, 1)
                    for j in range(4, 8):
                        pe.wait_ge(down_free, 8 * pair + j - 3)
                        for m in range(2):
                            mm = down_product(n, j, m)
                        mm.then_inc(*((down_full, 1) if j < 7 else (unit_used, 2)))

                def down_product(n, j, m):
                    b, half = j // 2, j % 2
                    hi, lo = (r[:, half * HALF:(half + 1) * HALF] for r in parts(n + m))
                    tok = slice(b * P, (b + 1) * P)
                    return split_product(bank(4 + j % 4), h_hi[:, m, tok], h_lo[:, m, tok], hi, lo, m == 0, m == 1)

                def down(n, pair, i):
                    ready(n + 1, i * 6)
                    pe.wait_ge(h_lo_done, i * 2 + (2 * pair + 2))
                    for j in range(8):
                        was = 8 * pair + j - 3
                        if was > 0:
                            pe.wait_ge(down_free, i * 8 + was)
                        elif pair == 0:
                            pe.wait_ge(down_free, i * 8 + max(was, 0))
                        for m in range(2):
                            mm = down_product(n, j, m)
                        if j < 7:
                            mm.then_inc(down_full, 1)
                        else:
                            mm.then_inc(unit_used, 2)

                pair0, chunk0 = FF_PAIRS * f, 2 * FF_PAIRS * f
                first_units() if f == 0 else first_units_2()
                n = n0 + 4
                if f == 0:
                    pe.wait_ge(xt_lo, T_X1)
                with pe.Fori(0, FF_PAIRS - 1) as i:
                    gate_up(0, n, chunk0 + 2, i)
                    down(n + 2, pair0, i)
                    gate_up(1, n + 4, chunk0 + 3, i)
                last_down(n0 + 6 * FF_PAIRS - 2, pair0 + FF_PAIRS - 1)

            def tiles(s, n0, lhs, chunk_ready, touched):
                def product(j, k):
                    b, half = j // 2, j % 2
                    hi, lo = (r[:, half * HALF:(half + 1) * HALF] for r in parts(n0 + k))
                    a_hi, a_lo = lhs(k)
                    tok = slice(b * P, (b + 1) * P)
                    return split_product(bank(j), a_hi[:, tok], a_lo[:, tok], hi, lo, k == 0, k == KC - 1)

                def turn_block(b):
                    pe.wait_ge(ln_done, TB * (s + 1) + b + 1)
                    pe.wait_ge(tile_free, 8 * s + 2 * b + 2)
                    turn_rows((T_X2, T_X3)[s] + 2 * b, xb[:, b, :])

                for k in range(2):
                    ready(n0 + k)
                    chunk_ready(k)
                    for j in (0, 1, 5, 6, 2, 3, 4, 7):
                        if k == 0:
                            touched(j)
                        mm = product(j, k)
                    mm.then_inc(unit_used, 1)
                for j in range(6):
                    for k in range(2, KC):
                        if j == 0:
                            ready(n0 + k)
                            chunk_ready(k)
                        mm = product(j, k)
                    mm.then_inc(tile_full, 1)
                    if j == 4:
                        turn_block(0)
                for k in range(2, KC):
                    product(6, k)
                    product(7, k).then_inc(unit_used, 1)
                    if k == KC // 2:
                        turn_block(1)

            pe.wait_ge(consts, 1)
            ffn(0, U_FFN1)
            for m in range(KC):
                ready(U_MK + m)
                if m >= 2:
                    proj_is_out(pe, O_MK + m - 2)
                elif m == 0:
                    pe.wait_ge(h_full, 2 * FF_PAIRS)
                project(U_MK + m, bank((O_MK + m) % 2)[:, 0:MEM], (memT_hi, memT_lo), MEM)
                if m in AFTER_MK:
                    b = AFTER_MK.index(m)
                    pe.wait_ge(ln_done, b + 1)
                    turn_rows(T_X1 + 2 * b, xa[:, b, :])
            pe.wait_ge(xt_lo, T_MEM2)

            def project_out(n, o):
                ready(n)
                if o >= 2:
                    proj_is_out(pe, o - 2)
                project(n, bank(o % 2))

            def branch(n, o, b_hi, b_lo):
                ready(n)
                hi, lo = (r.rearrange("p (k c) -> p k c", k=4) for r in parts(n))
                for e in range(2):
                    proj_is_out(pe, o + e - 2)
                    cols = slice(e * P, (e + 1) * P)
                    for k in range(4):
                        mm = split_product(bank((o + e) % 2), hi[:, k, cols], lo[:, k, cols], b_hi[:, k, :], b_lo[:, k, :],
                                           k == 0, k == 3)
                    mm.then_inc(*((branch_full, 1) if e == 0 else (unit_used, 1)))

            def t_bank(n):
                if n >= 2:
                    t_is_out(pe, n - 2)
                return bank(5 + n % 2)

            def scores(H):
                if H >= 1:
                    pe.wait_ge(exp_done, H)
                pe.wait_ge(stack_lo, H + 1)
                own, _ = rows_of(H)

                def logits(dst, tok, keys, hh, low, stop):
                    pe.matmul(dst, q_st[:, H % 2, tok], hh[:, keys], start=False, stop=False)
                    return pe.matmul(dst, q_st[own, H % 2, tok], low[own, keys], start=False, stop=stop)

                if H < SWA_HEADS:
                    if H == 0:
                        pe.wait_ge(ks_split, 1)
                    for q in range(TB):
                        at = sc[:, WINDOW * q:WINDOW * (q + 1)]
                        pe.matmul(at, ident_b[:, :], (mask_s if q else mask_0)[:, :], start=True, stop=False)
                        k0 = P * max(q - 1, 0)
                        mm = logits(at[:, WINDOW - (P * (q + 1) - k0):], slice(q * P, (q + 1) * P), slice(k0, P * (q + 1)),
                                    ks_hh[:, H // 4, :], ks_ll[:, H // 4, :], True)
                else:
                    h = H - SWA_HEADS
                    pe.wait_ge(cq_made, h + 1)
                    for q in (3, 2, 0, 1):
                        c0, w = FOX_AT[q]
                        tok = slice(q * P, (q + 1) * P)
                        pe.matmul(sc[:, c0:c0 + w], c_qh[:, h % 2, tok], c_k[:, 0:w], start=True, stop=False)
                        logits(sc[:, c0:c0 + w], tok, slice(0, w), k_hh[:, h % 2, :], k_low[:, h % 2, :], False)
                        mm = pe.matmul(sc[:, c0 + w - P:c0 + w], ident_b[:, :], mask_c[:, :], start=False, stop=True)
                mm.then_inc(s_full, 1)

            def transposed_probs(H):
                pe.wait_ge(p_done, H + 1)
                for b, (n, blocks) in enumerate(zip(head_uses(H), swa_transposes() if H < SWA_HEADS else fox_transposes())):
                    dst = t_bank(n)
                    for q, k, col in blocks:
                        src = p_at(H, q, k)
                        mm = pe.transpose(dst[:, col - HALF * b:col - HALF * b + P], prob[:, src:src + P], ident[:, :])
                    mm.then_inc(t_full, 1)

            def values(H):
                for n in head_uses(H):
                    t_is_out(pe, n)
                if H % 2 == 0 and H >= 2:
                    pe.wait_ge(o_lo, H // 2)
                dst = ps[7][HD * (H % 2):HD * (H % 2 + 1), :]
                for k in range(TB):
                    if H < SWA_HEADS:
                        v = vs[:, k, HD * (H // 4):HD * (H // 4 + 1)]
                        end, src = min(SEQ, P * k + WINDOW), SWA_T[k]
                    else:
                        h = H - SWA_HEADS
                        v = vf[:, k, HD * h:HD * (h + 1)]
                        end, src = SEQ, FOX_T[k]
                    mm = pe.matmul(dst[:, P * k:end], v, probT[:, src:src + end - P * k], start=k == 0, stop=k == TB - 1,
                                   skip_group_check=True)
                mm.then_inc(o_full, 1)

            def swapped(n, src, o):
                proj_is_out(pe, o)
                pe.matmul(t_bank(n), swap[:, :], src, start=True, stop=True).then_inc(t_full, 1)

            project_out(U_F, O_F)
            project_out(U_KS, O_KS)
            pe.wait_ge(f_dve, 2)
            turn(fe, t_bank(T_F), 0).then_inc(t_full, 1)
            project_out(U_VS, O_VS)
            swapped(T_KS, kraw[:, :], O_KS)
            t_is_out(pe, T_F)
            pe.wait_ge(zeroed, 1)
            dst = t_bank(T_C)
            for k in range(TB):
                mm = pe.matmul(dst[:, k * P:], lsn[:, k, :], tri_f[:, 0:SEQ - k * P], start=k == 0, stop=k == TB - 1)
            mm.then_inc(t_full, 1)
            project_out(U_QS, O_QS)
            proj_is_out(pe, O_VS)
            turn(gate[:, 0, :], t_bank(T_VS), 0).then_inc(t_full, 1)
            for m in range(1, 4):
                project_out(U_QS + m, O_QS + m)
                swapped(T_QS + m - 1, qs[:, m - 1, :], O_QS + m - 1)
            pe.wait_ge(consts, 2)
            for H in range(HEADS):
                for u in fill(H % 8):
                    if H < SWA_HEADS:
                        project_out(U_QF + u, O_QF + u)
                    elif u % 3 < 2:
                        project_out(U_G0 + u, O_G0 + 4 * (u // 3) + u % 3)
                    else:
                        pe.wait_ge(o_lo, SWA_HEADS // 2)
                        branch(U_G0 + u, O_G0 + 4 * (u // 3) + 2, os_hi, os_lo)
                if H == 0:
                    swapped(T_QS + 3, qs[:, 3, :], O_QS + 3)
                if H >= 1:
                    transposed_probs(H - 1)
                if H < SWA_HEADS:
                    for u in fill(H):
                        if u >= 8:
                            proj_is_out(pe, O_VF + u - 8)
                            turn(gate[:, (u - 7) % 2, :], t_bank(T_VF[u - 8]), 0).then_inc(t_full, 1)
                if H == SWA_HEADS:
                    for o in range(O_QF, O_VF):
                        proj_is_out(pe, o)
                    pe.wait_ge(c_made, 4)
                scores(H)
                if H >= 1:
                    values(H - 1)
            for u in range(12):
                o = O_G1 + 4 * (u // 3) + u % 3
                if u % 3 < 2:
                    project_out(U_G1 + u, o)
                else:
                    pe.wait_ge(o_lo, HEADS // 2)
                    branch(U_G1 + u, o, of_hi, of_lo)
                if u == 0:
                    transposed_probs(HEADS - 1)
                    values(HEADS - 1)
                elif u == 9:
                    pe.wait_ge(mem_in_ok, 32)
                    pe.wait_ge(exp_done, HEADS)
                    pe.wait_ge(o_lo, HEADS // 2)
                    for b in range(MB):
                        turn_rows(T_MEM2 + 2 * b, mem_in[:, b, :])

            def merged_chunk(k):
                hi, lo = (m0_hi, m0_lo) if k < 4 else (m1_hi, m1_lo)
                return hi[:, k % 4, :], lo[:, k % 4, :]

            def mixer_touched(j):
                if j < 2:
                    proj_is_out(pe, O_MQ - 2 + (O_MQ + j) % 2)
                elif j < 5:
                    pe.wait_ge(xt_lo, T_MEM2 + j - 1)
                elif j < 7:
                    t_is_out(pe, T_END - 2 + (T_END + j - 5) % 2)
                else:
                    pe.wait_ge(xt_lo, T_X2)

            tiles(0, U_OUT, merged_chunk, lambda k: pe.wait_ge(merged_lo, k + 1), mixer_touched)

            def mem_value_tiles(k, b):
                for half in range(2):
                    if k == 0:
                        pe.wait_ge(tile_free, 5 + 2 * b + half)
                    hi, lo = (r[:, half * HALF:(half + 1) * HALF] for r in parts(U_MV + k))
                    mm = split_product(bank(4 + 2 * b + half), memT_hi[:, k, b * P:(b + 1) * P],
                                       memT_lo[:, k, b * P:(b + 1) * P], hi, lo, k == 0, k == KC - 1)
                return mm

            for pair in range(KC // 2):
                for k in (2 * pair, 2 * pair + 1):
                    ready(U_MV + k)
                    mem_value_tiles(k, 0)
                for k in (2 * pair, 2 * pair + 1):
                    mem_value_tiles(k, 1).then_inc(unit_used, 1)
                if pair < 2:
                    b = 2 + pair
                    pe.wait_ge(ln_done, TB + b + 1)
                    turn_rows(T_X2 + 2 * b, xb[:, b, :])
            pe.wait_ge(xt_lo, T_X3)

            def mem_scores(h):
                for m in range(2):
                    proj_is_out(pe, O_MQ + 2 * h + m)
                pe.wait_ge(exp_done, HEADS + h)
                for b in range(TB):
                    for m in range(2):
                        mm = pe.matmul(sc[:, b * MEM:(b + 1) * MEM], qm[:, 2 * h + m, b * P:(b + 1) * P], km[:, 2 * h + m, :],
                                       start=m == 0, stop=m == 1)
                mm.then_inc(s_full, 1)

            def mem_transposed_probs(h):
                pe.wait_ge(p_done, HEADS + h + 1)
                for m in range(MB):
                    if h >= 1:
                        pe.wait_ge(mt_free[m], h)
                    elif m == 0:
                        pe.wait_ge(vm_done, 4)
                    for b in range(TB):
                        mm = pe.transpose(bank(4 + m)[:, b * P:(b + 1) * P], prob[:, MEM * b + P * m:MEM * b + P * (m + 1)],
                                          ident[:, :])
                    mm.then_inc(mt_full, 1)

            def mem_values(h):
                for m in range(MB):
                    pe.wait_ge(mt_free[m], h + 1)
                for e in range(2):
                    if h >= 1:
                        pe.wait_ge(om_lo_done, 2 * h + e - 1)
                    for m in range(MB):
                        c0 = 2 * P * h + P * e
                        mm = pe.matmul(bank(6 + e), vm[:, m, c0:c0 + P], probT[:, HALF * m:HALF * (m + 1)],
                                       start=m == 0, stop=m == MB - 1)
                    mm.then_inc(om_full, 1)

            for h in range(MEM_HEADS + 1):
                if h < MEM_HEADS:
                    for m in range(2):
                        project_out(U_MQ + 2 * h + m, O_MQ + 2 * h + m)
                if h >= 1:
                    mem_transposed_probs(h - 1)
                if h < MEM_HEADS:
                    mem_scores(h)
                if h >= 1:
                    mem_values(h - 1)

            def memory_touched(j):
                if j < 2:
                    proj_is_out(pe, O_END - 2 + (O_END + j) % 2)
                elif j < 4:
                    pe.wait_ge(exp_done, HEADS + MEM_HEADS)
                elif j < 6:
                    pe.wait_ge(mt_free[j - 4], MEM_HEADS)
                else:
                    pe.wait_ge(om_lo_done, j + 1)

            tiles(1, U_MO, lambda k: (om_hi[:, k, :], om_lo[:, k, :]), lambda k: pe.wait_ge(om_lo_done, k + 1), memory_touched)
            pe.wait_ge(tile_free, 14)
            ffn(1, U_FFN2)

        @block.scalar
        def _(act):
            copy = ACT.Copy

            def prep(n, i=None):
                if i is None:
                    act.wait_ge(landed[n % RAW], 16 * (n // RAW + 1))
                    if n >= RING:
                        act.wait_ge(unit_used, n - RING + 1)
                else:
                    act.wait_ge(landed[n % RAW], i * 32 + 16 * (n // RAW + 1))
                    act.wait_ge(unit_used, i * 6 + max(n - RING + 1, 0))
                src, dst = raw[:, n % RAW, :], ring_hi[:, n % RING, :]
                if n == U_F:
                    src, dst = forget_views(n, ring_hi)
                nc.scalar.activation(dst, src, copy).then_inc(unit_hi, 1)

            def high(dst, src, done):
                nc.scalar.activation(dst, src, copy).then_inc(done, 1)

            def turned_high(n, dst, b):
                act.wait_ge(xt_full, n + 1)
                e = n % 2
                high(dst[:, 4 * e:4 * e + 4, b * P:(b + 1) * P], turned(xt_bank(n)), xt_hi)

            def standardize(n, x, b):
                act.wait_ge(shift_done, n * TB + b + 1)
                for cols in halves(n, b):
                    nc.scalar.activation(x[:, b, cols], x[:, b, cols], ACT.Identity, scale=rstd[:, b:b + 1],
                                         bias=shift[:, b:b + 1]).then_inc(standard, 1)

            def turned_pair(n, b):
                for e in range(2):
                    turned_high(n + 2 * b + e, xT_hi, b)

            def layer_norm(n, t0, u):
                standardize(n, xb, 0)
                turned_pair(t0, 0)
                standardize(n, xb, 1)
                prep(u)
                turned_pair(t0, 1)
                standardize(n, xb, 2)
                for k in (1, 2, 3):
                    prep(u + k)
                standardize(n, xb, 3)
                turned_pair(t0, 2)

            def ffn(f, n0):
                chunk0 = 2 * FF_PAIRS * f

                def sigmoid(side, n, chunk, i=None):
                    if i is None:
                        act.wait_ge(unit_used, n + 1)
                        if chunk >= 2:
                            act.wait_ge(gated, chunk - 1)
                    else:
                        act.wait_ge(unit_used, i * 6 + (n + 1))
                        act.wait_ge(gated, i * 2 + (chunk - 1))
                    nc.scalar.activation(sig[:, side, :], bank(2 * side), ACT.Sigmoid).then_inc(sig_done, 1)

                def hidden_high(side, chunk, used, i=None):
                    act.wait_ge(h_full, chunk + 1 if i is None else i * 2 + (chunk + 1))
                    act.wait_ge(unit_used, used if i is None else i * 6 + used)
                    high(h_hi[:, side, :], hf[:, side, :], h_hi_done)

                if f == 0:
                    prep(n0 + 3)
                    sigmoid(0, n0, chunk0)
                    for n in range(T_MEM, T_X1):
                        turned_high(n, memT_hi, (n - T_MEM) // 2)
                else:
                    sigmoid(0, n0, chunk0)
                for k in range(4, 6):
                    prep(n0 + k)
                hidden_high(0, chunk0, n0 + 1)
                sigmoid(1, n0 + 2, chunk0 + 1)
                n = n0 + 4
                with act.Fori(0, FF_PAIRS - 1) as i:
                    prep(n + 2, i)
                    prep(n + 3, i)
                    prep(n + 4, i)
                    hidden_high(1, chunk0 + 1, n - 2, i)
                    prep(n + 5, i)
                    sigmoid(0, n, chunk0 + 2, i)
                    prep(n + 6, i)
                    prep(n + 7, i)
                    hidden_high(0, chunk0 + 2, n + 4, i)
                    sigmoid(1, n + 4, chunk0 + 3, i)
                if f == 0:
                    for k in range(3):
                        prep(U_MK + k)
                hidden_high(1, chunk0 + 2 * FF_PAIRS - 1, n0 + 6 * FF_PAIRS - 6 + 2)

            act.dma_start(bias_rows[0:2 * KC, :], t["mix_b_gate"].rearrange("g (m p) -> (g m) p", p=P)).then_inc(small_in, 16)
            act.dma_start(bias_rows[2 * KC:2 * KC + 1, :].rearrange("a (r h) -> a r h", h=FOX_HEADS),
                          t["mix_b_forget"].unsqueeze(1).to_broadcast([1, FOX_COPIES, FOX_HEADS])).then_inc(small_in, 16)
            act.dma_start(sinks[:, :], t["swa_sinks"].to_broadcast([P, SWA_HEADS])).then_inc(small_in, 16)
            for n in range(8):
                turned_high(n, xT_hi, n // 2)
                if n in (3, 7):
                    for u in (0, 1) if n == 3 else (2,):
                        prep(u)
            ffn(0, U_FFN1)
            prep(U_MK + 3)
            standardize(0, xa, 0)
            for m in range(KC):
                act.wait_ge(unit_used, U_MK + m + 1)
                nc.scalar.activation(km[:, m, :], bank((O_MK + m) % 2)[:, 0:MEM], copy).then_inc(proj_free[(O_MK + m) % 2], 1)
                if m in AFTER_MK:
                    turned_pair(T_X1, AFTER_MK.index(m))
                if m < TB - 1:
                    standardize(0, xa, m + 1)
                if m < 2:
                    prep(U_MK + m + 4)
                elif m >= 3:
                    for n in (6, 7) if m == 3 else (m + 4,):
                        prep(U_MK + n)

            def output(n, o):
                act.wait_ge(unit_used, n + 1)
                return bank(o % 2)

            prep(U_F + 4)
            act.wait_ge(bias_made, 2)
            nc.scalar.activation(fz[:, :], output(U_F, O_F), ACT.Identity, bias=b_f[:, 0:1]).then_inc(proj_free[O_F % 2], 1)
            act.wait_ge(f_dve, 1)
            nc.scalar.activation(fa[:, :], fe[:, :], ACT.Exp, scale=-1.0).then_inc(f_act, 1)
            act.wait_ge(f_act, 1)
            nc.scalar.activation(fb[:, :], fa[:, :], ACT.Ln, bias=1.0).then_inc(f_act, 1)
            prep(U_KS + 4)
            nc.scalar.activation(kraw[:, :], output(U_KS, O_KS), copy).then_inc(proj_free[O_KS % 2], 1)
            prep(U_VS + 4)
            nc.scalar.activation(gate[:, 0, :], output(U_VS, O_VS), copy).then_inc(proj_free[O_VS % 2], 1)
            act.wait_ge(spilled, 16 * TB)
            act.wait_ge(rope_done, 1)
            for kv in range(SWA_KV):
                for e in range(2):
                    ins = nc.scalar.activation(ks_hh[HD * e:HD * (e + 1), kv, :], kraw[HD * kv:HD * (kv + 1), :], copy)
            ins.then_inc(ks_made, 1)
            for m in range(4):
                prep(U_QS + m + 4)
                nc.scalar.activation(qs[:, m, :], output(U_QS + m, O_QS + m), copy, scale=QK_SCALE)\
                    .then_inc(proj_free[(O_QS + m) % 2], 1)

            def copied_probs(H):
                for e, n in enumerate(head_uses(H)):
                    if e != 1:
                        act.wait_ge(t_full, n + 1)
                        w = HALF if e == 0 else 2 * P
                        nc.scalar.activation(probT[:, HALF * e:HALF * e + w], bank(5 + n % 2)[:, 0:w], copy)\
                            .then_inc(t_free[n % 2], 1)

            def exponentials(H, at, sink=None):
                act.wait_ge(ntop_done, H + 1)
                if sink is not None:
                    nc.scalar.activation(esink[:, :], ntop[:, :], ACT.Exp, bias=sinks[:, sink:sink + 1])
                for q, (c0, w) in sorted(at.items()):
                    ins = nc.scalar.activation(prob[:, c0:c0 + w], sc[:, c0:c0 + w], ACT.Exp, bias=ntop[:, q:q + 1],
                                               accum_out=rsum[:, q:q + 1])
                ins.then_inc(exp_done, 1)

            def pair_high(H):
                act.wait_ge(o_full, H + 1)
                m = H // 2
                high((os_hi if m < 4 else of_hi)[:, m % 4, :], bank(7), o_hi)

            def gate_tanh(n, o, g, m):
                nc.scalar.activation(gate[:, m % 2, :], output(n, o), ACT.Tanh, bias=b_gate[:, g, m:m + 1], scale=0.5)\
                    .then_inc(proj_free[o % 2], 1)

            def stack_high(H):
                own, other = rows_of(H)
                q, k = query_key(H)
                if H < SWA_HEADS:
                    act.wait_ge(rope_done, H // 2 + 2)
                elif H == SWA_HEADS:
                    for o in range(O_QF, O_VF):
                        proj_is_out(act, o)
                if H >= 2:
                    act.wait_ge(s_full, H - 1)
                ins = nc.scalar.activation(q_st[own, H % 2, :], q[own, :], copy)
                if k is not None:
                    nc.scalar.activation(k_hh[own, H % 2, :], k[own, :], copy)
                    ins = nc.scalar.activation(k_hh[other, H % 2, :], k[own, :], copy)
                ins.then_inc(stack_hi, 1)

            stack_high(0)
            at_swa = {q: (WINDOW * q, WINDOW) for q in range(TB)}
            act.wait_ge(small_in, 48)
            for H in range(HEADS):
                for u in fill(H % 8):
                    if H < SWA_HEADS:
                        n, o = U_QF + u, O_QF + u
                        prep(n + 4)
                        if u == 2:
                            act.wait_ge(rope_done, 5)
                        if u < 4:
                            nc.scalar.activation(qf[:, u, :], output(n, o), copy, scale=QK_SCALE).then_inc(proj_free[o % 2], 1)
                        elif u >= 8:
                            v = u - 8
                            act.wait_ge(t_full, (T_VF[v - 2] if v >= 2 else T_VS) + 1)
                            nc.scalar.activation(gate[:, (v + 1) % 2, :], output(n, o), copy).then_inc(proj_free[o % 2], 1)
                    else:
                        n = U_G0 + u
                        prep(n + 4)
                        if u % 3 < 2:
                            o, m = O_G0 + 4 * (u // 3) + u % 3, 2 * (u // 3) + u % 3
                            if m >= 2:
                                proj_is_out(act, o - 2)
                            else:
                                act.wait_ge(t_full, T_VF[3] + 1)
                            gate_tanh(n, o, 0, m)
                if H >= 1:
                    copied_probs(H - 1)
                exponentials(H, at_swa if H < SWA_HEADS else FOX_AT, H if H < SWA_HEADS else None)
                if H >= 2 and H % 2 == 0:
                    pair_high(H - 1)
                if H + 1 < HEADS:
                    stack_high(H + 1)

            def merged_high(m):
                act.wait_ge(merged, m + 1)
                if m >= 4:
                    act.wait_ge(unit_used, U_G1 + 11)
                hi = (m0_hi if m < 4 else m1_hi)[:, m % 4, :]
                nc.scalar.activation(hi, part[:, m, :], copy, scale=0.5).then_inc(merged_hi, 1)

            for u in range(12):
                n = U_G1 + u
                prep(n + 4)
                if u % 3 < 2:
                    o, m = O_G1 + 4 * (u // 3) + u % 3, 2 * (u // 3) + u % 3
                    if m >= 2:
                        act.wait_ge(merged, m - 1)
                    else:
                        proj_is_out(act, O_G1 - 2 + m)
                    gate_tanh(n, o, 1, m)
                if u == 0:
                    copied_probs(HEADS - 1)
                    pair_high(HEADS - 1)
                if u in (3, 6):
                    for m in (0, 1) if u == 3 else (2, 3):
                        merged_high(m)
            act.wait_ge(unit_used, U_G1 + 12)
            for n in range(T_MEM2, T_X2):
                turned_high(n, memT_hi, (n - T_MEM2) // 2)
            for m in range(4, KC):
                merged_high(m)
            for m in range(4, KC):
                prep(U_OUT + m)
            layer_norm(1, T_X2, U_MV)
            prep(U_MV + 4)
            prep(U_MV + 5)
            prep(U_MV + 6)
            turned_pair(T_X2, 3)
            prep(U_MV + 7)
            for k in range(4):
                prep(U_MQ + k)
            act.wait_ge(unit_used, U_MV + KC)
            for b in range(MB):
                for half in range(2):
                    nc.scalar.activation(vm[:, b, half * HALF:(half + 1) * HALF], bank(4 + 2 * b + half), copy).then_inc(vm_done, 1)
            for h in range(MEM_HEADS + 1):
                if h < MEM_HEADS:
                    for m in range(2):
                        n, o = U_MQ + 2 * h + m, O_MQ + 2 * h + m
                        prep(n + 4)
                        nc.scalar.activation(qm[:, 2 * h + m, :], output(n, o), copy, scale=MEM_SCALE).then_inc(proj_free[o % 2], 1)
                if h >= 1:
                    act.wait_ge(mt_full, 2 * h - 1)
                    nc.scalar.activation(probT[:, 0:HALF], bank(4), copy).then_inc(mt_free[0], 1)
                if h < MEM_HEADS:
                    exponentials(HEADS + h, at_swa)
                if h >= 1:
                    for e in range(2):
                        m = 2 * (h - 1) + e
                        act.wait_ge(om_full, m + 1)
                        high(om_hi[:, m, :], bank(6 + e), om_hi_done)
            for m in range(4, KC):
                prep(U_MO + m)
            layer_norm(2, T_X3, U_FFN2)
            turned_pair(T_X3, 3)
            ffn(1, U_FFN2)
            for b in range(TB):
                standardize(3, xb, b)

        @block.vector
        def _(dve):
            def low(dst, src, hi, done):
                nc.vector.tensor_tensor(dst, src, hi.bitcast(F32), ALU.subtract).then_inc(done, 1)

            def split(n, i=None):
                dve.wait_ge(unit_hi, n + 1 if i is None else i * 6 + (n + 1))
                src, dst, hi = raw[:, n % RAW, :], ring_lo[:, n % RING, :], ring_hi[:, n % RING, :]
                if n == U_F:
                    src, dst = forget_views(n, ring_lo)
                    hi = forget_views(n, ring_hi)[1]
                low(dst, src, hi, unit_lo)

            def turned_low(n, hi, lo, b):
                dve.wait_ge(xt_hi, n + 1)
                e = n % 2
                at = (slice(None), slice(4 * e, 4 * e + 4), slice(b * P, (b + 1) * P))
                low(lo[at], turned(xt_bank(n)), hi[at], xt_lo)

            def scale_residual(x, blocks, turned_uses=None):
                for b in blocks:
                    if turned_uses is not None:
                        dve.wait_ge(xt_full, turned_uses + 2 * b + 2)
                    nc.vector.tensor_scalar(x[:, b, :], x[:, b, :], ALPHA, None, ALU.mult).then_inc(scaled, 1)

            def add_tile(x, j, src, done):
                at = (slice(None), j // 2, slice(HALF * (j % 2), HALF * (j % 2 + 1)))
                nc.vector.tensor_tensor(x[at], x[at], src, ALU.add).then_inc(done, 1)

            def block_stats(n, x, b, done, count):
                dve.wait_ge(done, count)
                for e in range(2):
                    nc.vector.bn_stats(stats[:, b, e, :], x[:, b, HALF * e:HALF * (e + 1)]).then_inc(stats_done, 1)
                dve.wait_ge(stats_done, 2 * (n * TB + b) + 2)
                nc.vector.bn_aggr(mv[:, b, :], stats[:, b, :, :]).then_inc(mean_done, 1)

            def gain(n, x, b, between=None):
                if b == 0:
                    dve.wait_ge(gains_in, 32 * (n + 1))
                for e, cols in enumerate(halves(n, b)):
                    count = n * TB + b + 1 + e
                    dve.wait_ge(standard, count)
                    nc.vector.tensor_tensor(x[:, b, cols], x[:, b, cols], ln_g[:, cols], ALU.mult).then_inc(gained, 1)
                    if between is not None:
                        split(between)
                    if b == TB - 1:
                        dve.wait_ge(gained, count)
                        if n < 3:
                            dve.wait_ge(ln_done, count - 1)
                        nc.vector.tensor_tensor(x[:, b, cols], x[:, b, cols], ln_b[:, cols], ALU.add)\
                            .then_inc(ln_done if n < 3 else last_done, 1)

            def ffn(f, n0, x):
                chunk0, pair0 = 2 * FF_PAIRS * f, FF_PAIRS * f

                def hidden(side, n, chunk, i=None):
                    dve.wait_ge(sig_done, chunk + 1 if i is None else i * 2 + (chunk + 1))
                    nc.vector.tensor_tensor(hf[:, side, :], sig[:, side, :], bank(2 * side), ALU.mult).then_inc(gated, 1)
                    dve.wait_ge(unit_used, n + 1 if i is None else i * 6 + (n + 1))
                    dve.wait_ge(gated, chunk + 1 if i is None else i * 2 + (chunk + 1))
                    nc.vector.scalar_tensor_tensor(out=hf[:, side, :], in0=hf[:, side, :], scalar=0.5, in1=bank(2 * side + 1),
                                                   op0=ALU.mult, op1=ALU.mult).then_inc(h_full, 1)

                def hidden_low(side, chunk, i=None):
                    dve.wait_ge(h_hi_done, chunk + 1 if i is None else i * 2 + (chunk + 1))
                    low(h_lo[:, side, :], hf[:, side, :], h_hi[:, side, :], h_lo_done)

                def add_down(js, n, pair, i=None):
                    for j in js:
                        if j < 7:
                            full = 7 * pair + j + 1
                            dve.wait_ge(down_full, full if i is None else i * 7 + full)
                        else:
                            dve.wait_ge(unit_used, n + 1 if i is None else i * 6 + (n + 1))
                        was = 8 * pair + j - 7
                        if i is None:
                            dve.wait_ge(down_free, was)
                        elif was > 0:
                            dve.wait_ge(down_free, i * 8 + was)
                        else:
                            dve.wait_ge(down_free, i * 8 + max(was, 0))
                        add_tile(x, j, bank(4 + j % 4), down_free)

                if f == 0:
                    split(n0 + 3)
                    scale_residual(xa, range(TB), 0)
                hidden(0, n0 + 1, chunk0)
                if f == 0:
                    for n in range(T_MEM, T_X1):
                        turned_low(n, memT_hi, memT_lo, (n - T_MEM) // 2)
                split(n0 + 4)
                split(n0 + 5)
                hidden_low(0, chunk0)
                dve.wait_ge(scaled, TB * (1 + 3 * f))
                n = n0 + 4
                with dve.Fori(0, FF_PAIRS - 1) as i:
                    hidden(1, n - 1, chunk0 + 1, i)
                    split(n + 2, i)
                    split(n + 3, i)
                    split(n + 4, i)
                    hidden_low(1, chunk0 + 1, i)
                    split(n + 5, i)
                    split(n + 6, i)
                    hidden(0, n + 1, chunk0 + 2, i)
                    add_down((0, 1), n + 3, pair0, i)
                    split(n + 7, i)
                    add_down(range(2, 8), n + 3, pair0, i)
                    hidden_low(0, chunk0 + 2, i)
                last = n0 + 6 * FF_PAIRS - 1
                if f == 0:
                    for k in range(3):
                        split(U_MK + k)
                hidden(1, last - 2, chunk0 + 2 * FF_PAIRS - 1)
                hidden_low(1, chunk0 + 2 * FF_PAIRS - 1)
                for b in range(TB):
                    add_down((2 * b, 2 * b + 1), last, pair0 + FF_PAIRS - 1)
                    block_stats(3 * f, x, b, down_free, 8 * (pair0 + FF_PAIRS - 1) + 2 * b + 2)
                    if b == 2 and f == 0:
                        split(U_MK + 3)
                    if b == TB - 1 and f == 0:
                        turned_pair(T_X1, 0)
                    if b >= 1:
                        gain(3 * f, x, b - 1)
                gain(3 * f, x, TB - 1, U_MK + 4 if f == 0 else None)

            def turned_pair(n, b):
                for e in range(2):
                    turned_low(n + 2 * b + e, xT_hi, xT_lo, b)

            for n in range(8):
                turned_low(n, xT_hi, xT_lo, n // 2)
                if n == 3:
                    split(0)
                    split(1)
                    dve.wait_ge(bias_turned, 1)
                    nc.vector.tensor_scalar(b_gate[:, :, :].rearrange("p g m -> p (g m)"), bank(7)[:, 0:2 * KC], 0.5, None,
                                            ALU.mult).then_inc(bias_made, 1)
                    nc.vector.tensor_copy(b_f[:, :], bank(7)[:, 2 * KC:2 * KC + 1]).then_inc(bias_made, 1)
            split(2)
            dve.wait_ge(consts, 2)
            nc.vector.tensor_reduce(pick_part[:, 0:6], pick[:, :, :], AX.X, ALU.add).then_inc(dve_consts, 1)
            dve.wait_ge(dve_consts, 1)
            nc.vector.tensor_reduce(pick_part[:, 6:8], pick_part[:, 0:6].rearrange("p (a b) -> p a b", a=2), AX.X, ALU.add)\
                .then_inc(dve_consts, 1)
            nc.vector.tensor_reduce(pick_head[:, :], pick[:, :, :].rearrange("p k h -> p h k"), AX.X, ALU.add)\
                .then_inc(dve_consts, 1)
            dve.wait_ge(dve_consts, 2)
            nc.vector.tensor_scalar(pick_part[:, 0:3], pick_part[:, 0:3], -1.0, None, ALU.mult).then_inc(dve_consts, 1)
            ffn(0, U_FFN1, xa)
            for m in range(1, KC):
                split(U_MK + m + 4)
                if m < TB:
                    turned_pair(T_X1, m)

            ropes = [0]

            def rotate(x, n):
                if ropes[0]:
                    dve.wait_ge(rope_done, ropes[0])
                ropes[0] += 1
                dve.wait_ge(t_full, n + 1)
                nc.vector.tensor_tensor(rot[:, :], bank(5 + n % 2), sin_t[:, :], ALU.mult).then_inc(t_free[n % 2], 1)
                nc.vector.tensor_tensor(x, x, cos_t[:, :], ALU.mult).then_inc(rope_cos, 1)
                t_is_out(dve, n)
                dve.wait_ge(rope_cos, ropes[0])
                nc.vector.tensor_tensor(x, x, rot[:, :], ALU.add).then_inc(rope_done, 1)

            split(U_F + 4)
            proj_is_out(dve, O_F)
            nc.vector.scalar_tensor_tensor(out=fe[:, :], in0=fz[:, :], scalar=-1.0, in1=fz[:, :], op0=ALU.mult,
                                           op1=ALU.max).then_inc(f_dve, 1)
            dve.wait_ge(f_act, 2)
            nc.vector.scalar_tensor_tensor(out=fe[:, :], in0=fz[:, :], scalar=0.0, in1=fb[:, :], op0=ALU.min,
                                           op1=ALU.subtract).then_inc(f_dve, 1)
            split(U_KS + 4)
            dve.wait_ge(t_full, T_F + 1)
            nc.vector.tensor_copy(lsn[:, :, :].rearrange("p k c -> p (k c)"), bank(5 + T_F % 2)).then_inc(t_free[T_F % 2], 1)
            split(U_VS + 4)
            dve.wait_ge(angles_in, 32)
            rotate(kraw[:, :], T_KS)
            dve.wait_ge(t_full, T_C + 1)
            c = bank(5 + T_C % 2)
            nc.vector.tensor_copy(c_hi[:, :], c).then_inc(f_dve, 1)
            dve.wait_ge(f_dve, 3)
            nc.vector.tensor_tensor(fz[:, :], c, c_hi[:, :], ALU.subtract).then_inc(t_free[T_C % 2], 1)
            t_is_out(dve, T_C)
            nc.vector.tensor_copy(c_mid[:, :], fz[:, :]).then_inc(f_dve, 1)
            dve.wait_ge(f_dve, 4)
            nc.vector.tensor_tensor(fe[:, :], fz[:, :], c_mid[:, :], ALU.subtract).then_inc(f_dve, 1)
            dve.wait_ge(f_dve, 5)
            nc.vector.tensor_copy(c_lo[:, :], fe[:, :]).then_inc(f_dve, 1)
            dve.wait_ge(f_dve, 6)
            dve.wait_ge(dve_consts, 4)
            for side, (first, acc, dst) in enumerate(((3, fa, c_q), (0, fb, c_k))):
                nc.vector.tensor_scalar(acc[:, :], c_hi[:, :], pick_part[:, first:first + 1], pick_part[:, 6 + side:7 + side],
                                        ALU.mult, ALU.add).then_inc(f_dve, 1)
                dve.wait_ge(f_dve, 7 + side)
                nc.vector.scalar_tensor_tensor(out=acc[:, :], in0=c_mid[:, :], scalar=pick_part[:, first + 1:first + 2],
                                               in1=acc[:, :], op0=ALU.mult, op1=ALU.add).then_inc(c_made, 1)
                dve.wait_ge(c_made, 1 + 2 * side)
                nc.vector.scalar_tensor_tensor(out=dst[:, :], in0=c_lo[:, :], scalar=pick_part[:, first + 2:first + 3],
                                               in1=acc[:, :], op0=ALU.mult, op1=ALU.add).then_inc(c_made, 1)
            split(U_QS + 4)
            dve.wait_ge(t_full, T_VS + 1)
            nc.vector.tensor_copy(vs[:, :, :].rearrange("p k c -> p (k c)"), bank(5 + T_VS % 2)).then_inc(t_free[T_VS % 2], 1)
            for m in range(1, 4):
                split(U_QS + m + 4)
                rotate(qs[:, m - 1, :], T_QS + m - 1)

            def copied_probs(H):
                n = head_uses(H)[1]
                dve.wait_ge(t_full, n + 1)
                w = 3 * P if H < SWA_HEADS else HALF
                nc.vector.tensor_copy(probT[:, HALF:HALF + w], bank(5 + n % 2)[:, 0:w]).then_inc(t_free[n % 2], 1)

            def maxima(H, at, sink=None):
                if H == 0:
                    dve.wait_ge(small_in, 48)
                dve.wait_ge(s_full, H + 1)
                if len({w for _, w in at.values()}) == 1:
                    nc.vector.tensor_reduce(top[:, :], sc[:, 0:TB * WINDOW].rearrange("p (q k) -> p q k", q=TB), AX.X, ALU.max)\
                        .then_inc(top_done, 1)
                else:
                    for q, (c0, w) in at.items():
                        ins = nc.vector.tensor_reduce(top[:, q:q + 1], sc[:, c0:c0 + w], AX.X, ALU.max)
                    ins.then_inc(top_done, 1)
                dve.wait_ge(top_done, H + 1)
                if sink is None:
                    nc.vector.tensor_scalar(ntop[:, :], top[:, :], -1.0, None, ALU.mult).then_inc(ntop_done, 1)
                else:
                    nc.vector.tensor_scalar(ntop[:, :], top[:, :], sinks[:, sink:sink + 1], -1.0, ALU.max, ALU.mult)\
                        .then_inc(ntop_done, 1)

            def normalize_probs(H, at, sink=None):
                dve.wait_ge(exp_done, H + 1)
                if sink is not None:
                    nc.vector.tensor_tensor(rsum[:, :], rsum[:, :], esink[:, :], ALU.add).then_inc(sink_added, 1)
                    dve.wait_ge(sink_added, sink + 1)
                nc.vector.reciprocal(rinv[:, :], rsum[:, :]).then_inc(inverse_done, 1)
                dve.wait_ge(inverse_done, H + 1)
                for q, (c0, w) in sorted(at.items()):
                    ins = nc.vector.tensor_scalar(prob[:, c0:c0 + w], prob[:, c0:c0 + w], rinv[:, q:q + 1], None, ALU.mult)
                ins.then_inc(p_done, 1)

            def pair_low(H):
                m = H // 2
                dve.wait_ge(o_hi, m + 1)
                hi, lo = (os_hi, os_lo) if m < 4 else (of_hi, of_lo)
                low(lo[:, m % 4, :], bank(7), hi[:, m % 4, :], o_lo)

            def branch_output(n, o, e):
                if e == 0:
                    dve.wait_ge(branch_full, branches[0] + 1)
                    branches[0] += 1
                else:
                    dve.wait_ge(unit_used, n + 1)
                return bank((o + e) % 2)

            def stack_low(H):
                own, other = rows_of(H)
                q, k = query_key(H)
                dve.wait_ge(stack_hi, H + 1)
                ins = nc.vector.tensor_tensor(q_st[other, H % 2, :], q[own, :], q_st[own, H % 2, :].bitcast(F32), ALU.subtract)
                if k is not None:
                    ins = nc.vector.tensor_tensor(k_low[own, H % 2, :], k[own, :], k_hh[own, H % 2, :].bitcast(F32), ALU.subtract)
                ins.then_inc(stack_lo, 1)

            dve.wait_ge(ks_made, 1)
            for kv in range(SWA_KV):
                src = slice(HD * kv, HD * (kv + 1))
                for e in range(2):
                    ins = nc.vector.tensor_tensor(ks_ll[HD * e:HD * (e + 1), kv, :], kraw[src, :], ks_hh[src, kv, :].bitcast(F32),
                                                  ALU.subtract)
            ins.then_inc(ks_split, 1)
            stack_low(0)
            branches = [0]
            at_swa = {q: (WINDOW * q, WINDOW) for q in range(TB)}
            for H in range(HEADS):
                for u in fill(H % 8):
                    n = (U_QF if H < SWA_HEADS else U_G0) + u
                    split(n + 4)
                    if H < SWA_HEADS and 4 <= u < 8:
                        m, o = u - 4, O_QF + u
                        dve.wait_ge(unit_used, n + 1)
                        nc.vector.tensor_copy(kf[:, m, :], bank(o % 2)).then_inc(proj_free[o % 2], 1)
                    elif H >= SWA_HEADS and u % 3 == 2:
                        o = O_G0 + 4 * (u // 3) + 2
                        for e in range(2):
                            m = 2 * (u // 3) + e
                            proj_is_out(dve, o + e - 2)
                            nc.vector.scalar_tensor_tensor(out=part[:, m, :], in0=gate[:, e, :], scalar=1.0,
                                                           in1=branch_output(n, o, e), op0=ALU.add, op1=ALU.mult)\
                                .then_inc(proj_free[(o + e) % 2], 1)
                if H == 0:
                    rotate(qs[:, 3, :], T_QS + 3)
                if H >= 1:
                    copied_probs(H - 1)
                if H < SWA_HEADS:
                    for u in fill(H):
                        if u >= 8:
                            v, use = u - 8, T_VF[u - 8]
                            dve.wait_ge(t_full, use + 1)
                            nc.vector.tensor_copy(vf[:, :, v * P:(v + 1) * P], turned(5 + use % 2)).then_inc(t_free[use % 2], 1)
                at, sink = (at_swa, H) if H < SWA_HEADS else (FOX_AT, None)
                maxima(H, at, sink)
                if H >= 2 and H % 2 == 0:
                    pair_low(H - 1)
                normalize_probs(H, at, sink)
                if H + 1 < HEADS:
                    stack_low(H + 1)

            def merged_low_part(m):
                dve.wait_ge(merged_hi, m + 1)
                hi, lo = (m0_hi, m0_lo) if m < 4 else (m1_hi, m1_lo)
                nc.vector.scalar_tensor_tensor(out=lo[:, m % 4, :], in0=part[:, m, :], scalar=0.5,
                                               in1=hi[:, m % 4, :].bitcast(F32), op0=ALU.mult, op1=ALU.subtract)\
                    .then_inc(merged_lo, 1)

            for u in range(12):
                n = U_G1 + u
                split(n + 4)
                if u == 0:
                    copied_probs(HEADS - 1)
                    pair_low(HEADS - 1)
                if u % 3 == 2:
                    o = O_G1 + 4 * (u // 3) + 2
                    for e in range(2):
                        m = 2 * (u // 3) + e
                        proj_is_out(dve, o + e - 2)
                        nc.vector.scalar_tensor_tensor(out=gate[:, e, :], in0=gate[:, e, :], scalar=1.0,
                                                       in1=branch_output(n, o, e), op0=ALU.add, op1=ALU.mult)\
                            .then_inc(proj_free[(o + e) % 2], 1)
                        proj_is_out(dve, o + e)
                        nc.vector.tensor_tensor(part[:, m, :], part[:, m, :], gate[:, e, :], ALU.add).then_inc(merged, 1)
                if u in (3, 6):
                    for m in (0, 1) if u == 3 else (2, 3):
                        merged_low_part(m)
            for n in range(T_MEM2, T_X2):
                turned_low(n, memT_hi, memT_lo, (n - T_MEM2) // 2)
            for m in range(4, KC):
                merged_low_part(m)
            dve.wait_ge(back, 16 * TB)
            scale_residual(xb, range(TB))

            def project_tiles(s, ln, n0, t0, splits, last_splits):
                dve.wait_ge(scaled, TB * (s + 2))
                for b in range(TB):
                    for e in range(2):
                        j = 2 * b + e
                        if j < 6:
                            dve.wait_ge(tile_full, 6 * s + j + 1)
                        else:
                            dve.wait_ge(unit_used, n0 + KC)
                        add_tile(xb, j, bank(j), tile_free)
                    block_stats(ln, xb, b, tile_free, 8 * s + 2 * b + 2)
                    for n in splits[b]:
                        split(n)
                    gain(ln, xb, b)
                    if 1 <= b <= 2:
                        turned_pair(t0, b - 1)
                    if b == 2:
                        for n in last_splits:
                            split(n)
                turned_pair(t0, 2)

            for n in range(U_OUT + 4, U_OUT + KC):
                split(n)
            project_tiles(0, 1, U_OUT, T_X2, ((), (), (U_MV,), (U_MV + 2, U_MV + 3)), (U_MV + 1,))
            for k in range(4, 7):
                split(U_MV + k)
            turned_pair(T_X2, 3)
            split(U_MV + 7)
            for k in range(4):
                split(U_MQ + k)
            scale_residual(xb, range(TB), T_X2)
            for h in range(MEM_HEADS + 1):
                if h < MEM_HEADS:
                    for m in range(2):
                        split(U_MQ + 2 * h + m + 4)
                if h >= 1:
                    dve.wait_ge(mt_full, 2 * h)
                    nc.vector.tensor_copy(probT[:, HALF:2 * HALF], bank(5)).then_inc(mt_free[1], 1)
                if h < MEM_HEADS:
                    maxima(HEADS + h, at_swa)
                    normalize_probs(HEADS + h, at_swa)
                if h >= 1:
                    for e in range(2):
                        m = 2 * (h - 1) + e
                        dve.wait_ge(om_hi_done, m + 1)
                        low(om_lo[:, m, :], bank(6 + e), om_hi[:, m, :], om_lo_done)
            for n in range(U_MO + 4, U_MO + KC):
                split(n)
            u = U_FFN2
            project_tiles(1, 2, U_MO, T_X3, ((), (), (u,), (u + 2, u + 3)), (u + 1,))
            turned_pair(T_X3, 3)
            scale_residual(xb, range(TB), T_X3)
            ffn(1, U_FFN2, xb)


_INS = ["x", "mem", "ffn1_w_gate", "ffn1_w_up", "ffn1_w_down", "ln1_g", "ln1_b", "mix_w_in", "mix_b_gate",
        "mix_b_forget", "swa_sinks", "mix_w_branch_swa", "mix_w_branch_fox", "mix_w_out", "ln2_g", "ln2_b",
        "mem_w_q", "mem_w_k", "mem_w_v", "mem_w_o", "ln3_g", "ln3_b", "ffn2_w_gate", "ffn2_w_up", "ffn2_w_down",
        "ln4_g", "ln4_b"]


def kernel(**inputs):
    import numpy as _np
    import concourse.bacc as _bacc
    from concourse.bass_utils import run_bass_kernel_spmd as _run

    nc = _bacc.Bacc("TRN2", target_bir_lowering=False, num_devices=1)
    arrays, tensors = {}, {}
    for name in _INS:
        a = _np.ascontiguousarray(inputs[name])
        arrays[f"in_{name}"] = a
        ap = nc.dram_tensor(f"in_{name}", a.shape, F32, kind="ExternalInput").ap()
        if len(a.shape) == 3:
            ap = ap[0]
        tensors[name] = ap
    half = HD // 2
    freq = _np.float32(ROPE_THETA) ** (-_np.arange(half, dtype=_np.float32) / half)
    angle = _np.arange(SEQ, dtype=_np.float32)[None, :] * _np.tile(freq, P // half)[:, None]
    arrays["in_rope"] = _np.stack([_np.cos(angle), _np.sin(angle)])
    tensors["rope"] = nc.dram_tensor("in_rope", (2, P, SEQ), F32, kind="ExternalInput").ap()
    out = nc.dram_tensor("out", (1, SEQ, D), F32, kind="ExternalOutput").ap()
    spill = nc.dram_tensor("x_spill", (SEQ, D), F32, kind="Internal").ap()
    program(nc, tensors, out[0], spill)
    r = _run(nc, [arrays], core_ids=[0])
    return r.results[0]["out"]
```

```python
from contextlib import ExitStack

import concourse.bass as bass
from concourse import mybir

F32 = mybir.dt.float32
F32R = mybir.dt.float32r
BF16 = mybir.dt.bfloat16
ACT = mybir.ActivationFunctionType
ALU = mybir.AluOpType
AX = mybir.AxisListType

P = 128
D = 1024
SEQ = 512
TB = SEQ // P
KC = D // P
HALF = 512
HD = 64
SWA_HEADS, SWA_KV, FOX_HEADS = 8, 2, 8
WINDOW = 256
CHUNK = 64
MEM = 256
MB = MEM // P
MEM_HEADS = 4
D_FF = 2816
FF_PAIRS = D_FF // P // 2
ALPHA = 2.0 ** 0.25
LN_EPS = 1e-5
ROPE_THETA = 10000.0
NEG = -1e30
QK_SCALE = HD ** -0.5
MEM_SCALE = (D // MEM_HEADS) ** -0.5

C_QS = 0
C_KS = C_QS + SWA_HEADS * HD
C_VS = C_KS + SWA_KV * HD
C_QF = C_VS + SWA_KV * HD
C_KF = C_QF + FOX_HEADS * HD
C_VF = C_KF + FOX_HEADS * HD
C_F = C_VF + FOX_HEADS * HD
C_G = C_F + FOX_HEADS

U_FFN1 = 0
U_MK = U_FFN1 + 6 * FF_PAIRS
U_F = U_MK + KC
U_KS = U_F + 1
U_VS = U_KS + 1
U_QS = U_VS + 1
U_QF = U_QS + 4
U_KF = U_QF + 4
U_VF = U_KF + 4
U_G0 = U_VF + 4
U_G1 = U_G0 + 12
U_OUT = U_G1 + 12
U_MV = U_OUT + KC
U_MQ = U_MV + KC
U_MO = U_MQ + KC
U_FFN2 = U_MO + KC
T_MEM = 2 * TB
T_X1 = T_MEM + 2 * MB
T_MEM2 = T_X1 + 2 * TB
T_X2 = T_MEM2 + 2 * MB
T_X3 = T_X2 + 2 * TB
FOX_COPIES = P // FOX_HEADS
POOL_BLOCKS = (TB - 1, TB - 1, TB - 1, 2)
AFTER_MK = (1, 3, 4, 5)
RAW = 3
RING = 6

O_MK = 0
O_F = O_MK + KC
O_KS = O_F + 1
O_VS = O_KS + 1
O_QS = O_VS + 1
O_QF = O_QS + 4
O_KF = O_QF + 4
O_VF = O_KF + 4
O_G0 = O_VF + 4
O_G1 = O_G0 + 16
O_MQ = O_G1 + 16
O_END = O_MQ + KC

HEADS = SWA_HEADS + FOX_HEADS

T_F, T_C, T_VS = 0, 1, 2


def fill(slot):
    first = 3 * (slot // 2) + (slot % 2)
    return range(first, first + 1 + slot % 2)


def t_uses():
    n, heads, values = T_VS + 1, [], {}
    for slot in range(HEADS + 1):
        if slot >= 1:
            heads.append(n)
            n += 2 if slot - 1 < SWA_HEADS else 3
        if slot < SWA_HEADS:
            for u in fill(slot):
                if u >= 8:
                    values[u - 8] = n
                    n += 1
    return heads, values, n


T_HEAD, T_VF, T_END = t_uses()

FOX_AT = {3: (0, 512), 2: (512, 384), 0: (896, 128), 1: (1024, 256)}
FOX_T = {0: 0, 1: 512, 2: 1024, 3: 896}
SWA_T = {0: 0, 1: 256, 2: 512, 3: 768}


def fox_transposes():
    every = [(q, k, FOX_T[k] + P * (q - k)) for k in range(TB) for q in range(k, TB)]
    return [[x for x in every if x[2] // HALF == b] for b in range(3)]


def swa_transposes():
    every = [(q, k, SWA_T[k] + P * (q - k)) for k in range(TB) for q in (k, k + 1) if q < TB]
    return [[x for x in every if x[2] // HALF == b] for b in range(2)]


def program(nc, t, out, x_spill):
    ctx = ExitStack()
    with ctx:
        base = [(nc.sbuf_base + 63) // 64 * 64]

        def place(name, shape, dt, at=None):
            size = 2 if dt == BF16 else 4
            for n in shape[1:]:
                size *= n
            where = base[0] if at is None else at
            if at is None:
                base[0] += (size + 31) // 32 * 32
            return nc.alloc_sbuf_tensor_at(name, shape, dt, offset=where)

        def zone(kib):
            where = base[0]
            base[0] += kib * 1024
            return where

        def sem(name):
            return ctx.enter_context(nc.semaphore(name))

        ring_hi = place("ring_hi", [P, RING, D], F32R)
        ring_lo = place("ring_lo", [P, RING, D], F32R)
        z_xh, z_xl, z_r = zone(16), zone(16), zone(32)
        xT_hi = place("xT_hi", [P, KC, SEQ], F32R, z_xh)
        xT_lo = place("xT_lo", [P, KC, SEQ], F32R, z_xl)
        h_hi = place("h_hi", [P, 2, SEQ], F32R, z_r)
        h_lo = place("h_lo", [P, 2, SEQ], F32R, z_r + 4096)
        os_hi = place("os_hi", [P, 4, SEQ], F32R, z_r)
        os_lo = place("os_lo", [P, 4, SEQ], F32R, z_r + 8192)
        of_hi = place("of_hi", [P, 4, SEQ], F32R, z_r + 16384)
        of_lo = place("of_lo", [P, 4, SEQ], F32R, z_r + 24576)
        memT_hi = place("memT_hi", [P, KC, MEM], F32R, z_r + 16384)
        memT_lo = place("memT_lo", [P, KC, MEM], F32R, z_r + 24576)
        m0_hi = place("m0_hi", [P, 4, SEQ], F32R, z_r)
        m0_lo = place("m0_lo", [P, 4, SEQ], F32R, z_r + 8192)
        m1_hi = place("m1_hi", [P, 4, SEQ], F32R, z_xh)
        m1_lo = place("m1_lo", [P, 4, SEQ], F32R, z_xl)
        om_hi = place("om_hi", [P, KC, SEQ], F32R, z_r)
        om_lo = place("om_lo", [P, KC, SEQ], F32R, z_r + 16384)

        raw = place("raw", [P, RAW, D], F32)
        z_a, z_b, z_q, z_v = zone(16), zone(16), zone(8), zone(8)
        z_p = zone(10)
        xa = place("xa", [P, TB, D], F32, z_a)
        xb = place("xb", [P, TB, D], F32, z_b)
        part = place("part", [P, KC, SEQ], F32, z_a)
        qm_hi = place("qm_hi", [P, 2, 2, SEQ], F32R, z_a)
        qm_lo = place("qm_lo", [P, 2, 2, SEQ], F32R, z_a + 8192)
        qs = place("qs", [P, 4, SEQ], F32, z_a)
        ks_hh = place("ks_hh", [P, SWA_KV, SEQ], F32R, z_a + 8192)
        ks_ll = place("ks_ll", [P, SWA_KV, SEQ], F32R, z_a + 12288)
        kf = place("kf", [P, 4, SEQ], F32, z_b)
        q_st = place("q_st", [P, 2, SEQ], F32R, z_b + 8192)
        k_hh = place("k_hh", [P, 2, SEQ], F32R, z_b + 12288)
        z_k = zone(4)
        pm_hi = place("pm_hi", [P, 2 * HALF], F32R, z_p + 5120)
        pm_lo = place("pm_lo", [P, 2 * HALF], F32R, z_k)
        k_low = place("k_low", [P, 2, SEQ], F32R, z_k)
        qf = place("qf", [P, 4, SEQ], F32, z_q)
        vf = place("vf", [P, TB, FOX_HEADS * HD], F32, z_v)
        vm_hi = place("vm_hi", [P, MB, D], F32R, z_v)
        vm_lo = place("vm_lo", [P, MB, D], F32R, z_q)
        mem_in = place("mem_in", [P, MB, D], F32, z_v)
        sig = place("sig", [P, 2, SEQ], F32, z_q)
        hf = place("hf", [P, 2, SEQ], F32, z_q + 4096)
        fz = place("fz", [P, SEQ], F32, z_v)
        fe = place("fe", [P, SEQ], F32, z_v + 2048)
        fa = place("fa", [P, SEQ], F32, z_v + 4096)
        fb = place("fb", [P, SEQ], F32, z_v + 6144)
        prob = place("prob", [P, 1280], F32, z_p)
        probT = place("probT", [P, 1280], F32, z_p + 5120)
        ln_g = place("ln_g", [P, D], F32, z_p)
        ln_b = place("ln_b", [P, D], F32, z_p + 4096)
        lsn = place("lsn", [P, TB, P], F32, z_p)
        tri_f = place("tri_f", [P, SEQ], F32, z_p + 5120)
        rot = [place(f"rot{i}", [P, SEQ], F32, at) for i, at in enumerate((z_p + 2048, z_q + 2048))]
        kraw = place("kraw", [P, SEQ], F32, z_p + 7168)
        cos_t = place("cos_t", [P, SEQ], F32, z_q + 4096)
        sin_t = place("sin_t", [P, SEQ], F32, z_q + 6144)
        z_km = zone(8)
        km = place("km", [P, KC, MEM], F32, z_km)
        km_lo = place("km_lo", [P, KC, MEM], F32R, z_km)
        km_hi = place("km_hi", [P, KC, MEM], F32R, base[0])
        vs = place("vs", [P, TB, P], F32)
        gate = place("gate", [P, 2, SEQ], F32)
        c_hi = place("c_hi", [P, SEQ], BF16, z_p + 4096)
        c_mid = place("c_mid", [P, SEQ], BF16, z_p)
        c_lo = place("c_lo", [P, SEQ], BF16, z_p + 1024)
        c_q = place("c_q", [P, SEQ], BF16)
        c_k = place("c_k", [P, SEQ], BF16)
        c_qh = place("c_qh", [P, 2, SEQ], BF16)
        ident = place("ident", [P, P], F32)
        ident_b = place("ident_b", [P, P], BF16)
        mask_s = place("mask_s", [P, WINDOW], BF16)
        mask_0 = place("mask_0", [P, WINDOW], BF16)
        mask_c = place("mask_c", [P, P], BF16)
        pick = place("pick", [P, 6, FOX_HEADS], F32)
        pick_part = place("pick_part", [P, 8], F32)
        pick_head = place("pick_head", [P, FOX_HEADS], F32)
        bias_rows = place("bias_rows", [2 * KC + 1, P], F32, z_p + 8192)
        b_gate = place("b_gate", [P, 2, KC], F32)
        b_f = place("b_f", [P, 1], F32)
        sinks = place("sinks", [P, SWA_HEADS], F32)
        stats = place("stats", [P, TB, 2, 6], F32)
        mv = place("mv", [P, TB, 2], F32)
        rstd = place("rstd", [P, TB], F32)
        neg_mean = place("neg_mean", [P, TB], F32)
        shift = place("shift", [P, TB], F32)
        veps = place("veps", [P, TB], F32)
        expo = place("expo", [P, 1], F32)
        top = place("top", [P, 4], F32)
        ntop = place("ntop", [P, 4], F32)
        rsum = place("rsum", [P, 4], F32)
        esink = place("esink", [P, 4], F32)
        rinv = place("rinv", [P, 4], F32)

        ps = [ctx.enter_context(nc.psum_tensor(f"bank{i}", [P, HALF], F32)) for i in range(2)]
        sc = ctx.enter_context(nc.psum_tensor("banks_scores", [P, 3 * HALF], F32))
        ps += [sc[:, HALF * i:HALF * (i + 1)] for i in range(3)]
        ps += [ctx.enter_context(nc.psum_tensor(f"bank{i}", [P, HALF], F32)) for i in range(5, 8)]

        landed = [sem(f"unit_landed{i}") for i in range(RAW)]
        unit_hi = sem("unit_hi")
        unit_lo = sem("unit_lo")
        unit_used = sem("unit_used")
        x_in = [sem(f"x_in{i}") for i in range(TB)]
        mem_in_ok = sem("mem_in_ok")
        small_in, bias_turned, bias_made = sem("small_in"), sem("bias_turned"), sem("bias_made")
        gains_in = sem("gains_in")
        pool_step = sem("pool_step")
        consts = sem("consts")
        zeroed = sem("zeroed")
        dve_consts = sem("dve_consts")
        xt_full, xt_hi, xt_lo = sem("xt_full"), sem("xt_hi"), sem("xt_lo")
        sig_done, gated = sem("sig_done"), sem("gated")
        h_full, h_hi_done, h_lo_done = sem("h_full"), sem("h_hi_done"), sem("h_lo_done")
        scaled = sem("scaled")
        down_full = sem("down_full")
        sums = sem("sums")
        stats_done, mean_done, eps_added, rstd_done = sem("stats_done"), sem("mean_done"), sem("eps_added"), sem("rstd_done")
        shift_done = sem("shift_done")
        standard = sem("standard")
        gained, ln_done = sem("gained"), sem("ln_done")
        centred = sem("centred")
        last_done = sem("last_done")
        proj_free = [sem(f"proj_free{i}") for i in range(2)]
        branch_full = sem("branch_full")
        f_act, f_dve = sem("f_act"), sem("f_dve")
        t_full = sem("t_full")
        t_free = [sem(f"t_free{i}") for i in range(2)]
        s_full, top_done, ntop_done, exp_done = sem("s_full"), sem("top_done"), sem("ntop_done"), sem("exp_done")
        sink_added, inverse_done, p_done = sem("sink_added"), sem("inverse_done"), sem("p_done")
        o_full, o_hi, o_lo = sem("o_full"), sem("o_hi"), sem("o_lo")
        ks_split = sem("ks_split")
        stack_hi, stack_lo = sem("stack_hi"), sem("stack_lo")
        c_made, cq_made = sem("c_made"), sem("cq_made")
        rope_sin = sem("rope_sin")
        angles_in, rope_cos, rope_done, ks_made = sem("angles_in"), sem("rope_cos"), sem("rope_done"), sem("ks_made")
        merged, merged_hi, merged_lo = sem("merged"), sem("merged_hi"), sem("merged_lo")
        tile_full, tile_free = sem("tile_full"), sem("tile_free")
        vm_hi_done, vm_done = sem("vm_hi_done"), sem("vm_done")
        km_hi_done, km_split = sem("km_hi_done"), sem("km_split")
        qm_hi_done, pm_hi_done = sem("qm_hi_done"), sem("pm_hi_done")
        mt_full = sem("mt_full")
        mt_free = [sem(f"mt_free{i}") for i in range(2)]
        om_full, om_hi_done, om_lo_done = sem("om_full"), sem("om_hi_done"), sem("om_lo_done")
        spilled, back, stored = sem("spilled"), sem("back"), sem("stored")

        block = ctx.enter_context(nc.Block())

        def rows_of(H):
            own, other = slice(HD * (H % 2), HD * (H % 2 + 1)), slice(HD * (1 - H % 2), HD * (2 - H % 2))
            return own, other

        def query_key(H):
            if H < SWA_HEADS:
                return qs[:, H // 2, :], None
            m = (H - SWA_HEADS) // 2
            return qf[:, m, :], kf[:, m, :]

        def proj_is_out(eng, o):
            eng.wait_ge(proj_free[o % 2], o // 2 + 1)

        def t_is_out(eng, n):
            eng.wait_ge(t_free[n % 2], n // 2 + 1)

        def head_uses(H):
            n = T_HEAD[H]
            return range(n, n + (2 if H < SWA_HEADS else 3))

        def p_at(H, q, k):
            return WINDOW * q + P * (k - q + 1) if H < SWA_HEADS else FOX_AT[q][0] + P * k

        def bank(i):
            return ps[i][:, :]

        def tile_sums(f, pair, j):
            return 8 * (f + 1 + pair) + j

        def xt_bank(n):
            if n < T_MEM:
                return n
            if n < T_X1:
                return 4 + (n - T_MEM)
            if n < T_MEM2:
                return 2 + n % 2
            if n < T_X2:
                return (2, 3, 4, 7)[n - T_MEM2]
            if n < T_X3:
                return (n - T_X2) % 4
            return n - T_X3

        def halves(n, b):
            if n == 3 and b == TB - 1:
                return slice(0, HALF), slice(HALF, D)
            return (slice(0, D),)

        def turned(i):
            return ps[i][:, :].rearrange("p (c n) -> p c n", n=P)

        def forget_views(n, ring):
            src = raw[:, n % RAW, 0:KC * FOX_HEADS].rearrange("p (k h) -> p k h", k=KC).unsqueeze(2)
            dst = ring[:, n % RING, :].rearrange("p (k r h) -> p k r h", k=KC, h=FOX_HEADS)
            return src.to_broadcast([P, KC, FOX_COPIES, FOX_HEADS]), dst

        @block.sync
        def _(sp):
            def load(n, src, form=None, off=None):
                dst = raw[:, n % RAW, :]
                if form == "columns":
                    dst = dst.rearrange("p (k c) -> p k c", k=KC)
                elif form == "branch":
                    dst = dst.rearrange("p (k c) -> p k c", k=4)
                elif form == "forget":
                    dst = raw[:, n % RAW, 0:KC * FOX_HEADS].rearrange("p (k c) -> p k c", k=KC)
                if off is not None:
                    sp.wait_ge(unit_lo, off + (n - RAW + 1))
                elif n >= RAW:
                    sp.wait_ge(unit_lo, n - RAW + 1)
                sp.dma_start(dst, src).then_inc(landed[n % RAW], 16)

            def columns(w, c0):
                return w.rearrange("(k p) c -> p k c", p=P)[:, :, c0:c0 + P]

            def rows(w, r):
                return w[r * P:(r + 1) * P, :]

            def load_x(blocks):
                for b in blocks:
                    sp.dma_start(xa[:, b, :], t["x"][b * P:(b + 1) * P, :]).then_inc(x_in[b], 16)

            def ffn_units(n0, w_gate, w_up, w_down):
                for m in range(2):
                    load(n0 + 2 * m, columns(w_gate, m * P), "columns")
                    if n0 == U_FFN1 and m == 0:
                        load_x((2,))
                    load(n0 + 2 * m + 1, columns(w_up, m * P), "columns")
                    if n0 == U_FFN1 and m == 0:
                        load_x((3,))
                g = w_gate.rearrange("(k p) (m c) -> p k m c", p=P, c=P)
                u = w_up.rearrange("(k p) (m c) -> p k m c", p=P, c=P)
                d = w_down.rearrange("(m p) c -> p m c", p=P)
                n = n0 + 4
                with sp.Fori(0, FF_PAIRS - 1) as i:
                    for m in range(2):
                        chunk = bass.ds(i * 2 + (2 + m), 1)
                        load(n + 4 * m, g[:, :, chunk, :].rearrange("p k m c -> p k (m c)"), "columns", i * 6)
                        load(n + 4 * m + 1, u[:, :, chunk, :].rearrange("p k m c -> p k (m c)"), "columns", i * 6)
                        if m == 0:
                            for r in range(2):
                                load(n + 2 + r, d[:, bass.ds(i * 2 + r, 1), :].rearrange("p m c -> p (m c)"), None, i * 6)
                for r in range(2):
                    load(n0 + 6 * FF_PAIRS - 2 + r, rows(w_down, 2 * FF_PAIRS - 2 + r))

            load_x((0, 1))
            ffn_units(U_FFN1, t["ffn1_w_gate"], t["ffn1_w_up"], t["ffn1_w_down"])
            for m in range(KC):
                load(U_MK + m, columns(t["mem_w_k"], m * P), "columns")
            w_in = t["mix_w_in"]
            load(U_F, w_in.rearrange("(k p) c -> p k c", p=P)[:, :, C_F:C_F + FOX_HEADS], "forget")
            load(U_KS, columns(w_in, C_KS), "columns")
            load(U_VS, columns(w_in, C_VS), "columns")
            for first, col in ((U_QS, C_QS), (U_QF, C_QF), (U_KF, C_KF), (U_VF, C_VF)):
                for m in range(4):
                    load(first + m, columns(w_in, col + m * P), "columns")
            for g, (first, w) in enumerate(((U_G0, t["mix_w_branch_swa"]), (U_G1, t["mix_w_branch_fox"]))):
                for u in range(4):
                    for e in range(2):
                        load(first + 3 * u + e, columns(w_in, C_G + g * D + (2 * u + e) * P), "columns")
                    load(first + 3 * u + 2, w.rearrange("(k p) c -> p k c", p=P)[:, :, 2 * P * u:2 * P * (u + 1)], "branch")
            for m in range(KC):
                load(U_OUT + m, rows(t["mix_w_out"], m))
            for m in range(KC):
                load(U_MV + m, rows(t["mem_w_v"], m))
            for m in range(KC):
                load(U_MQ + m, columns(t["mem_w_q"], m * P), "columns")
            for m in range(KC):
                load(U_MO + m, rows(t["mem_w_o"], m))
            ffn_units(U_FFN2, t["ffn2_w_gate"], t["ffn2_w_up"], t["ffn2_w_down"])
            for b in range(TB):
                for e, cols in enumerate(halves(3, b)):
                    if b < 2:
                        sp.wait_ge(ln_done, 3 * TB + b + 1)
                    else:
                        sp.wait_ge(last_done, b + e - 1)
                    sp.dma_start(out[b * P:(b + 1) * P, cols], xb[:, b, cols]).then_inc(stored, 16)
            sp.wait_ge(stored, 16 * (TB + 1))

        @block.gpsimd
        def _(pool):
            steps = [0]

            def step(ins):
                steps[0] += 1
                ins.then_inc(pool_step, 1)
                pool.wait_ge(pool_step, steps[0])

            def load_gains(n, after=None):
                pool.dma_start(ln_g[:, :], t[f"ln{n}_g"].to_broadcast([P, D])).then_inc(gains_in, 16)
                pool.dma_start(ln_b[:, :], t[f"ln{n}_b"].to_broadcast([P, D])).then_inc(gains_in, 16)

            def load_mem():
                pool.dma_start(mem_in[:, :, :], t["mem"].rearrange("(b p) d -> p b d", p=P)).then_inc(mem_in_ok, 16)

            def inverse_deviation(n, b):
                count, col = n * TB + b + 1, slice(b, b + 1)
                pool.wait_ge(mean_done, count)
                nc.gpsimd.tensor_scalar(veps[:, col], mv[:, b, 1:2], LN_EPS, None, ALU.add).then_inc(eps_added, 1)
                nc.gpsimd.tensor_scalar(neg_mean[:, col], mv[:, b, 0:1], -1.0, None, ALU.mult).then_inc(eps_added, 1)
                pool.wait_ge(eps_added, 2 * count)
                nc.gpsimd.tensor_tensor(rstd[:, col], veps[:, col], expo[:, :], ALU.pow).then_inc(rstd_done, 1)
                pool.wait_ge(rstd_done, count)
                nc.gpsimd.tensor_tensor(shift[:, col], neg_mean[:, col], rstd[:, col], ALU.mult).then_inc(shift_done, 1)

            def add_bias(n, x, b):
                if b == 0:
                    pool.wait_ge(gains_in, 32 * (n + 1))
                pool.wait_ge(gained, n * TB + b + 1)
                nc.gpsimd.tensor_tensor(x[:, b, :], x[:, b, :], ln_b[:, :], ALU.add).then_inc(ln_done, 1)

            def layer_norm(n, x, lag):
                for b in range(TB + lag):
                    if b < TB:
                        inverse_deviation(n, b)
                    if 0 <= b - lag < POOL_BLOCKS[n]:
                        add_bias(n, x, b - lag)

            step(nc.gpsimd.memset(ident[:, :], 0.0))
            nc.gpsimd.affine_select(out=ident[:, :], in_=ident[:, :], compare_op=ALU.not_equal, fill=1.0, base=0,
                                    pattern=[[-1, P]], channel_multiplier=1).then_inc(consts, 1)
            pool.wait_ge(consts, 1)
            step(nc.gpsimd.memset(ident_b[:, :], 0.0))
            step(nc.gpsimd.affine_select(out=ident_b[:, :], in_=ident_b[:, :], compare_op=ALU.not_equal, fill=1.0, base=0,
                                         pattern=[[-1, P]], channel_multiplier=1))
            step(nc.gpsimd.memset(expo[:, :], -0.5))
            step(nc.gpsimd.memset(mask_s[:, :], NEG))
            step(nc.gpsimd.memset(mask_0[:, :], NEG))
            step(nc.gpsimd.memset(mask_s[0:CHUNK, CHUNK:3 * CHUNK], 0.0))
            step(nc.gpsimd.memset(mask_s[CHUNK:P, 2 * CHUNK:WINDOW], 0.0))
            step(nc.gpsimd.memset(mask_0[0:CHUNK, 2 * CHUNK:3 * CHUNK], 0.0))
            step(nc.gpsimd.memset(mask_0[CHUNK:P, 2 * CHUNK:WINDOW], 0.0))
            step(nc.gpsimd.memset(mask_c[:, :], 0.0))
            step(nc.gpsimd.affine_select(out=mask_c[:, :], in_=mask_c[:, :], compare_op=ALU.is_ge, fill=NEG, base=0,
                                         pattern=[[-1, P]], channel_multiplier=1))
            step(nc.gpsimd.memset(pick[:, :, :], 0.0))
            nc.gpsimd.affine_select(out=pick[:, :, :], in_=pick[:, :, :], compare_op=ALU.not_equal, fill=1.0, base=0,
                                    pattern=[[-FOX_HEADS, 6], [-1, FOX_HEADS]], channel_multiplier=1).then_inc(consts, 1)
            pool.wait_ge(consts, 2)
            pool.wait_ge(x_in[TB - 1], 16)
            load_mem()
            pool.wait_ge(unit_used, 1)
            load_gains(1)
            layer_norm(0, xa, 1)
            for b in range(TB):
                pool.wait_ge(ln_done, b + 1)
                pool.dma_start(x_spill[b * P:(b + 1) * P, :], xa[:, b, :]).then_inc(spilled, 16)
            for angles, row in ((cos_t, 0), (sin_t, 1)):
                pool.dma_start(angles[:, :], t["rope"][row]).then_inc(angles_in, 16)
            step(nc.gpsimd.memset(tri_f[:, :], 1.0))
            nc.gpsimd.affine_select(out=tri_f[:, :], in_=tri_f[:, :], compare_op=ALU.is_ge, fill=0.0, base=0,
                                    pattern=[[1, SEQ]], channel_multiplier=-1).then_inc(zeroed, 1)
            pool.wait_ge(zeroed, 1)
            pool.wait_ge(dve_consts, 4)
            pool.wait_ge(c_made, 2)
            for h in range(FOX_HEADS):
                if h >= 2:
                    pool.wait_ge(s_full, SWA_HEADS + h - 1)
                nc.gpsimd.tensor_scalar(c_qh[:, h % 2, :], c_q[:, :], pick_head[:, h:h + 1], None, ALU.mult).then_inc(cq_made, 1)
                pool.wait_ge(cq_made, h + 1)
            pool.wait_ge(s_full, HEADS)
            for b in range(TB):
                pool.dma_start(xb[:, b, :], x_spill[b * P:(b + 1) * P, :]).then_inc(back, 16)
            pool.wait_ge(o_full, HEADS)
            load_mem()
            load_gains(2)
            layer_norm(1, xb, 0)
            pool.wait_ge(om_full, KC)
            pool.wait_ge(ln_done, 2 * TB)
            load_gains(3)
            layer_norm(2, xb, 0)
            pool.wait_ge(ln_done, 3 * TB)
            load_gains(4)
            layer_norm(3, xb, 1)

        @block.tensor
        def _(pe):
            def parts(n):
                return ring_hi[:, n % RING, :], ring_lo[:, n % RING, :]

            def split_product(dst, hi, lo, mhi, mlo, start, stop):
                pe.matmul(dst, hi, mhi, start=start, stop=False)
                pe.matmul(dst, hi, mlo, start=False, stop=False)
                return pe.matmul(dst, lo, mhi, start=False, stop=stop)

            def ready(n, off=None):
                pe.wait_ge(unit_lo, n + 1 if off is None else off + (n + 1))

            def project(n, dst, acts=(xT_hi, xT_lo), width=SEQ):
                hi, lo = (r.rearrange("p (k c) -> p k c", k=KC) for r in parts(n))
                for k in range(KC):
                    mm = split_product(dst, hi[:, k, :], lo[:, k, :], acts[0][:, k, 0:width], acts[1][:, k, 0:width],
                                       k == 0, k == KC - 1)
                mm.then_inc(unit_used, 1)

            def turn(src, dst, c0):
                for c in range(4):
                    mm = pe.transpose(dst[:, c * P:(c + 1) * P], src[:, (c0 + c) * P:(c0 + c + 1) * P], ident[:, :])
                return mm

            def turn_rows(n, src):
                for e in range(2):
                    if T_X1 <= n + e < T_MEM2:
                        pe.wait_ge(xt_lo, n + e - 1)
                    elif T_X2 + 4 <= n + e < T_X3:
                        pe.wait_ge(xt_lo, n + e - 3)
                    turn(src, bank(xt_bank(n + e)), 4 * e).then_inc(xt_full, 1)

            def ffn(f, n0):
                def gate_up(side, n, chunk, i=None):
                    for m in range(2):
                        ready(n + m, None if i is None else i * 6)
                        if m == 0 and i is not None:
                            pe.wait_ge(h_full, i * 2 + (chunk - 1))
                        elif m == 0 and chunk >= 2:
                            pe.wait_ge(h_full, chunk - 1)
                        project(n + m, bank(2 * side + m))

                def half_units(n, side, part, units=range(2)):
                    toks = slice(SEQ // 2 * part, SEQ // 2 * (part + 1))
                    for m in units:
                        ready(n + m)
                        hi, lo = (r.rearrange("p (k c) -> p k c", k=KC) for r in parts(n + m))
                        for k in range(KC):
                            mm = split_product(bank(2 * side + m)[:, toks], hi[:, k, :], lo[:, k, :], xT_hi[:, k, toks],
                                               xT_lo[:, k, toks], k == 0, k == KC - 1)
                        if part == 1:
                            mm.then_inc(unit_used, 1)

                def first_units():
                    for b in range(TB):
                        pe.wait_ge(x_in[b], 16)
                        if b == TB - 1:
                            pe.wait_ge(bias_made, 2)
                        turn_rows(2 * b, xa[:, b, :])
                        if b == 1:
                            pe.wait_ge(small_in, 48)
                            pe.transpose(bank(7)[:, 0:2 * KC + 1], bias_rows[:, :], ident[0:2 * KC + 1, 0:2 * KC + 1])\
                                .then_inc(bias_turned, 1)
                        if b % 2:
                            pe.wait_ge(xt_lo, 2 * b + 2)
                            half_units(n0, 0, b // 2)
                    pe.wait_ge(mem_in_ok, 16)
                    for b in range(MB):
                        turn_rows(T_MEM + 2 * b, mem_in[:, b, :])
                    gate_up(1, n0 + 2, chunk0 + 1)

                def first_units_2():
                    pe.wait_ge(xt_lo, T_X3 + 4)
                    half_units(n0, 0, 0)
                    pe.wait_ge(ln_done, 2 * TB + 3)
                    turn_rows(T_X3 + 4, xb[:, 2, :])
                    half_units(n0 + 2, 1, 0, (0,))
                    pe.wait_ge(tile_free, 16)
                    pe.wait_ge(ln_done, 3 * TB)
                    turn_rows(T_X3 + 6, xb[:, 3, :])
                    half_units(n0 + 2, 1, 0, (1,))
                    pe.wait_ge(xt_lo, T_X3 + 8)
                    for side in range(2):
                        half_units(n0 + 2 * side, side, 1)

                def last_down(n, pair):
                    for m in range(2):
                        ready(n + m)
                        pe.wait_ge(h_lo_done, 2 * pair + 1 + m)
                        for j in range(4):
                            if m == 0:
                                pe.wait_ge(sums, tile_sums(f, pair, j - 3))
                            mm = down_product(n, j, m)
                            if m == 1:
                                mm.then_inc(down_full, 1)
                    for j in range(4, 8):
                        pe.wait_ge(sums, tile_sums(f, pair, j - 3))
                        for m in range(2):
                            mm = down_product(n, j, m)
                        mm.then_inc(*((down_full, 1) if j < 7 else (unit_used, 2)))

                def down_product(n, j, m):
                    b, half = j // 2, j % 2
                    hi, lo = (r[:, half * HALF:(half + 1) * HALF] for r in parts(n + m))
                    tok = slice(b * P, (b + 1) * P)
                    return split_product(bank(4 + j % 4), h_hi[:, m, tok], h_lo[:, m, tok], hi, lo, m == 0, m == 1)

                def down(n, pair, i):
                    ready(n + 1, i * 6)
                    pe.wait_ge(h_lo_done, i * 2 + (2 * pair + 2))
                    for j in range(8):
                        pe.wait_ge(sums, i * 8 + tile_sums(f, pair, j - 3))
                        for m in range(2):
                            mm = down_product(n, j, m)
                        if j < 7:
                            mm.then_inc(down_full, 1)
                        else:
                            mm.then_inc(unit_used, 2)

                pair0, chunk0 = FF_PAIRS * f, 2 * FF_PAIRS * f
                first_units() if f == 0 else first_units_2()
                n = n0 + 4
                if f == 0:
                    pe.wait_ge(xt_lo, T_X1)
                with pe.Fori(0, FF_PAIRS - 1) as i:
                    gate_up(0, n, chunk0 + 2, i)
                    down(n + 2, pair0, i)
                    gate_up(1, n + 4, chunk0 + 3, i)
                last_down(n0 + 6 * FF_PAIRS - 2, pair0 + FF_PAIRS - 1)

            def tile_product(j, k, n0, lhs):
                b, half = j // 2, j % 2
                hi, lo = (r[:, half * HALF:(half + 1) * HALF] for r in parts(n0 + k))
                a_hi, a_lo = lhs(k)
                tok = slice(b * P, (b + 1) * P)
                return split_product(bank(j), a_hi[:, tok], a_lo[:, tok], hi, lo, k == 0, k == KC - 1)

            def tiles(s, n0, lhs, chunk_ready, touched, done=()):
                def product(j, k):
                    return tile_product(j, k, n0, lhs)

                def turn_block(b):
                    pe.wait_ge(ln_done, TB * (s + 1) + b + 1)
                    pe.wait_ge(tile_free, 8 * s + 2 * b + 2)
                    turn_rows((T_X2, T_X3)[s] + 2 * b, xb[:, b, :])

                for k in range(2):
                    ready(n0 + k)
                    chunk_ready(k)
                    for j in ((5, 6, 0, 1, 2, 3, 4, 7), (2, 3, 4, 5, 6, 7, 0, 1))[s]:
                        if (j, k) in done:
                            continue
                        if k == 0:
                            touched(j)
                        mm = product(j, k)
                    mm.then_inc(unit_used, 1)
                for j in range(6):
                    for k in range(2, KC):
                        if j == 0:
                            ready(n0 + k)
                            chunk_ready(k)
                        if (j, k) in done:
                            continue
                        mm = product(j, k)
                    mm.then_inc(tile_full, 1)
                    if j == 4:
                        turn_block(0)
                for k in range(2, KC):
                    product(6, k)
                    product(7, k).then_inc(unit_used, 1)
                    if k == KC // 2:
                        turn_block(1)

            pe.wait_ge(consts, 1)
            ffn(0, U_FFN1)
            for m in range(KC):
                ready(U_MK + m)
                if m >= 2:
                    proj_is_out(pe, O_MK + m - 2)
                elif m == 0:
                    pe.wait_ge(h_full, 2 * FF_PAIRS)
                project(U_MK + m, bank((O_MK + m) % 2)[:, 0:MEM], (memT_hi, memT_lo), MEM)
                if m in AFTER_MK:
                    b = AFTER_MK.index(m)
                    pe.wait_ge(ln_done, b + 1)
                    turn_rows(T_X1 + 2 * b, xa[:, b, :])
            pe.wait_ge(xt_lo, T_MEM2)

            def project_out(n, o):
                ready(n)
                if o >= 2:
                    proj_is_out(pe, o - 2)
                project(n, bank(o % 2))

            def branch(n, o, b_hi, b_lo):
                ready(n)
                hi, lo = (r.rearrange("p (k c) -> p k c", k=4) for r in parts(n))
                for e in range(2):
                    proj_is_out(pe, o + e - 2)
                    cols = slice(e * P, (e + 1) * P)
                    for k in range(4):
                        mm = split_product(bank((o + e) % 2), hi[:, k, cols], lo[:, k, cols], b_hi[:, k, :], b_lo[:, k, :],
                                           k == 0, k == 3)
                    mm.then_inc(*((branch_full, 1) if e == 0 else (unit_used, 1)))

            def t_bank(n):
                if n >= 2:
                    t_is_out(pe, n - 2)
                return bank(5 + n % 2)

            def scores(H):
                if H >= 1:
                    pe.wait_ge(exp_done, H)
                pe.wait_ge(stack_lo, H + 1)
                own, _ = rows_of(H)

                def logits(dst, tok, keys, hh, low, stop):
                    pe.matmul(dst, q_st[:, H % 2, tok], hh[:, keys], start=False, stop=False)
                    return pe.matmul(dst, q_st[own, H % 2, tok], low[own, keys], start=False, stop=stop)

                if H < SWA_HEADS:
                    if H == 0:
                        pe.wait_ge(ks_split, 1)
                    for q in range(TB):
                        at = sc[:, WINDOW * q:WINDOW * (q + 1)]
                        pe.matmul(at, ident_b[:, :], (mask_s if q else mask_0)[:, :], start=True, stop=False)
                        k0 = P * max(q - 1, 0)
                        mm = logits(at[:, WINDOW - (P * (q + 1) - k0):], slice(q * P, (q + 1) * P), slice(k0, P * (q + 1)),
                                    ks_hh[:, H // 4, :], ks_ll[:, H // 4, :], True)
                else:
                    h = H - SWA_HEADS
                    pe.wait_ge(cq_made, h + 1)
                    for q in (3, 2, 0, 1):
                        c0, w = FOX_AT[q]
                        tok = slice(q * P, (q + 1) * P)
                        pe.matmul(sc[:, c0:c0 + w], c_qh[:, h % 2, tok], c_k[:, 0:w], start=True, stop=False)
                        logits(sc[:, c0:c0 + w], tok, slice(0, w), k_hh[:, h % 2, :], k_low[:, h % 2, :], False)
                        mm = pe.matmul(sc[:, c0 + w - P:c0 + w], ident_b[:, :], mask_c[:, :], start=False, stop=True)
                mm.then_inc(s_full, 1)

            def transposed_probs(H, banks=range(2)):
                pe.wait_ge(p_done, H + 1)
                for b in banks:
                    n, blocks = head_uses(H)[b], (swa_transposes() if H < SWA_HEADS else fox_transposes())[b]
                    dst = t_bank(n)
                    for q, k, col in blocks:
                        src = p_at(H, q, k)
                        mm = pe.transpose(dst[:, col - HALF * b:col - HALF * b + P], prob[:, src:src + P], ident[:, :])
                    mm.then_inc(t_full, 1)

            def values(H):
                for n in head_uses(H):
                    t_is_out(pe, n)
                if H % 2 == 0 and H >= 2:
                    pe.wait_ge(o_lo, H // 2)
                dst = ps[7][HD * (H % 2):HD * (H % 2 + 1), :]
                for k in range(TB):
                    if H < SWA_HEADS:
                        v = vs[:, k, HD * (H // 4):HD * (H // 4 + 1)]
                        end, src = min(SEQ, P * k + WINDOW), SWA_T[k]
                    else:
                        h = H - SWA_HEADS
                        v = vf[:, k, HD * h:HD * (h + 1)]
                        end, src = SEQ, FOX_T[k]
                    mm = pe.matmul(dst[:, P * k:end], v, probT[:, src:src + end - P * k], start=k == 0, stop=k == TB - 1,
                                   skip_group_check=True)
                mm.then_inc(o_full, 1)

            project_out(U_F, O_F)
            project_out(U_KS, O_KS)
            pe.wait_ge(f_dve, 2)
            turn(fe, t_bank(T_F), 0).then_inc(t_full, 1)
            project_out(U_VS, O_VS)
            t_is_out(pe, T_F)
            pe.wait_ge(zeroed, 1)
            dst = t_bank(T_C)
            for k in range(TB):
                mm = pe.matmul(dst[:, k * P:], lsn[:, k, :], tri_f[:, 0:SEQ - k * P], start=k == 0, stop=k == TB - 1)
            mm.then_inc(t_full, 1)
            project_out(U_QS, O_QS)
            proj_is_out(pe, O_VS)
            turn(gate[:, 0, :], t_bank(T_VS), 0).then_inc(t_full, 1)
            for m in range(1, 4):
                project_out(U_QS + m, O_QS + m)
            pe.wait_ge(consts, 2)
            for H in range(HEADS):
                if H == SWA_HEADS + 1:
                    values(H - 2)
                for i, u in enumerate(fill(H % 8)):
                    if H < SWA_HEADS:
                        project_out(U_QF + u, O_QF + u)
                    elif u % 3 < 2:
                        project_out(U_G0 + u, O_G0 + 4 * (u // 3) + u % 3)
                    else:
                        pe.wait_ge(o_lo, SWA_HEADS // 2)
                        branch(U_G0 + u, O_G0 + 4 * (u // 3) + 2, os_hi, os_lo)
                    if i == 0 and H >= 2 and H != SWA_HEADS + 1:
                        values(H - 2)
                if H >= 1:
                    transposed_probs(H - 1)
                if H == SWA_HEADS:
                    for o in range(O_QF, O_VF):
                        proj_is_out(pe, o)
                    pe.wait_ge(c_made, 4)
                scores(H)
                if H > SWA_HEADS:
                    transposed_probs(H - 1, (2,))
                elif H < SWA_HEADS:
                    for u in fill(H):
                        if u >= 8:
                            proj_is_out(pe, O_VF + u - 8)
                            turn(gate[:, (u - 7) % 2, :], t_bank(T_VF[u - 8]), 0).then_inc(t_full, 1)
            for u in range(12):
                o = O_G1 + 4 * (u // 3) + u % 3
                if u % 3 < 2:
                    project_out(U_G1 + u, o)
                else:
                    pe.wait_ge(o_lo, HEADS // 2)
                    branch(U_G1 + u, o, of_hi, of_lo)
                if u == 0:
                    values(HEADS - 2)
                    transposed_probs(HEADS - 1, range(3))
                    values(HEADS - 1)
                elif u == 9:
                    pe.wait_ge(mem_in_ok, 32)
                    pe.wait_ge(exp_done, HEADS)
                    pe.wait_ge(o_lo, HEADS // 2)
                    for b in range(MB):
                        turn_rows(T_MEM2 + 2 * b, mem_in[:, b, :])

            def merged_chunk(k):
                hi, lo = (m0_hi, m0_lo) if k < 4 else (m1_hi, m1_lo)
                return hi[:, k % 4, :], lo[:, k % 4, :]

            def mixer_touched(j):
                if j < 2:
                    proj_is_out(pe, O_MQ - 2 + (O_MQ + j) % 2)
                elif j < 5:
                    pe.wait_ge(xt_lo, T_MEM2 + j - 1)
                elif j < 7:
                    t_is_out(pe, T_END - 2 + (T_END + j - 5) % 2)
                else:
                    pe.wait_ge(xt_lo, T_X2)

            tiles(0, U_OUT, merged_chunk, lambda k: pe.wait_ge(merged_lo, k + 1), mixer_touched)

            def mem_value_tiles(k, b):
                for half in range(2):
                    if k == 0:
                        pe.wait_ge(tile_free, 5 + 2 * b + half)
                    hi, lo = (r[:, half * HALF:(half + 1) * HALF] for r in parts(U_MV + k))
                    mm = split_product(bank(4 + 2 * b + half), memT_hi[:, k, b * P:(b + 1) * P],
                                       memT_lo[:, k, b * P:(b + 1) * P], hi, lo, k == 0, k == KC - 1)
                return mm

            for pair in range(KC // 2):
                for k in (2 * pair, 2 * pair + 1):
                    ready(U_MV + k)
                    mem_value_tiles(k, 0)
                for k in (2 * pair, 2 * pair + 1):
                    mem_value_tiles(k, 1).then_inc(unit_used, 1)
                if pair < 2:
                    b = 2 + pair
                    pe.wait_ge(ln_done, TB + b + 1)
                    turn_rows(T_X2 + 2 * b, xb[:, b, :])
            pe.wait_ge(xt_lo, T_X3)

            def mem_scores(h):
                if h == 0:
                    pe.wait_ge(km_split, 1)
                for m in range(2):
                    proj_is_out(pe, O_MQ + 2 * h + m)
                pe.wait_ge(exp_done, HEADS + h)
                for b in range(TB):
                    for m in range(2):
                        tok, c = slice(b * P, (b + 1) * P), 2 * h + m
                        mm = split_product(sc[:, b * MEM:(b + 1) * MEM], qm_hi[:, h % 2, m, tok], qm_lo[:, h % 2, m, tok],
                                           km_hi[:, c, :], km_lo[:, c, :], m == 0, m == 1)
                mm.then_inc(s_full, 1)

            def mem_transposed_probs(h):
                pe.wait_ge(p_done, HEADS + h + 1)
                for m in range(MB):
                    if h >= 1:
                        pe.wait_ge(mt_free[m], h)
                    elif m == 0:
                        pe.wait_ge(vm_done, 4)
                    for b in range(TB):
                        mm = pe.transpose(bank(4 + m)[:, b * P:(b + 1) * P], prob[:, MEM * b + P * m:MEM * b + P * (m + 1)],
                                          ident[:, :])
                    mm.then_inc(mt_full, 1)

            def mem_values(h):
                for m in range(MB):
                    pe.wait_ge(mt_free[m], h + 1)
                for e in range(2):
                    if h >= 1:
                        pe.wait_ge(om_lo_done, 2 * h + e - 1)
                    for m in range(MB):
                        c0 = 2 * P * h + P * e
                        keys = slice(HALF * m, HALF * (m + 1))
                        mm = split_product(bank(6 + e), vm_hi[:, m, c0:c0 + P], vm_lo[:, m, c0:c0 + P], pm_hi[:, keys],
                                           pm_lo[:, keys], m == 0, m == MB - 1)
                    mm.then_inc(om_full, 1)

            def memory_out(k):
                return om_hi[:, k, :], om_lo[:, k, :]

            early = []

            def early_products(ks):
                for k in ks:
                    ready(U_MO + k)
                    pe.wait_ge(om_lo_done, k + 1)
                    for j in range(2):
                        if k == 0:
                            proj_is_out(pe, O_END - 2 + (O_END + j) % 2)
                        tile_product(j, k, U_MO, memory_out)
                        early.append((j, k))

            project_out(U_MQ, O_MQ)
            for h in range(MEM_HEADS):
                project_out(U_MQ + 2 * h + 1, O_MQ + 2 * h + 1)
                if h >= 2:
                    mem_values(h - 2)
                if h < MEM_HEADS - 1:
                    project_out(U_MQ + 2 * h + 2, O_MQ + 2 * h + 2)
                if h >= 1:
                    mem_transposed_probs(h - 1)
                mem_scores(h)
            early_products((0, 1))
            mem_values(MEM_HEADS - 2)
            mem_transposed_probs(MEM_HEADS - 1)
            early_products((2,))
            mem_values(MEM_HEADS - 1)

            def memory_touched(j):
                if 2 <= j < 4:
                    pe.wait_ge(exp_done, HEADS + MEM_HEADS)
                elif 4 <= j < 6:
                    pe.wait_ge(mt_free[j - 4], MEM_HEADS)
                elif j >= 6:
                    pe.wait_ge(om_lo_done, j + 1)

            tiles(1, U_MO, memory_out, lambda k: pe.wait_ge(om_lo_done, k + 1), memory_touched, early)
            pe.wait_ge(tile_free, 14)
            ffn(1, U_FFN2)

        @block.scalar
        def _(act):
            copy = ACT.Copy

            def prep(n, i=None):
                if i is None:
                    act.wait_ge(landed[n % RAW], 16 * (n // RAW + 1))
                    if n >= RING:
                        act.wait_ge(unit_used, n - RING + 1)
                else:
                    act.wait_ge(landed[n % RAW], i * 32 + 16 * (n // RAW + 1))
                    act.wait_ge(unit_used, i * 6 + max(n - RING + 1, 0))
                src, dst = raw[:, n % RAW, :], ring_hi[:, n % RING, :]
                if n == U_F:
                    src, dst = forget_views(n, ring_hi)
                nc.scalar.activation(dst, src, copy).then_inc(unit_hi, 1)

            def high(dst, src, done):
                nc.scalar.activation(dst, src, copy).then_inc(done, 1)

            def turned_high(n, dst, b):
                act.wait_ge(xt_full, n + 1)
                e = n % 2
                high(dst[:, 4 * e:4 * e + 4, b * P:(b + 1) * P], turned(xt_bank(n)), xt_hi)

            def standardize(n, x, b):
                act.wait_ge(shift_done, n * TB + b + 1)
                nc.scalar.activation(x[:, b, :], x[:, b, :], ACT.Identity, scale=rstd[:, b:b + 1],
                                     bias=shift[:, b:b + 1]).then_inc(standard, 1)

            def turned_pair(n, b):
                for e in range(2):
                    turned_high(n + 2 * b + e, xT_hi, b)

            def layer_norm(n, t0, u):
                standardize(n, xb, 0)
                turned_pair(t0, 0)
                standardize(n, xb, 1)
                prep(u)
                turned_pair(t0, 1)
                standardize(n, xb, 2)
                for k in (1, 2, 3):
                    prep(u + k)
                standardize(n, xb, 3)
                turned_pair(t0, 2)

            def ffn(f, n0):
                chunk0 = 2 * FF_PAIRS * f

                def sigmoid(side, n, chunk, i=None):
                    if i is None:
                        act.wait_ge(unit_used, n + 1)
                        if chunk >= 2:
                            act.wait_ge(gated, chunk - 1)
                    else:
                        act.wait_ge(unit_used, i * 6 + (n + 1))
                        act.wait_ge(gated, i * 2 + (chunk - 1))
                    nc.scalar.activation(sig[:, side, :], bank(2 * side), ACT.Sigmoid).then_inc(sig_done, 1)

                def hidden_high(side, chunk, used, i=None):
                    act.wait_ge(h_full, chunk + 1 if i is None else i * 2 + (chunk + 1))
                    act.wait_ge(unit_used, used if i is None else i * 6 + used)
                    high(h_hi[:, side, :], hf[:, side, :], h_hi_done)

                if f == 0:
                    prep(n0 + 3)
                    sigmoid(0, n0, chunk0)
                    for n in range(T_MEM, T_X1):
                        turned_high(n, memT_hi, (n - T_MEM) // 2)
                else:
                    sigmoid(0, n0, chunk0)
                for k in range(4, 6):
                    prep(n0 + k)
                hidden_high(0, chunk0, n0 + 1)
                sigmoid(1, n0 + 2, chunk0 + 1)
                n = n0 + 4
                with act.Fori(0, FF_PAIRS - 1) as i:
                    prep(n + 2, i)
                    prep(n + 3, i)
                    prep(n + 4, i)
                    hidden_high(1, chunk0 + 1, n - 2, i)
                    prep(n + 5, i)
                    sigmoid(0, n, chunk0 + 2, i)
                    prep(n + 6, i)
                    prep(n + 7, i)
                    hidden_high(0, chunk0 + 2, n + 4, i)
                    sigmoid(1, n + 4, chunk0 + 3, i)
                if f == 0:
                    for k in range(3):
                        prep(U_MK + k)
                hidden_high(1, chunk0 + 2 * FF_PAIRS - 1, n0 + 6 * FF_PAIRS - 6 + 2)

            act.dma_start(bias_rows[0:2 * KC, :], t["mix_b_gate"].rearrange("g (m p) -> (g m) p", p=P)).then_inc(small_in, 16)
            act.dma_start(bias_rows[2 * KC:2 * KC + 1, :].rearrange("a (r h) -> a r h", h=FOX_HEADS),
                          t["mix_b_forget"].unsqueeze(1).to_broadcast([1, FOX_COPIES, FOX_HEADS])).then_inc(small_in, 16)
            act.dma_start(sinks[:, :], t["swa_sinks"].to_broadcast([P, SWA_HEADS])).then_inc(small_in, 16)
            for n in range(8):
                turned_high(n, xT_hi, n // 2)
                if n in (3, 7):
                    for u in (0, 1) if n == 3 else (2,):
                        prep(u)
            ffn(0, U_FFN1)
            prep(U_MK + 3)
            standardize(0, xa, 0)
            for m in range(KC):
                act.wait_ge(unit_used, U_MK + m + 1)
                nc.scalar.activation(km[:, m, :], bank((O_MK + m) % 2)[:, 0:MEM], copy).then_inc(proj_free[(O_MK + m) % 2], 1)
                if m in AFTER_MK:
                    turned_pair(T_X1, AFTER_MK.index(m))
                if m < TB - 1:
                    standardize(0, xa, m + 1)
                if m < 2:
                    prep(U_MK + m + 4)
                elif m >= 3:
                    for n in (6, 7) if m == 3 else (m + 4,):
                        prep(U_MK + n)

            def output(n, o):
                act.wait_ge(unit_used, n + 1)
                return bank(o % 2)

            def rotary_parts(x, n, o, turn, scale):
                src, half = output(n, o), HD // 2
                nc.scalar.activation(x, src, copy, scale=scale)
                if turn >= 2:
                    act.wait_ge(rope_done, turn - 1)
                for first in range(0, P, HD):
                    low_half, high_half = slice(first, first + half), slice(first + half, first + HD)
                    nc.scalar.activation(rot[turn % 2][low_half, :], src[high_half, :], copy, scale=-scale)
                    ins = nc.scalar.activation(rot[turn % 2][high_half, :], src[low_half, :], copy, scale=scale)
                ins.then_inc(proj_free[o % 2], 1)

            prep(U_F + 4)
            act.wait_ge(bias_made, 2)
            nc.scalar.activation(fz[:, :], output(U_F, O_F), ACT.Identity, bias=b_f[:, 0:1]).then_inc(proj_free[O_F % 2], 1)
            act.wait_ge(f_dve, 1)
            nc.scalar.activation(fa[:, :], fe[:, :], ACT.Exp, scale=-1.0).then_inc(f_act, 1)
            act.wait_ge(f_act, 1)
            nc.scalar.activation(fb[:, :], fa[:, :], ACT.Ln, bias=1.0).then_inc(f_act, 1)
            prep(U_KS + 4)
            rotary_parts(kraw[:, :], U_KS, O_KS, 0, 1.0)
            prep(U_VS + 4)
            nc.scalar.activation(gate[:, 0, :], output(U_VS, O_VS), copy).then_inc(proj_free[O_VS % 2], 1)
            act.wait_ge(spilled, 16 * TB)
            act.wait_ge(rope_done, 1)
            for kv in range(SWA_KV):
                for e in range(2):
                    ins = nc.scalar.activation(ks_hh[HD * e:HD * (e + 1), kv, :], kraw[HD * kv:HD * (kv + 1), :], copy)
            ins.then_inc(ks_made, 1)
            for m in range(4):
                prep(U_QS + m + 4)
                rotary_parts(qs[:, m, :], U_QS + m, O_QS + m, 1 + m, QK_SCALE)

            def copied_probs(H):
                for e, n in enumerate(head_uses(H)):
                    if e != 1:
                        act.wait_ge(t_full, n + 1)
                        w = HALF if e == 0 else 2 * P
                        nc.scalar.activation(probT[:, HALF * e:HALF * e + w], bank(5 + n % 2)[:, 0:w], copy)\
                            .then_inc(t_free[n % 2], 1)

            def exponentials(H, at, sink=None):
                act.wait_ge(ntop_done, H + 1)
                if sink is not None:
                    nc.scalar.activation(esink[:, :], ntop[:, :], ACT.Exp, bias=sinks[:, sink:sink + 1])
                for q, (c0, w) in sorted(at.items()):
                    ins = nc.scalar.activation(prob[:, c0:c0 + w], sc[:, c0:c0 + w], ACT.Exp, bias=ntop[:, q:q + 1],
                                               accum_out=rsum[:, q:q + 1])
                ins.then_inc(exp_done, 1)

            def pair_high(H):
                act.wait_ge(o_full, H + 1)
                m = H // 2
                high((os_hi if m < 4 else of_hi)[:, m % 4, :], bank(7), o_hi)

            def gate_tanh(n, o, g, m):
                nc.scalar.activation(gate[:, m % 2, :], output(n, o), ACT.Tanh, bias=b_gate[:, g, m:m + 1], scale=0.5)\
                    .then_inc(proj_free[o % 2], 1)

            def stack_high(H):
                own, other = rows_of(H)
                q, k = query_key(H)
                if H < SWA_HEADS:
                    act.wait_ge(rope_done, H // 2 + 2)
                elif H == SWA_HEADS:
                    for o in range(O_QF, O_VF):
                        proj_is_out(act, o)
                if H >= 2:
                    act.wait_ge(s_full, H - 1)
                ins = nc.scalar.activation(q_st[own, H % 2, :], q[own, :], copy)
                if k is not None:
                    nc.scalar.activation(k_hh[own, H % 2, :], k[own, :], copy)
                    ins = nc.scalar.activation(k_hh[other, H % 2, :], k[own, :], copy)
                ins.then_inc(stack_hi, 1)

            stack_high(0)
            at_swa = {q: (WINDOW * q, WINDOW) for q in range(TB)}
            act.wait_ge(small_in, 48)
            for H in range(HEADS):
                for i, u in enumerate(fill(H % 8)):
                    if i == 1 and 3 <= H != SWA_HEADS + 1:
                        pair_high(H - 2)
                    if H < SWA_HEADS:
                        n, o = U_QF + u, O_QF + u
                        prep(n + 4)
                        if u in (1, 2):
                            act.wait_ge(rope_done, 5)
                        if u < 4:
                            nc.scalar.activation(qf[:, u, :], output(n, o), copy, scale=QK_SCALE).then_inc(proj_free[o % 2], 1)
                        elif u >= 8:
                            v = u - 8
                            act.wait_ge(t_full, (T_VF[v - 2] if v >= 2 else T_VS) + 1)
                            nc.scalar.activation(gate[:, (v + 1) % 2, :], output(n, o), copy).then_inc(proj_free[o % 2], 1)
                    else:
                        n = U_G0 + u
                        prep(n + 4)
                        if u % 3 < 2:
                            o, m = O_G0 + 4 * (u // 3) + u % 3, 2 * (u // 3) + u % 3
                            if m >= 2:
                                proj_is_out(act, o - 2)
                            else:
                                act.wait_ge(t_full, T_VF[3] + 1)
                            gate_tanh(n, o, 0, m)
                if H >= 1:
                    copied_probs(H - 1)
                if H == SWA_HEADS:
                    pair_high(H - 1)
                exponentials(H, at_swa if H < SWA_HEADS else FOX_AT, H if H < SWA_HEADS else None)
                if H + 1 < HEADS:
                    stack_high(H + 1)

            def merged_high(m):
                act.wait_ge(merged, m + 1)
                if m >= 4:
                    act.wait_ge(unit_used, U_G1 + 11)
                hi = (m0_hi if m < 4 else m1_hi)[:, m % 4, :]
                nc.scalar.activation(hi, part[:, m, :], copy, scale=0.5).then_inc(merged_hi, 1)

            for u in range(12):
                n = U_G1 + u
                prep(n + 4)
                if u % 3 < 2:
                    o, m = O_G1 + 4 * (u // 3) + u % 3, 2 * (u // 3) + u % 3
                    if m >= 2:
                        act.wait_ge(merged, m - 1)
                    else:
                        proj_is_out(act, O_G1 - 2 + m)
                    gate_tanh(n, o, 1, m)
                if u == 0:
                    copied_probs(HEADS - 1)
                    pair_high(HEADS - 1)
                if u in (3, 6):
                    for m in (0, 1) if u == 3 else (2, 3):
                        merged_high(m)
            prep(U_OUT + 4)
            act.wait_ge(unit_used, U_G1 + 12)
            for n in range(T_MEM2, T_X2):
                turned_high(n, memT_hi, (n - T_MEM2) // 2)
            for m in range(4, KC):
                merged_high(m)
            for m in range(5, KC):
                prep(U_OUT + m)
            layer_norm(1, T_X2, U_MV)
            prep(U_MV + 4)
            prep(U_MV + 5)
            prep(U_MV + 6)
            turned_pair(T_X2, 3)
            prep(U_MV + 7)
            for e in range(2):
                high(km_hi[:, 4 * e:4 * e + 4, :], km[:, 4 * e:4 * e + 4, :], km_hi_done)
            for k in range(4):
                prep(U_MQ + k)
            act.wait_ge(unit_used, U_MV + KC)
            for b in range(MB):
                for half in range(2):
                    high(vm_hi[:, b, half * HALF:(half + 1) * HALF], bank(4 + 2 * b + half), vm_hi_done)
            def query_high(c):
                h, m, o = c // 2, c % 2, O_MQ + c
                if h >= 2:
                    act.wait_ge(s_full, HEADS + h - 1)
                nc.scalar.activation(qm_hi[:, h % 2, m, :], output(U_MQ + c, o), copy, scale=MEM_SCALE).then_inc(qm_hi_done, 1)
                prep(U_MQ + c + 4)

            def outputs_high(h):
                for e in range(2):
                    m = 2 * h + e
                    act.wait_ge(om_full, m + 1)
                    high(om_hi[:, m, :], bank(6 + e), om_hi_done)

            query_high(0)
            for h in range(MEM_HEADS + 1):
                if h < MEM_HEADS:
                    query_high(2 * h + 1)
                if h >= 2:
                    outputs_high(h - 2)
                if h < MEM_HEADS - 1:
                    query_high(2 * h + 2)
                if h >= 1:
                    for m in range(MB):
                        act.wait_ge(mt_full, 2 * h - 1 + m)
                        high(pm_hi[:, HALF * m:HALF * (m + 1)], bank(4 + m), pm_hi_done)
                if h < MEM_HEADS:
                    exponentials(HEADS + h, at_swa)
            outputs_high(MEM_HEADS - 1)
            for m in range(4, KC):
                prep(U_MO + m)
            layer_norm(2, T_X3, U_FFN2)
            turned_pair(T_X3, 3)
            ffn(1, U_FFN2)
            for b in range(TB - 1):
                standardize(3, xb, b)

        @block.vector
        def _(dve):
            def low(dst, src, hi, done):
                nc.vector.tensor_tensor(dst, src, hi.bitcast(F32), ALU.subtract).then_inc(done, 1)

            def split(n, i=None):
                dve.wait_ge(unit_hi, n + 1 if i is None else i * 6 + (n + 1))
                src, dst, hi = raw[:, n % RAW, :], ring_lo[:, n % RING, :], ring_hi[:, n % RING, :]
                if n == U_F:
                    src, dst = forget_views(n, ring_lo)
                    hi = forget_views(n, ring_hi)[1]
                low(dst, src, hi, unit_lo)

            def turned_low(n, hi, lo, b):
                dve.wait_ge(xt_hi, n + 1)
                e = n % 2
                at = (slice(None), slice(4 * e, 4 * e + 4), slice(b * P, (b + 1) * P))
                low(lo[at], turned(xt_bank(n)), hi[at], xt_lo)

            def scale_residual(x, blocks, turned_uses=None, done=(scaled, 1)):
                for b in blocks:
                    if turned_uses is not None:
                        dve.wait_ge(xt_full, turned_uses + 2 * b + 2)
                    nc.vector.tensor_scalar(x[:, b, :], x[:, b, :], ALPHA, None, ALU.mult).then_inc(*done)

            def add_tile(x, j, src, done):
                at = (slice(None), j // 2, slice(HALF * (j % 2), HALF * (j % 2 + 1)))
                nc.vector.tensor_tensor(x[at], x[at], src, ALU.add).then_inc(done, 1)

            def block_stats(n, x, b, done, count):
                dve.wait_ge(done, count)
                for e in range(2):
                    nc.vector.bn_stats(stats[:, b, e, :], x[:, b, HALF * e:HALF * (e + 1)]).then_inc(stats_done, 1)
                dve.wait_ge(stats_done, 2 * (n * TB + b) + 2)
                nc.vector.bn_aggr(mv[:, b, :], stats[:, b, :, :]).then_inc(mean_done, 1)

            def gain(n, x, b, between=None):
                if b == 0:
                    dve.wait_ge(gains_in, 32 * (n + 1))
                count = n * TB + b + 1
                dve.wait_ge(standard, count)
                nc.vector.tensor_tensor(x[:, b, :], x[:, b, :], ln_g[:, :], ALU.mult).then_inc(gained, 1)
                if between is not None:
                    split(between)
                if b >= POOL_BLOCKS[n]:
                    dve.wait_ge(gained, count)
                    if n < 3:
                        dve.wait_ge(ln_done, count - 1)
                    nc.vector.tensor_tensor(x[:, b, :], x[:, b, :], ln_b[:, :], ALU.add)\
                        .then_inc(ln_done if n < 3 else last_done, 1)

            def last_blocks(x):
                b = TB - 1
                gain(3, x, b - 1)
                dve.wait_ge(mean_done, 4 * TB)
                nc.vector.scalar_tensor_tensor(out=x[:, b, :], in0=x[:, b, :], scalar=mv[:, b, 0:1], in1=ln_g[:, :],
                                               op0=ALU.subtract, op1=ALU.mult).then_inc(centred, 1)
                dve.wait_ge(rstd_done, 4 * TB)
                dve.wait_ge(centred, 1)
                for cols in halves(3, b):
                    nc.vector.scalar_tensor_tensor(out=x[:, b, cols], in0=x[:, b, cols], scalar=rstd[:, b:b + 1],
                                                   in1=ln_b[:, cols], op0=ALU.mult, op1=ALU.add).then_inc(last_done, 1)

            def ffn(f, n0, x):
                chunk0, pair0 = 2 * FF_PAIRS * f, FF_PAIRS * f

                def hidden(side, n, chunk, i=None):
                    dve.wait_ge(sig_done, chunk + 1 if i is None else i * 2 + (chunk + 1))
                    nc.vector.tensor_tensor(hf[:, side, :], sig[:, side, :], bank(2 * side), ALU.mult).then_inc(gated, 1)
                    dve.wait_ge(unit_used, n + 1 if i is None else i * 6 + (n + 1))
                    dve.wait_ge(gated, chunk + 1 if i is None else i * 2 + (chunk + 1))
                    nc.vector.scalar_tensor_tensor(out=hf[:, side, :], in0=hf[:, side, :], scalar=0.5, in1=bank(2 * side + 1),
                                                   op0=ALU.mult, op1=ALU.mult).then_inc(h_full, 1)

                def hidden_low(side, chunk, i=None):
                    dve.wait_ge(h_hi_done, chunk + 1 if i is None else i * 2 + (chunk + 1))
                    low(h_lo[:, side, :], hf[:, side, :], h_hi[:, side, :], h_lo_done)

                def add_down(js, n, pair, i=None):
                    for j in js:
                        if j < 7:
                            full = 7 * pair + j + 1
                            dve.wait_ge(down_full, full if i is None else i * 7 + full)
                        else:
                            dve.wait_ge(unit_used, n + 1 if i is None else i * 6 + (n + 1))
                        was = tile_sums(f, pair, j - 7)
                        dve.wait_ge(sums, was if i is None else i * 8 + was)
                        add_tile(x, j, bank(4 + j % 4), sums)

                if f == 0:
                    split(n0 + 3)
                    scale_residual(xa, range(TB), 0, (sums, 2))
                hidden(0, n0 + 1, chunk0)
                if f == 0:
                    for n in range(T_MEM, T_X1):
                        turned_low(n, memT_hi, memT_lo, (n - T_MEM) // 2)
                split(n0 + 4)
                split(n0 + 5)
                hidden_low(0, chunk0)
                n = n0 + 4
                with dve.Fori(0, FF_PAIRS - 1) as i:
                    hidden(1, n - 1, chunk0 + 1, i)
                    split(n + 2, i)
                    split(n + 3, i)
                    split(n + 4, i)
                    hidden_low(1, chunk0 + 1, i)
                    split(n + 5, i)
                    split(n + 6, i)
                    hidden(0, n + 1, chunk0 + 2, i)
                    add_down((0, 1), n + 3, pair0, i)
                    split(n + 7, i)
                    add_down(range(2, 8), n + 3, pair0, i)
                    hidden_low(0, chunk0 + 2, i)
                last = n0 + 6 * FF_PAIRS - 1
                if f == 0:
                    for k in range(3):
                        split(U_MK + k)
                hidden(1, last - 2, chunk0 + 2 * FF_PAIRS - 1)
                hidden_low(1, chunk0 + 2 * FF_PAIRS - 1)
                for b in range(TB):
                    add_down((2 * b, 2 * b + 1), last, pair0 + FF_PAIRS - 1)
                    block_stats(3 * f, x, b, sums, tile_sums(f, pair0 + FF_PAIRS - 1, 2 * b + 2))
                    if b == 2 and f == 0:
                        split(U_MK + 3)
                    if b == TB - 1 and f == 0:
                        turned_pair(T_X1, 0)
                    if 1 <= b < TB - f:
                        gain(3 * f, x, b - 1)
                if f == 0:
                    gain(0, x, TB - 1, U_MK + 4)
                else:
                    last_blocks(x)

            def turned_pair(n, b):
                for e in range(2):
                    turned_low(n + 2 * b + e, xT_hi, xT_lo, b)

            for n in range(8):
                turned_low(n, xT_hi, xT_lo, n // 2)
                if n == 3:
                    split(0)
                    split(1)
                    dve.wait_ge(bias_turned, 1)
                    nc.vector.tensor_scalar(b_gate[:, :, :].rearrange("p g m -> p (g m)"), bank(7)[:, 0:2 * KC], 0.5, None,
                                            ALU.mult).then_inc(bias_made, 1)
                    nc.vector.tensor_copy(b_f[:, :], bank(7)[:, 2 * KC:2 * KC + 1]).then_inc(bias_made, 1)
            split(2)
            dve.wait_ge(consts, 2)
            nc.vector.tensor_reduce(pick_part[:, 0:6], pick[:, :, :], AX.X, ALU.add).then_inc(dve_consts, 1)
            dve.wait_ge(dve_consts, 1)
            nc.vector.tensor_reduce(pick_part[:, 6:8], pick_part[:, 0:6].rearrange("p (a b) -> p a b", a=2), AX.X, ALU.add)\
                .then_inc(dve_consts, 1)
            nc.vector.tensor_reduce(pick_head[:, :], pick[:, :, :].rearrange("p k h -> p h k"), AX.X, ALU.add)\
                .then_inc(dve_consts, 1)
            dve.wait_ge(dve_consts, 2)
            nc.vector.tensor_scalar(pick_part[:, 0:3], pick_part[:, 0:3], -1.0, None, ALU.mult).then_inc(dve_consts, 1)
            ffn(0, U_FFN1, xa)
            for m in range(1, KC):
                split(U_MK + m + 4)
                if m < TB:
                    turned_pair(T_X1, m)

            ropes = [0]

            def rotate(x, o):
                buf = rot[ropes[0] % 2]
                ropes[0] += 1
                proj_is_out(dve, o)
                nc.vector.tensor_tensor(buf[:, :], buf[:, :], sin_t[:, :], ALU.mult).then_inc(rope_sin, 1)
                nc.vector.tensor_tensor(x, x, cos_t[:, :], ALU.mult).then_inc(rope_cos, 1)
                dve.wait_ge(rope_sin, ropes[0])
                dve.wait_ge(rope_cos, ropes[0])
                nc.vector.tensor_tensor(x, x, buf[:, :], ALU.add).then_inc(rope_done, 1)

            split(U_F + 4)
            proj_is_out(dve, O_F)
            nc.vector.scalar_tensor_tensor(out=fe[:, :], in0=fz[:, :], scalar=-1.0, in1=fz[:, :], op0=ALU.mult,
                                           op1=ALU.max).then_inc(f_dve, 1)
            dve.wait_ge(f_act, 2)
            nc.vector.scalar_tensor_tensor(out=fe[:, :], in0=fz[:, :], scalar=0.0, in1=fb[:, :], op0=ALU.min,
                                           op1=ALU.subtract).then_inc(f_dve, 1)
            split(U_KS + 4)
            dve.wait_ge(t_full, T_F + 1)
            nc.vector.tensor_copy(lsn[:, :, :].rearrange("p k c -> p (k c)"), bank(5 + T_F % 2)).then_inc(t_free[T_F % 2], 1)
            split(U_VS + 4)
            dve.wait_ge(angles_in, 32)
            rotate(kraw[:, :], O_KS)
            dve.wait_ge(t_full, T_C + 1)
            c = bank(5 + T_C % 2)
            nc.vector.tensor_copy(c_hi[:, :], c).then_inc(f_dve, 1)
            dve.wait_ge(f_dve, 3)
            nc.vector.tensor_tensor(fz[:, :], c, c_hi[:, :], ALU.subtract).then_inc(t_free[T_C % 2], 1)
            t_is_out(dve, T_C)
            nc.vector.tensor_copy(c_mid[:, :], fz[:, :]).then_inc(f_dve, 1)
            dve.wait_ge(f_dve, 4)
            nc.vector.tensor_tensor(fe[:, :], fz[:, :], c_mid[:, :], ALU.subtract).then_inc(f_dve, 1)
            dve.wait_ge(f_dve, 5)
            nc.vector.tensor_copy(c_lo[:, :], fe[:, :]).then_inc(f_dve, 1)
            dve.wait_ge(f_dve, 6)
            dve.wait_ge(dve_consts, 4)
            for side, (first, acc, dst) in enumerate(((3, fa, c_q), (0, fb, c_k))):
                nc.vector.tensor_scalar(acc[:, :], c_hi[:, :], pick_part[:, first:first + 1], pick_part[:, 6 + side:7 + side],
                                        ALU.mult, ALU.add).then_inc(f_dve, 1)
                dve.wait_ge(f_dve, 7 + side)
                nc.vector.scalar_tensor_tensor(out=acc[:, :], in0=c_mid[:, :], scalar=pick_part[:, first + 1:first + 2],
                                               in1=acc[:, :], op0=ALU.mult, op1=ALU.add).then_inc(c_made, 1)
                dve.wait_ge(c_made, 1 + 2 * side)
                nc.vector.scalar_tensor_tensor(out=dst[:, :], in0=c_lo[:, :], scalar=pick_part[:, first + 2:first + 3],
                                               in1=acc[:, :], op0=ALU.mult, op1=ALU.add).then_inc(c_made, 1)
            split(U_QS + 4)
            dve.wait_ge(t_full, T_VS + 1)
            nc.vector.tensor_copy(vs[:, :, :].rearrange("p k c -> p (k c)"), bank(5 + T_VS % 2)).then_inc(t_free[T_VS % 2], 1)
            for m in range(1, 4):
                split(U_QS + m + 4)
                rotate(qs[:, m - 1, :], O_QS + m - 1)

            def copied_probs(H):
                n = head_uses(H)[1]
                dve.wait_ge(t_full, n + 1)
                w = 3 * P if H < SWA_HEADS else HALF
                nc.vector.tensor_copy(probT[:, HALF:HALF + w], bank(5 + n % 2)[:, 0:w]).then_inc(t_free[n % 2], 1)

            def maxima(H, at, sink=None):
                if H == 0:
                    dve.wait_ge(small_in, 48)
                dve.wait_ge(s_full, H + 1)
                if len({w for _, w in at.values()}) == 1:
                    nc.vector.tensor_reduce(top[:, :], sc[:, 0:TB * WINDOW].rearrange("p (q k) -> p q k", q=TB), AX.X, ALU.max)\
                        .then_inc(top_done, 1)
                else:
                    for q, (c0, w) in at.items():
                        ins = nc.vector.tensor_reduce(top[:, q:q + 1], sc[:, c0:c0 + w], AX.X, ALU.max)
                    ins.then_inc(top_done, 1)
                dve.wait_ge(top_done, H + 1)
                if sink is None:
                    nc.vector.tensor_scalar(ntop[:, :], top[:, :], -1.0, None, ALU.mult).then_inc(ntop_done, 1)
                else:
                    nc.vector.tensor_scalar(ntop[:, :], top[:, :], sinks[:, sink:sink + 1], -1.0, ALU.max, ALU.mult)\
                        .then_inc(ntop_done, 1)

            def normalize_probs(H, at, sink=None):
                dve.wait_ge(exp_done, H + 1)
                if sink is not None:
                    nc.vector.tensor_tensor(rsum[:, :], rsum[:, :], esink[:, :], ALU.add).then_inc(sink_added, 1)
                    dve.wait_ge(sink_added, sink + 1)
                nc.vector.reciprocal(rinv[:, :], rsum[:, :]).then_inc(inverse_done, 1)
                dve.wait_ge(inverse_done, H + 1)
                for q, (c0, w) in sorted(at.items()):
                    ins = nc.vector.tensor_scalar(prob[:, c0:c0 + w], prob[:, c0:c0 + w], rinv[:, q:q + 1], None, ALU.mult)
                ins.then_inc(p_done, 1)

            def pair_low(H):
                m = H // 2
                dve.wait_ge(o_hi, m + 1)
                hi, lo = (os_hi, os_lo) if m < 4 else (of_hi, of_lo)
                low(lo[:, m % 4, :], bank(7), hi[:, m % 4, :], o_lo)

            def branch_output(n, o, e):
                if e == 0:
                    dve.wait_ge(branch_full, branches[0] + 1)
                    branches[0] += 1
                else:
                    dve.wait_ge(unit_used, n + 1)
                return bank((o + e) % 2)

            def stack_low(H):
                own, other = rows_of(H)
                q, k = query_key(H)
                dve.wait_ge(stack_hi, H + 1)
                ins = nc.vector.tensor_tensor(q_st[other, H % 2, :], q[own, :], q_st[own, H % 2, :].bitcast(F32), ALU.subtract)
                if k is not None:
                    ins = nc.vector.tensor_tensor(k_low[own, H % 2, :], k[own, :], k_hh[own, H % 2, :].bitcast(F32), ALU.subtract)
                ins.then_inc(stack_lo, 1)

            dve.wait_ge(ks_made, 1)
            for kv in range(SWA_KV):
                src = slice(HD * kv, HD * (kv + 1))
                for e in range(2):
                    ins = nc.vector.tensor_tensor(ks_ll[HD * e:HD * (e + 1), kv, :], kraw[src, :], ks_hh[src, kv, :].bitcast(F32),
                                                  ALU.subtract)
            ins.then_inc(ks_split, 1)
            stack_low(0)
            branches = [0]
            at_swa = {q: (WINDOW * q, WINDOW) for q in range(TB)}
            for H in range(HEADS):
                for i, u in enumerate(fill(H % 8)):
                    if i == 1 and 3 <= H != SWA_HEADS + 1:
                        pair_low(H - 2)
                    n = (U_QF if H < SWA_HEADS else U_G0) + u
                    split(n + 4)
                    if H < SWA_HEADS and 4 <= u < 8:
                        m, o = u - 4, O_QF + u
                        dve.wait_ge(unit_used, n + 1)
                        nc.vector.tensor_copy(kf[:, m, :], bank(o % 2)).then_inc(proj_free[o % 2], 1)
                    elif H >= SWA_HEADS and u % 3 == 2:
                        o = O_G0 + 4 * (u // 3) + 2
                        for e in range(2):
                            m = 2 * (u // 3) + e
                            proj_is_out(dve, o + e - 2)
                            nc.vector.scalar_tensor_tensor(out=part[:, m, :], in0=gate[:, e, :], scalar=1.0,
                                                           in1=branch_output(n, o, e), op0=ALU.add, op1=ALU.mult)\
                                .then_inc(proj_free[(o + e) % 2], 1)
                if H == 0:
                    rotate(qs[:, 3, :], O_QS + 3)
                if H >= 1:
                    copied_probs(H - 1)
                if H < SWA_HEADS:
                    for u in fill(H):
                        if u >= 8:
                            v, use = u - 8, T_VF[u - 8]
                            dve.wait_ge(t_full, use + 1)
                            nc.vector.tensor_copy(vf[:, :, v * P:(v + 1) * P], turned(5 + use % 2)).then_inc(t_free[use % 2], 1)
                at, sink = (at_swa, H) if H < SWA_HEADS else (FOX_AT, None)
                maxima(H, at, sink)
                if H == SWA_HEADS:
                    pair_low(H - 1)
                normalize_probs(H, at, sink)
                if H + 1 < HEADS:
                    stack_low(H + 1)

            def merged_low_part(m):
                dve.wait_ge(merged_hi, m + 1)
                hi, lo = (m0_hi, m0_lo) if m < 4 else (m1_hi, m1_lo)
                nc.vector.scalar_tensor_tensor(out=lo[:, m % 4, :], in0=part[:, m, :], scalar=0.5,
                                               in1=hi[:, m % 4, :].bitcast(F32), op0=ALU.mult, op1=ALU.subtract)\
                    .then_inc(merged_lo, 1)

            for u in range(12):
                n = U_G1 + u
                split(n + 4)
                if u == 0:
                    copied_probs(HEADS - 1)
                    pair_low(HEADS - 1)
                if u % 3 == 2:
                    o = O_G1 + 4 * (u // 3) + 2
                    for e in range(2):
                        m = 2 * (u // 3) + e
                        proj_is_out(dve, o + e - 2)
                        nc.vector.scalar_tensor_tensor(out=gate[:, e, :], in0=gate[:, e, :], scalar=1.0,
                                                       in1=branch_output(n, o, e), op0=ALU.add, op1=ALU.mult)\
                            .then_inc(proj_free[(o + e) % 2], 1)
                        proj_is_out(dve, o + e)
                        nc.vector.tensor_tensor(part[:, m, :], part[:, m, :], gate[:, e, :], ALU.add).then_inc(merged, 1)
                if u in (3, 6):
                    for m in (0, 1) if u == 3 else (2, 3):
                        merged_low_part(m)
            split(U_OUT + 4)
            for n in range(T_MEM2, T_X2):
                turned_low(n, memT_hi, memT_lo, (n - T_MEM2) // 2)
            for m in range(4, KC):
                merged_low_part(m)
            dve.wait_ge(back, 16 * TB)
            scale_residual(xb, range(TB))

            def project_tiles(s, ln, n0, t0, splits, last_splits):
                dve.wait_ge(scaled, TB * (s + 1))
                for b in range(TB):
                    for e in range(2):
                        j = 2 * b + e
                        if j < 6:
                            dve.wait_ge(tile_full, 6 * s + j + 1)
                        else:
                            dve.wait_ge(unit_used, n0 + KC)
                        add_tile(xb, j, bank(j), tile_free)
                    block_stats(ln, xb, b, tile_free, 8 * s + 2 * b + 2)
                    for n in splits[b]:
                        split(n)
                    gain(ln, xb, b)
                    if 1 <= b <= 2:
                        turned_pair(t0, b - 1)
                    if b == 2:
                        for n in last_splits:
                            split(n)
                turned_pair(t0, 2)

            for n in range(U_OUT + 5, U_OUT + KC):
                split(n)
            project_tiles(0, 1, U_OUT, T_X2, ((), (), (U_MV,), (U_MV + 2, U_MV + 3)), (U_MV + 1,))
            for k in range(4, 7):
                split(U_MV + k)
            turned_pair(T_X2, 3)
            split(U_MV + 7)
            dve.wait_ge(km_hi_done, 2)
            low(km_lo[:, :, :], km[:, :, :], km_hi[:, :, :], km_split)
            for k in range(4):
                split(U_MQ + k)
            for b in range(MB):
                for half in range(2):
                    cols = slice(half * HALF, (half + 1) * HALF)
                    dve.wait_ge(vm_hi_done, 2 * b + half + 1)
                    low(vm_lo[:, b, cols], bank(4 + 2 * b + half), vm_hi[:, b, cols], vm_done)
            def query_low(c):
                h, m, o = c // 2, c % 2, O_MQ + c
                dve.wait_ge(qm_hi_done, c + 1)
                nc.vector.scalar_tensor_tensor(out=qm_lo[:, h % 2, m, :], in0=bank(o % 2), scalar=MEM_SCALE,
                                               in1=qm_hi[:, h % 2, m, :].bitcast(F32), op0=ALU.mult, op1=ALU.subtract)\
                    .then_inc(proj_free[o % 2], 1)
                split(U_MQ + c + 4)

            def outputs_low(h):
                for e in range(2):
                    m = 2 * h + e
                    dve.wait_ge(om_hi_done, m + 1)
                    low(om_lo[:, m, :], bank(6 + e), om_hi[:, m, :], om_lo_done)

            query_low(0)
            for h in range(MEM_HEADS + 1):
                if h < MEM_HEADS:
                    query_low(2 * h + 1)
                if h >= 2:
                    outputs_low(h - 2)
                if h < MEM_HEADS - 1:
                    query_low(2 * h + 2)
                if h >= 1:
                    for m in range(MB):
                        dve.wait_ge(pm_hi_done, 2 * h - 1 + m)
                        keys = slice(HALF * m, HALF * (m + 1))
                        low(pm_lo[:, keys], bank(4 + m), pm_hi[:, keys], mt_free[m])
                if h < MEM_HEADS:
                    maxima(HEADS + h, at_swa)
                    normalize_probs(HEADS + h, at_swa)
                if h == 0:
                    scale_residual(xb, range(TB), T_X2)
            outputs_low(MEM_HEADS - 1)
            for n in range(U_MO + 4, U_MO + KC):
                split(n)
            u = U_FFN2
            project_tiles(1, 2, U_MO, T_X3, ((), (), (u,), (u + 2, u + 3)), (u + 1,))
            turned_pair(T_X3, 3)
            scale_residual(xb, range(TB), T_X3, (sums, 2))
            ffn(1, U_FFN2, xb)


_INS = ["x", "mem", "ffn1_w_gate", "ffn1_w_up", "ffn1_w_down", "ln1_g", "ln1_b", "mix_w_in", "mix_b_gate",
        "mix_b_forget", "swa_sinks", "mix_w_branch_swa", "mix_w_branch_fox", "mix_w_out", "ln2_g", "ln2_b",
        "mem_w_q", "mem_w_k", "mem_w_v", "mem_w_o", "ln3_g", "ln3_b", "ffn2_w_gate", "ffn2_w_up", "ffn2_w_down",
        "ln4_g", "ln4_b"]


def kernel(**inputs):
    import numpy as _np
    import concourse.bacc as _bacc
    from concourse.bass_utils import run_bass_kernel_spmd as _run

    nc = _bacc.Bacc("TRN2", target_bir_lowering=False, num_devices=1)
    arrays, tensors = {}, {}
    for name in _INS:
        a = _np.ascontiguousarray(inputs[name])
        arrays[f"in_{name}"] = a
        ap = nc.dram_tensor(f"in_{name}", a.shape, F32, kind="ExternalInput").ap()
        if len(a.shape) == 3:
            ap = ap[0]
        tensors[name] = ap
    half = HD // 2
    freq = _np.float32(ROPE_THETA) ** (-_np.arange(half, dtype=_np.float32) / half)
    angle = _np.arange(SEQ, dtype=_np.float32)[None, :] * _np.tile(freq, P // half)[:, None]
    arrays["in_rope"] = _np.stack([_np.cos(angle), _np.sin(angle)])
    tensors["rope"] = nc.dram_tensor("in_rope", (2, P, SEQ), F32, kind="ExternalInput").ap()
    out = nc.dram_tensor("out", (1, SEQ, D), F32, kind="ExternalOutput").ap()
    spill = nc.dram_tensor("x_spill", (SEQ, D), F32, kind="Internal").ap()
    program(nc, tensors, out[0], spill)
    r = _run(nc, [arrays], core_ids=[0])
    return r.results[0]["out"]
```
